# Optimizing a Trainium2 kernel written in Bass

```python
import math
import jax, jax.numpy as jnp
from jax import lax
import numpy as np

D_MODEL = 1024
BATCH = 1
SEQ = 256
DEPTH = 2

D_MIX = D_MODEL
D_LRU = D_MIX // 2
D_ATT = D_MIX - D_LRU
HEAD_DIM = 64
N_HEADS = D_ATT // HEAD_DIM
N_KV_GROUPS = 2
HEADS_PER_GROUP = N_HEADS // N_KV_GROUPS
KV_WIDTH = N_KV_GROUPS * HEAD_DIM
LRU_BLOCKS = 8
LRU_BLOCK_W = D_LRU // LRU_BLOCKS
LRU_C = 8.0
CONV_WIDTH = 4
CMP_BLOCK = 32
CMP_STRIDE = 16
CMP_HIDDEN = 2 * HEAD_DIM
SEL_BLOCK = 64
N_SELECT = 16
WINDOW = 512
NSA_QBLOCK = 64
N_BRANCH = 3
N_BUCKETS = 32
MAX_EXACT = N_BUCKETS // 2
MAX_DISTANCE = 128
D_FF = 2816
N_EXPERTS = 8
TOP_K = 2
MOE_BLOCK = 128
N_DENSE = (DEPTH + 1) // 2
N_MOE = DEPTH // 2
OFF_Q = 2 * D_LRU
OFF_KV = OFF_Q + D_ATT
OFF_GATE = OFF_KV + 6 * KV_WIDTH
D_IN = OFF_GATE + N_BRANCH * N_HEADS
NEG_INF = -1e30
FORCE_SCORE = 1e4
RMS_EPS = 1e-6

kernel_name = 'hybrid_rglru_nsa_moe_trunk'

def rms_norm(x, g):
    xf = x.astype(jnp.float32)
    y = xf * lax.rsqrt(jnp.mean(xf * xf, axis=-1, keepdims=True) + RMS_EPS)
    return (y * g.astype(jnp.float32)).astype(x.dtype)

def t5_bucket(dist):
    n = jnp.maximum(dist, 0)
    nf = jnp.maximum(n, 1).astype(jnp.float32)
    large = MAX_EXACT + (jnp.log(nf / MAX_EXACT) / math.log(MAX_DISTANCE / MAX_EXACT)
                         * (N_BUCKETS - MAX_EXACT)).astype(jnp.int32)
    large = jnp.minimum(large, N_BUCKETS - 1)
    return jnp.where(n < MAX_EXACT, n, large)

def masked_softmax(s, mask):
    s = jnp.where(mask, s, NEG_INF)
    m = jnp.max(s, axis=-1, keepdims=True)
    e = jnp.where(mask, jnp.exp(s - m), 0.0)
    return e / jnp.maximum(jnp.sum(e, axis=-1, keepdims=True), 1e-30)

def rg_lru(x, wa, ba, wx, bx, lam):
    b_, s_, _ = x.shape
    xb = x.reshape(b_, s_, LRU_BLOCKS, LRU_BLOCK_W)
    r = jax.nn.sigmoid(jnp.einsum('bshi,hij->bshj', xb, wa).reshape(b_, s_, D_LRU) + ba)
    i = jax.nn.sigmoid(jnp.einsum('bshi,hij->bshj', xb, wx).reshape(b_, s_, D_LRU) + bx)
    log_a = -LRU_C * r * jax.nn.softplus(-lam)
    a = jnp.exp(log_a)
    u = jnp.sqrt(-jnp.expm1(2.0 * log_a)) * (i * x)

    def combine(c1, c2):
        a1, b1 = c1
        a2, b2 = c2
        return a1 * a2, a2 * b1 + b2

    _, h = lax.associative_scan(combine, (a, u), axis=1)
    return h

def lru_group(x_in, gate_in, conv_w, conv_b, wa, ba, wx, bx, lam):
    xc = lax.conv_general_dilated(x_in, conv_w[:, None, :], window_strides=(1,),
                                  padding=[(CONV_WIDTH - 1, 0)],
                                  dimension_numbers=('NWC', 'WIO', 'NWC'),
                                  feature_group_count=D_LRU) + conv_b
    return jax.nn.gelu(gate_in) * rg_lru(xc, wa, ba, wx, bx, lam)

def compress(kv, pos, w1, w2):
    s_ = kv.shape[2]
    n_cmp = (s_ - CMP_BLOCK) // CMP_STRIDE + 1
    idx = jnp.arange(n_cmp)[:, None] * CMP_STRIDE + jnp.arange(CMP_BLOCK)[None, :]
    blocks = kv[:, :, idx] + pos
    h = jax.nn.gelu(jnp.einsum('bgnld,ldc->bgnc', blocks, w1))
    return jnp.einsum('bgnc,cd->bgnd', h, w2)

def nsa_group(q, kc_raw, vc_raw, ks_raw, vs_raw, kw_raw, vw_raw, gates,
              q_g, k_g, cmp_pos, cmp_w1, cmp_w2, rel_bias):
    b_, s_ = q.shape[:2]
    G, HPG, QB = N_KV_GROUPS, HEADS_PER_GROUP, NSA_QBLOCK
    nqb = s_ // QB
    n_sel_blocks = s_ // SEL_BLOCK
    n_sel = min(N_SELECT, n_sel_blocks)
    n_cmp = (s_ - CMP_BLOCK) // CMP_STRIDE + 1
    scale = HEAD_DIM ** -0.5

    q = rms_norm(q.reshape(b_, s_, N_HEADS, HEAD_DIM), q_g)
    q_blocks = q.reshape(b_, nqb, QB, G, HPG, HEAD_DIM).transpose(1, 0, 3, 4, 2, 5)
    g_blocks = jax.nn.sigmoid(gates).reshape(b_, nqb, QB, N_BRANCH, G, HPG).transpose(1, 0, 4, 5, 2, 3)

    def kv_heads(t):
        return t.reshape(b_, s_, G, HEAD_DIM).transpose(0, 2, 1, 3)

    kc = rms_norm(compress(kv_heads(kc_raw), cmp_pos[0], cmp_w1[0], cmp_w2[0]), k_g)
    vc = compress(kv_heads(vc_raw), cmp_pos[1], cmp_w1[1], cmp_w2[1])
    ks_blk = rms_norm(kv_heads(ks_raw), k_g).reshape(b_, G, n_sel_blocks, SEL_BLOCK, HEAD_DIM)
    vs_blk = kv_heads(vs_raw).reshape(b_, G, n_sel_blocks, SEL_BLOCK, HEAD_DIM)
    pad = ((0, 0), (0, 0), (WINDOW, 0), (0, 0))
    kw_pad = jnp.pad(rms_norm(kv_heads(kw_raw), k_g), pad)
    vw_pad = jnp.pad(kv_heads(vw_raw), pad)

    cmp_start = jnp.arange(n_cmp) * CMP_STRIDE
    cmp_end = cmp_start + CMP_BLOCK - 1
    sel_start = jnp.arange(n_sel_blocks) * SEL_BLOCK
    overlap = jnp.clip(jnp.minimum(cmp_end[:, None], sel_start[None, :] + SEL_BLOCK - 1)
                       - jnp.maximum(cmp_start[:, None], sel_start[None, :]) + 1, 0, None)
    cmp_to_sel = overlap.astype(jnp.float32) / CMP_BLOCK
    rel_bias_g = rel_bias.reshape(N_BUCKETS, G, HPG).transpose(1, 0, 2)
    gather = jax.vmap(jax.vmap(lambda kb, ix: kb[ix]))
    bias_of = jax.vmap(lambda tb, bk: tb[bk], in_axes=(0, 1), out_axes=1)

    def head_bias(dist):
        bb = rel_bias[t5_bucket(dist)]
        return bb.transpose(2, 0, 1).reshape(G, HPG, *dist.shape).astype(jnp.float32)

    def block_fn(args):
        qb, gb, qi = args
        t = qi * QB + jnp.arange(QB)
        s = jnp.einsum('bghqd,bgnd->bghqn', qb, kc).astype(jnp.float32) * scale \
            + head_bias(t[:, None] - cmp_end[None, :])
        p_cmp = masked_softmax(s, cmp_end[None, :] <= t[:, None])
        o_cmp = jnp.einsum('bghqn,bgnd->bghqd', p_cmp.astype(vc.dtype), vc)
        imp = jnp.einsum('bghqn,nj->bgqj', p_cmp, cmp_to_sel)
        blk = jnp.arange(n_sel_blocks)
        score = jnp.where(blk[None, :] == (t // SEL_BLOCK)[:, None], FORCE_SCORE,
                          jnp.where(sel_start[None, :] <= t[:, None], imp, -1.0))
        top_val, top_idx = lax.top_k(score, n_sel)
        ks = gather(ks_blk, top_idx).reshape(b_, G, QB, n_sel * SEL_BLOCK, HEAD_DIM)
        vs = gather(vs_blk, top_idx).reshape(b_, G, QB, n_sel * SEL_BLOCK, HEAD_DIM)
        pos = (top_idx[..., None] * SEL_BLOCK + jnp.arange(SEL_BLOCK)).reshape(b_, G, QB, n_sel * SEL_BLOCK)
        valid = jnp.repeat(top_val >= 0, SEL_BLOCK, axis=-1) & (pos <= t[:, None])
        bias_s = jnp.moveaxis(bias_of(rel_bias_g, t5_bucket(t[:, None] - pos)), -1, 2).astype(jnp.float32)
        s = jnp.einsum('bghqd,bgqkd->bghqk', qb, ks).astype(jnp.float32) * scale + bias_s
        p = masked_softmax(s, valid[:, :, None])
        o_slc = jnp.einsum('bghqk,bgqkd->bghqd', p.astype(vs.dtype), vs)
        kw = lax.dynamic_slice_in_dim(kw_pad, qi * QB, WINDOW + QB, axis=2)
        vw = lax.dynamic_slice_in_dim(vw_pad, qi * QB, WINDOW + QB, axis=2)
        pos_w = qi * QB - WINDOW + jnp.arange(WINDOW + QB)
        dist = t[:, None] - pos_w[None, :]
        mask_w = (pos_w[None, :] >= 0) & (dist >= 0) & (dist < WINDOW)
        s = jnp.einsum('bghqd,bgkd->bghqk', qb, kw).astype(jnp.float32) * scale + head_bias(dist)
        p = masked_softmax(s, mask_w)
        o_win = jnp.einsum('bghqk,bgkd->bghqd', p.astype(vw.dtype), vw)
        gb = gb.astype(o_cmp.dtype)
        return gb[..., 0:1] * o_cmp + gb[..., 1:2] * o_slc + gb[..., 2:3] * o_win

    o = lax.map(block_fn, (q_blocks, g_blocks, jnp.arange(nqb)))
    return o.transpose(1, 0, 4, 2, 3, 5).reshape(b_, s_, D_ATT)

def swiglu(x, w_gate, w_up, w_down):
    return (jax.nn.silu(x @ w_gate) * (x @ w_up)) @ w_down

def moe_swiglu(x2d, w_router, w_gate, w_up, w_down):
    n_tok = x2d.shape[0]
    n_asg = n_tok * TOP_K
    logits = (x2d @ w_router).astype(jnp.float32)
    top_vals, top_idx = lax.top_k(logits, TOP_K)
    weights = jax.nn.softmax(top_vals, axis=-1)
    e_flat = top_idx.reshape(-1)
    tok_flat = jnp.arange(n_asg) // TOP_K
    w_flat = weights.reshape(-1)
    order = jnp.argsort(e_flat)
    e_sorted = e_flat[order]
    counts = jnp.bincount(e_flat, length=N_EXPERTS)
    padded = (counts + MOE_BLOCK - 1) // MOE_BLOCK * MOE_BLOCK
    pad_end = jnp.cumsum(padded)
    pad_start = pad_end - padded
    sort_start = jnp.cumsum(counts) - counts
    dest = pad_start[e_sorted] + (jnp.arange(n_asg) - sort_start[e_sorted])
    n_rows = n_asg + N_EXPERTS * MOE_BLOCK
    n_blk = n_rows // MOE_BLOCK
    x_buf = jnp.zeros((n_rows, x2d.shape[1]), x2d.dtype).at[dest].set(x2d[tok_flat[order]])
    tok_buf = jnp.zeros((n_rows,), jnp.int32).at[dest].set(tok_flat[order])
    w_buf = jnp.zeros((n_rows,), jnp.float32).at[dest].set(w_flat[order])
    blk_expert = jnp.minimum(jnp.searchsorted(pad_end, jnp.arange(n_blk) * MOE_BLOCK, side='right'),
                             N_EXPERTS - 1)

    def expert_block(args):
        xb, e = args
        return swiglu(xb, w_gate[e], w_up[e], w_down[e])

    y_buf = lax.map(expert_block, (x_buf.reshape(n_blk, MOE_BLOCK, -1), blk_expert)).reshape(n_rows, -1)
    return jax.ops.segment_sum(y_buf * w_buf[:, None].astype(y_buf.dtype), tok_buf, num_segments=n_tok)

def setup_inputs(seed: int = 0) -> dict:
    key = jax.random.key(seed)
    ks = jax.random.split(key, 32)

    def nrm(k, shape, scale):
        return jax.random.normal(k, shape, jnp.float32) * scale

    u = jax.random.uniform(ks[9], (DEPTH, D_LRU), jnp.float32, minval=0.9, maxval=0.999)
    a0 = u ** (1.0 / LRU_C)
    return {
        'x': nrm(ks[0], (BATCH, SEQ, D_MODEL), 1.0),
        'rel_bias': nrm(ks[1], (N_BUCKETS, N_HEADS), 0.5),
        'norm1_g': 1.0 + nrm(ks[2], (DEPTH, D_MODEL), 0.01),
        'w_in': nrm(ks[3], (DEPTH, D_MODEL, D_IN), D_MODEL ** -0.5),
        'conv_w': nrm(ks[4], (DEPTH, CONV_WIDTH, D_LRU), CONV_WIDTH ** -0.5),
        'conv_b': nrm(ks[5], (DEPTH, D_LRU), 0.01),
        'lru_wa': nrm(ks[6], (DEPTH, LRU_BLOCKS, LRU_BLOCK_W, LRU_BLOCK_W), LRU_BLOCK_W ** -0.5),
        'lru_ba': nrm(ks[7], (DEPTH, D_LRU), 0.01),
        'lru_wx': nrm(ks[8], (DEPTH, LRU_BLOCKS, LRU_BLOCK_W, LRU_BLOCK_W), LRU_BLOCK_W ** -0.5),
        'lru_bx': nrm(ks[10], (DEPTH, D_LRU), 0.01),
        'lru_lambda': jnp.log(a0) - jnp.log1p(-a0),
        'q_norm_g': 1.0 + nrm(ks[11], (DEPTH, HEAD_DIM), 0.01),
        'k_norm_g': 1.0 + nrm(ks[12], (DEPTH, HEAD_DIM), 0.01),
        'cmp_pos': nrm(ks[13], (DEPTH, 2, CMP_BLOCK, HEAD_DIM), 0.02),
        'cmp_w1': nrm(ks[14], (DEPTH, 2, CMP_BLOCK, HEAD_DIM, CMP_HIDDEN), (CMP_BLOCK * HEAD_DIM) ** -0.5),
        'cmp_w2': nrm(ks[15], (DEPTH, 2, CMP_HIDDEN, HEAD_DIM), CMP_HIDDEN ** -0.5),
        'gate_b': nrm(ks[16], (DEPTH, N_BRANCH * N_HEADS), 0.01),
        'out_norm_g': 1.0 + nrm(ks[17], (DEPTH, D_MIX), 0.01),
        'w_out': nrm(ks[18], (DEPTH, D_MIX, D_MODEL), D_MIX ** -0.5),
        'norm2_g': 1.0 + nrm(ks[19], (DEPTH, D_MODEL), 0.01),
        'ffn_w_gate': nrm(ks[20], (N_DENSE, D_MODEL, D_FF), D_MODEL ** -0.5),
        'ffn_w_up': nrm(ks[21], (N_DENSE, D_MODEL, D_FF), D_MODEL ** -0.5),
        'ffn_w_down': nrm(ks[22], (N_DENSE, D_FF, D_MODEL), D_FF ** -0.5),
        'router_w': nrm(ks[23], (N_MOE, D_MODEL, N_EXPERTS), D_MODEL ** -0.5),
        'moe_w_gate': nrm(ks[24], (N_MOE, N_EXPERTS, D_MODEL, D_FF), D_MODEL ** -0.5),
        'moe_w_up': nrm(ks[25], (N_MOE, N_EXPERTS, D_MODEL, D_FF), D_MODEL ** -0.5),
        'moe_w_down': nrm(ks[26], (N_MOE, N_EXPERTS, D_FF, D_MODEL), D_FF ** -0.5),
    }

def reference(x, rel_bias, norm1_g, w_in, conv_w, conv_b, lru_wa, lru_ba, lru_wx, lru_bx,
              lru_lambda, q_norm_g, k_norm_g, cmp_pos, cmp_w1, cmp_w2, gate_b, out_norm_g,
              w_out, norm2_g, ffn_w_gate, ffn_w_up, ffn_w_down, router_w, moe_w_gate,
              moe_w_up, moe_w_down):
    b_, s_, _ = x.shape
    split_at = [D_LRU, OFF_Q, OFF_KV] + [OFF_KV + j * KV_WIDTH for j in range(1, 7)]
    for l in range(DEPTH):
        h = rms_norm(x, norm1_g[l])
        proj = h @ w_in[l]
        (lru_x, lru_gate, q, kc, vc, ksl, vsl, kwn, vwn, gts) = jnp.split(proj, split_at, axis=-1)
        y_lru = lru_group(lru_x, lru_gate, conv_w[l], conv_b[l], lru_wa[l], lru_ba[l],
                          lru_wx[l], lru_bx[l], lru_lambda[l])
        y_att = nsa_group(q, kc, vc, ksl, vsl, kwn, vwn, gts + gate_b[l], q_norm_g[l], k_norm_g[l],
                          cmp_pos[l], cmp_w1[l], cmp_w2[l], rel_bias)
        mix = jnp.concatenate([rms_norm(y_lru, out_norm_g[l, :D_LRU]),
                               rms_norm(y_att, out_norm_g[l, D_LRU:])], axis=-1)
        x = x + mix @ w_out[l]
        h = rms_norm(x, norm2_g[l])
        if l % 2 == 0:
            f = swiglu(h, ffn_w_gate[l // 2], ffn_w_up[l // 2], ffn_w_down[l // 2])
        else:
            f = moe_swiglu(h.reshape(b_ * s_, D_MODEL), router_w[l // 2], moe_w_gate[l // 2],
                           moe_w_up[l // 2], moe_w_down[l // 2]).reshape(b_, s_, D_MODEL)
        x = x + f
    return x


_drawn_inputs = setup_inputs


def setup_inputs(seed=0):
    import zlib

    import numpy as np

    out = dict(_drawn_inputs(seed))
    spreads = {}
    factors = {'norm1_g': 3.047,
     'lru_ba': 7.074,
     'lru_bx': 8.0,
     'q_norm_g': 5.305,
     'k_norm_g': 6.623,
     'gate_b': 7.041,
     'out_norm_g': 3.258,
     'norm2_g': 4.543,
     'cmp_pos': 3.371}
    for name, (base, spread) in spreads.items():
        noise = np.random.default_rng([zlib.crc32(name.encode()), seed]).standard_normal(out[name].shape)
        drawn = base * np.exp(spread * noise) if base else spread * noise
        out[name] = __import__('jax').numpy.asarray(drawn.astype(out[name].dtype))
    for name, factor in factors.items():
        out[name] = (out[name] * factor).astype(out[name].dtype)
    return out
```

```python
from contextlib import ExitStack

import concourse.bass as bass
from concourse import mybir

F32 = mybir.dt.float32
I32 = mybir.dt.int32
U32 = mybir.dt.uint32
ALU = mybir.AluOpType
ACT = mybir.ActivationFunctionType
AX = mybir.AxisListType.X

P = 128
D = 1024
SEQ = 256
NT = SEQ // P
KD = D // P
DEPTH = 2
D_LRU = 512
NC_LRU = D_LRU // P
HD = 64
NH = 8
NG = 2
HPG = NH // NG
CONV = 4
CMP_BLOCK, CMP_STRIDE = 32, 16
N_CMP = (SEQ - CMP_BLOCK) // CMP_STRIDE + 1
CMP_SEEN = (P // CMP_STRIDE - CMP_BLOCK // CMP_STRIDE + 1, N_CMP)
L2 = CMP_BLOCK // 2
N_BUCKETS = 32
D_FF = 2816
NE = 8
D_IN = 2 * D_LRU + NH * HD + 6 * NG * HD + 3 * NH
OFF_Q = 2 * D_LRU
OFF_KV = OFF_Q + NH * HD
W_B = D_IN - OFF_KV - 2 * P
EPS = 1e-6
NEG = -1e30
U_LEN = 3 * P

SLOTS = 4
SLOT = 6 * D
FCOLS = D_FF // 4
FN = FCOLS // 2
FCH = D_FF // FN
FT = D_FF // P
DOWN = (6, 6, 6, 4)
HALF = FCH // 2
MIX_PIECES = 7
FFN_PIECES = 8 + len(DOWN)
ARENA = 17100
ROUTED0 = 2 * MIX_PIECES + FFN_PIECES
OVER = 3
JOBS = NE + OVER

R_G1, R_G2, R_OG = 0, 16, 32
R_CW, R_CB, R_BA, R_BX, R_LAM = 48, 80, 88, 96, 104
R_QG, R_KG, N_ROWS = 112, 114, 116


def done_tiles(c):
    return c * FN // P


def build(nc, x, rel_bias, norm1_g, w_in, conv_w, conv_b, lru_wa, lru_ba, lru_wx, lru_bx, lru_lambda,
          q_norm_g, k_norm_g, cmp_pos, cmp_w1, cmp_w2, gate_b, out_norm_g, w_out, norm2_g,
          ffn_w_gate, ffn_w_up, ffn_w_down, router_w, moe_w_gate, moe_w_up, moe_w_down,
          bucket_rows, out):
    ctx = ExitStack()
    with ctx:
        def sb(name, shape, dt=F32):
            return ctx.enter_context(nc.sbuf_tensor(name, shape, dt))

        def sem(name):
            return ctx.enter_context(nc.semaphore(name))

        ring = sb("ring", [P, SLOTS, SLOT])
        xs = sb("xs", [P, NT, D])
        xn = sb("xn", [P, NT, D])
        hT = sb("hT", [P, KD, SEQ])
        biasU = sb("biasU", [P, NH, 2 * P])
        ident = sb("ident", [P, P])
        flip = sb("flip", [P, P])
        ones = sb("ones", [P, P])
        before = sb("before", [P, P])
        slot_id = sb("slot_id", [P, P])
        prow = sb("prow", [N_ROWS, P])
        par = sb("par", [P, N_ROWS])
        posr = sb("posr", [HD, P])
        posT = sb("posT", [P, HD])
        gateb = sb("gateb", [P, DEPTH, 3 * NH])
        bucketT = sb("bucketT", [N_BUCKETS + 1, U_LEN])
        relb = sb("relb", [N_BUCKETS + 1, NH])
        urow = sb("urow", [NH, U_LEN])
        lruW = sb("lruW", [P, 2, NC_LRU, P])
        w2 = sb("w2", [P, DEPTH, 2, HD])
        rw = sb("rw", [P, KD, NE])
        nba = sb("nba", [P, 2, DEPTH * NC_LRU])
        sp4 = sb("sp4", [P, DEPTH * NC_LRU])
        cEPS = sb("cEPS", [P, 1])
        ssq = sb("ssq", [P, NT])
        rstd = sb("rstd", [P, NT])

        arena = sb("arena", [P, ARENA])
        at = [0]

        def mix(n, *dims):
            v = arena[:, at[0]:at[0] + n]
            at[0] += n
            assert at[0] <= ARENA
            if len(dims) == 2:
                v = v.rearrange("p (a b) -> p a b", a=dims[0])
            if len(dims) == 3:
                v = v.rearrange("p (a b c) -> p a b c", a=dims[0], b=dims[1])
            return v

        tok = mix(NT * 1304, NT, 1304)
        qn = mix(NT * 512, NT, HPG, P)
        kn = mix(NT * 256, NT, 2, P)
        sq = mix(NT * 1280, NT, 1280)
        qT = mix(HPG * SEQ, HPG, SEQ)
        kT = mix(2 * SEQ, 2, SEQ)
        kcv2 = mix(2 * NG * P, 2, NG, P)
        blk = mix(2 * L2 * NG * N_CMP, 2, L2 * NG * N_CMP)
        xpad = mix(NC_LRU * (SEQ + 4), NC_LRU, SEQ + 4)
        gT = mix(NC_LRU * SEQ, NC_LRU, SEQ)
        xc = mix(NC_LRU * SEQ, NC_LRU, SEQ)
        rr = arena[:, NT * 1304 + NT * 768:][:, 0:NC_LRU * SEQ].rearrange("p (a b) -> p a b", a=NC_LRU)
        ii = arena[:, NT * 1304 + NT * 768 + 1024:][:, 0:NC_LRU * SEQ].rearrange("p (a b) -> p a b", a=NC_LRU)
        aa = mix(NC_LRU * SEQ, NC_LRU, SEQ)
        tt = mix(NC_LRU * SEQ, NC_LRU, SEQ)
        sS = xn[:, 0, :].rearrange("p (b c) -> p b c", b=2)
        sP = xn[:, 1, :].rearrange("p (b c) -> p b c", b=2)
        skew = arena[:, at[0] - 2 * NC_LRU * SEQ:at[0]]
        sT = mix(2 * 512, 2, 512)
        cS = mix(NT * NH * 16, NT, NH, 16)
        small = mix(896)
        oS = arena[:, 0:NT * 512].rearrange("p (a b) -> p a b", a=NT)
        mixT = hT
        rms20 = small[:, 0:40].rearrange("p (a b) -> p a b", a=NT)
        gsig = small[:, 40:88].rearrange("p (a b) -> p a b", a=NT)
        hc = small[:, 88:148]
        hc2 = small[:, 148:208]
        hct = small[:, 208:268]
        kcn = small[0:NG * N_CMP, 268:396]
        kcsq = small[0:NG * N_CMP, 396:460]
        kcs = small[0:NG * N_CMP, 460:461]
        kcT = small[:, 462:492]
        vcs = small[0:N_CMP, 492:620]
        mx = small[:, 620:652]
        den = small[:, 652:684]
        cmx = small[:, 684:700]
        cden = small[:, 700:716]
        nrm = small[:, 716:724]
        cPT = hT[0:N_CMP].rearrange("p k (a q) -> p (k a) q", a=2)

        at[0] = 0
        hid = mix(NT * HALF * FN, NT, HALF * FN)
        sil = mix(2 * FN, 2, FN)
        hidT = mix(NT * FT * P, NT, FT, P)
        xg = mix(KD * P, KD, P)
        ye = mix(D)
        selM = mix(NT * P, NT, P)
        selW = mix(NT * P, NT, P)
        selT = mix(NT * P, NT, P)
        rt = mix(600)
        logit = rt[:, 0:16].rearrange("p (a b) -> p a b", a=NT)
        top8 = rt[:, 16:32].rearrange("p (a b) -> p a b", a=NT)
        idx8 = sb("idx8", [P, NT, 8], U32)
        idxf = rt[:, 32:48].rearrange("p (a b) -> p a b", a=NT)
        oh1 = rt[:, 48:64].rearrange("p (a b) -> p a b", a=NT)
        oh2 = rt[:, 64:80].rearrange("p (a b) -> p a b", a=NT)
        memb = rt[:, 80:96].rearrange("p (a b) -> p a b", a=NT)
        wexp = rt[:, 96:112].rearrange("p (a b) -> p a b", a=NT)
        pos = rt[:, 112:128].rearrange("p (a b) -> p a b", a=NT)
        wt = rt[:, 128:136]
        over = rt[:, 136:144]
        rank = rt[:, 144:152]
        pick = rt[:, 152:160]
        junk = rt[:, 160:176].rearrange("p (a b) -> p a b", a=NT)
        table = rt[:, 176:176 + 6 * JOBS].rearrange("p (j c) -> p j c", c=6)
        job = rt[:, 250:256]
        jobf = rt[:, 256:256 + JOBS + 1]
        jobi = sb("jobi", [P, JOBS + 2], I32)

        bank = [ctx.enter_context(nc.psum_tensor(f"bank{i}", [P, 512], F32)) for i in range(8)]

        urows_dram = nc.dram_tensor("urows", (NH, U_LEN), F32, kind="Internal").ap()

        names = """small_loaded relb_loaded rows_stored skew_loaded flip_done bias_ready lru_w_loaded gate_used down_used out_stored
            x_loaded consts_set params_transposed params_ready urow_done urow_ready
            root_done norm_ready normT_done hT_act hT_dve q_done kc_done kv_done gates_done lrux_done lrug_done
            tok_act tok_dve lrux_ready gate_ready
            qk_root_in qk_root qk_ready T_done qT_ready kT_ready kcv_ready blk_ready cmph_done hc_ready gelu_c_in gelu_c_th gelu_c_ready
            kc_done2 vc_ready kcn_in kcn_root kcn_ready kcT_done kcT_ready
            conv_ready rgate_done igate_done exp_r exp_i pre_sig sig_ready tanh_r pre_rec rec_ready sqrt_t mult_ready scan_ready
            gelu_in gelu_th gelu_ready ysq_ready ymix_ready
            gs_in gs_exp gs_ready cs_done cs_in cs_exp cp_ready cpT_done cpT_ready
            s_done s_ready e_ready p_ready pT_done pT_ready o_done o_ready oT_done oT_ready lsum_done mroot_in mroot rout_ready
            out_done x_mixed
            xg_done xg_ready gu_done silu_ready hid_ready hidT_done hidT_ready y_done y_ready comb_done comb_ready sel_ready selT_done selT_ready
            log_done job_ready texp_in texp pos_in pos_done jobs_ready ffn_done
            act_chain dve_chain pool_chain""".split()
        S = {n: sem(n) for n in names}
        loaded = [sem(f"slot{i}_loaded") for i in range(SLOTS)]

        def piece_at(p):
            return ring[:, p % SLOTS, :]

        def ring3(p, a, b):
            return piece_at(p)[:, 0:a * b].rearrange("p (a b) -> p a b", a=a)

        def wait_piece(eng, p):
            eng.wait_ge(loaded[p % SLOTS], 16 * (p // SLOTS + 1))

        block = ctx.enter_context(nc.Block())

        @block.sync
        def _(sp):
            sp.dma_start(xs[:, :, :], x[0].rearrange("(t p) d -> p t d", p=P)).then_inc(S["x_loaded"], 16)

            def freed(p):
                l, i = divmod(p, MIX_PIECES + FFN_PIECES)
                if i < MIX_PIECES:
                    return [("kc_done", l + 1), ("gates_done", 2 * l + 2), ("lrux_done", 2 * l + 2), ("lrug_done", 2 * l + 2),
                            ("cmph_done", l + 1), ("out_done", 8 * l + 4), ("out_done", 8 * l + 8)][i]
                i -= MIX_PIECES
                if i < 8:
                    return ("gate_used", i // 2 + 1) if i % 2 == 0 else ("gu_done", NT * (i + 1))
                return ("down_used", i - 7) if i < FFN_PIECES - 1 else ("y_done", NT)

            def load(p, dst, src):
                if p >= SLOTS:
                    name, count = freed(p - SLOTS)
                    sp.wait_ge(S[name], count)
                sp.dma_start(dst, src).then_inc(loaded[p % SLOTS], 16)

            def load_mix(l, p):
                wi = w_in[l].rearrange("(k p) n -> p k n", p=P)
                load(p, ring3(p, KD, 768), wi[:, :, OFF_Q:OFF_Q + 768])
                load(p + 1, ring3(p + 1, KD, W_B), wi[:, :, OFF_Q + 768:D_IN])
                load(p + 2, ring3(p + 2, KD, 512), wi[:, :, 0:D_LRU])
                load(p + 3, ring3(p + 3, KD, 512), wi[:, :, D_LRU:2 * D_LRU])
                load(p + 4, ring3(p + 4, 2 * L2, P), cmp_w1[l].rearrange("v (m e) d c -> (e d) (v m) c", e=2))
                wo = w_out[l].rearrange("(k p) n -> p k n", p=P)
                load(p + 5, ring3(p + 5, 4, D), wo[:, 0:4, :])
                load(p + 6, ring3(p + 6, 4, D), wo[:, 4:8, :])

            def ffn_piece(p, i, wg, wu, wd):
                if i < 8:
                    w = (wg, wu)[i % 2].rearrange("(k p) n -> p k n", p=P)
                    return ring3(p + i, KD, FCOLS), w[:, :, i // 2 * FCOLS:(i // 2 + 1) * FCOLS]
                n, t = DOWN[i - 8], sum(DOWN[:i - 8])
                return ring3(p + i, n, D), wd.rearrange("(t p) n -> p t n", p=P)[:, t:t + n, :]

            load_mix(0, 0)
            for i in range(FFN_PIECES):
                load(MIX_PIECES + i, *ffn_piece(MIX_PIECES, i, ffn_w_gate[0], ffn_w_up[0], ffn_w_down[0]))
            load_mix(1, MIX_PIECES + FFN_PIECES)
            for i in range(SLOTS):
                load(ROUTED0 + i, *ffn_piece(ROUTED0, i, moe_w_gate[0, 0], moe_w_up[0, 0], moe_w_down[0, 0]))
            sp.wait_ge(S["jobs_ready"], 1)
            njobs = sp.value_load(jobi[0:1, 0:1], min_val=NE, max_val=JOBS)
            def weights_of(j):
                e = sp.value_load(jobi[0:1, bass.ds(j + 1, 1)], min_val=0, max_val=NE - 1)
                first = sp.snap(e * (D * D_FF))
                row_reg = sp.to_reg(first + D)
                row = sp.snap(row_reg, min_val=D, max_val=(NE - 1) * D * D_FF + D)
                return [bass.AP(m.tensor, o, [[n, r], [1, n]]) for m, o, r, n in
                        ((moe_w_gate, row - D, D, D_FF), (moe_w_up, row - D, D, D_FF), (moe_w_down, row - D, D_FF, D))]

            def load_job(i, w, freed, count):
                sp.wait_ge(S[freed], count)
                dst, src = ffn_piece(ROUTED0, i, *w)
                sp.dma_start(dst, src).then_inc(loaded[(ROUTED0 + i) % SLOTS], 16)

            with sp.Fori(0, njobs) as j:
                w = weights_of(j)
                for k in range(FFN_PIECES - SLOTS):
                    if k % 2 == 0:
                        load_job(k + SLOTS, w, "gate_used", j * 4 + (4 + k // 2 + 1))
                    else:
                        load_job(k + SLOTS, w, "gu_done", j * FCH + (NT * FCH + k + 1))
                with sp.If(j + 1 < njobs):
                    w = weights_of(j + 1)
                    for k in range(len(DOWN) - 1):
                        load_job(k, w, "down_used", j * (len(DOWN) - 1) + (len(DOWN) - 1 + k + 1))
                    load_job(SLOTS - 1, w, "y_done", j + (NT + 1))
            sp.wait_ge(S["comb_ready"], njobs * 4)
            sp.dma_start(out[0].rearrange("(t p) d -> p t d", p=P), xs[:, :, :]).then_inc(S["out_stored"], 16)
            sp.wait_ge(S["out_stored"], 16)

        @block.gpsimd
        def _(pool):
            chain = [0]

            def link(ins):
                chain[0] += 1
                ins.then_inc(S["pool_chain"], 1)
                pool.wait_ge(S["pool_chain"], chain[0])

            link(pool.memset(relb[:, :], NEG))
            pool.dma_start(relb[0:N_BUCKETS, :], rel_bias).then_inc(S["relb_loaded"], 16)
            pool.dma_start(bucketT[:, :], bucket_rows).then_inc(S["relb_loaded"], 16)
            rows = [(R_G1, norm1_g.rearrange("l (k p) -> (l k) p", p=P)), (R_G2, norm2_g.rearrange("l (k p) -> (l k) p", p=P)),
                    (R_OG, out_norm_g.rearrange("l (k p) -> (l k) p", p=P)),
                    (R_CW, conv_w.rearrange("l w (k p) -> (l w k) p", p=P)), (R_CB, conv_b.rearrange("l (k p) -> (l k) p", p=P)),
                    (R_BA, lru_ba.rearrange("l (k p) -> (l k) p", p=P)), (R_BX, lru_bx.rearrange("l (k p) -> (l k) p", p=P)),
                    (R_LAM, lru_lambda.rearrange("l (k p) -> (l k) p", p=P))]
            for r, src in rows:
                pool.dma_start(prow[r:r + src.shape[0], :], src).then_inc(S["small_loaded"], 16)
            for half in range(2):
                pool.dma_start(prow[R_QG:R_QG + 2, half * HD:(half + 1) * HD], q_norm_g).then_inc(S["small_loaded"], 16)
                pool.dma_start(prow[R_KG:R_KG + 2, half * HD:(half + 1) * HD], k_norm_g).then_inc(S["small_loaded"], 16)
            pool.dma_start(posr[:, :], cmp_pos.rearrange("l v (m e) d -> (l v m) (e d)", e=2)).then_inc(S["small_loaded"], 16)
            pool.dma_start(gateb[:, :, :], gate_b.partition_broadcast(P)).then_inc(S["small_loaded"], 16)
            pool.dma_start(w2[:, :, :, :], cmp_w2.rearrange("l v c d -> c l v d")).then_inc(S["small_loaded"], 16)
            pool.dma_start(rw[:, :, :], router_w[0].rearrange("(k p) e -> p k e", p=P)).then_inc(S["small_loaded"], 16)
            link(pool.memset(ident[:, :], 0.0))
            link(pool.affine_select(out=ident[:, :], in_=ident[:, :], compare_op=ALU.not_equal, fill=1.0, base=0,
                                    pattern=[[-1, P]], channel_multiplier=1))
            link(pool.memset(flip[:, :], 0.0))
            link(pool.affine_select(out=flip[:, :], in_=flip[:, :], compare_op=ALU.not_equal, fill=1.0, base=1 - P,
                                    pattern=[[1, P]], channel_multiplier=1))
            link(pool.memset(ones[:, :], 1.0))
            link(pool.affine_select(out=before[:, :], in_=ones[:, :], compare_op=ALU.is_gt, fill=0.0, base=0,
                                    pattern=[[1, P]], channel_multiplier=-1))
            link(pool.iota(slot_id[:, :], pattern=[[1, P]], base=0, channel_multiplier=0,
                           allow_small_or_imprecise_dtypes=True))
            link(pool.memset(cEPS[:, :], EPS))
            pool.memset(lruW[:, :, :, :], 0.0).then_inc(S["consts_set"], 1)
            pool.wait_ge(S["consts_set"], 1)
            pool.wait_ge(S["urow_ready"], 1)
            pool.dma_start(urows_dram, urow[:, :]).then_inc(S["rows_stored"], 16)
            pool.wait_ge(S["rows_stored"], 16)
            pool.dma_start(skew.rearrange("p (h i) -> p h i", h=NH), bass.AP(urows_dram.tensor, 0, [[1, P], [U_LEN, NH], [1, 2 * P]]))\
                .then_inc(S["skew_loaded"], 16)

            for l in range(DEPTH):
                L = l + 1
                if l > 0:
                    pool.wait_ge(S["igate_done"], l)
                for e in range(2):
                    for w, src in enumerate((lru_wa, lru_wx)):
                        pool.dma_start(lruW[e * HD:(e + 1) * HD, w, :, e * HD:(e + 1) * HD],
                                       src[l].rearrange("(m e) i j -> e i m j", e=2)[e]).then_inc(S["lru_w_loaded"], 16)
                pool.wait_ge(S["gate_ready"], L)
                link(pool.tensor_tensor(tt, gT, gT, ALU.mult))
                link(pool.tensor_scalar(tt, tt, 0.044715, 1.0, ALU.mult, ALU.add))
                pool.tensor_tensor(tt, tt, gT, ALU.mult).then_inc(S["gelu_in"], 1)
                pool.wait_ge(S["gelu_th"], L)
                link(pool.tensor_scalar(tt, tt, 1.0, 0.5, ALU.add, ALU.mult))
                link(pool.tensor_tensor(gT, gT, tt, ALU.mult))
                pool.wait_ge(S["exp_r"], L)
                link(pool.tensor_scalar(rr, rr, 1.0, None, ALU.add))
                pool.wait_ge(S["exp_i"], L)
                pool.tensor_scalar(ii, ii, 1.0, None, ALU.add).then_inc(S["pre_sig"], 1)
                pool.wait_ge(S["sig_ready"], L)
                link(pool.tensor_tensor(ii, ii, xc, ALU.mult))
                pool.wait_ge(S["tanh_r"], L)
                pool.tensor_scalar(aa, rr, 1.0, None, ALU.add).then_inc(S["pre_rec"], 1)
                pool.wait_ge(S["rec_ready"], L)
                link(pool.tensor_tensor(ii, ii, aa, ALU.mult))
                pool.wait_ge(S["sqrt_t"], L)
                link(pool.tensor_tensor(ii, ii, tt, ALU.mult))
                link(pool.tensor_scalar(ii, ii, 2.0, None, ALU.mult))
                link(pool.tensor_scalar(rr, rr, -1.0, 1.0, ALU.mult, ALU.add))
                pool.tensor_tensor(aa, aa, rr, ALU.mult).then_inc(S["mult_ready"], 1)
                pool.wait_ge(S["scan_ready"], L)
                link(pool.tensor_tensor(xc, gT, tt, ALU.mult))
                pool.tensor_tensor(tt, xc, xc, ALU.mult).then_inc(S["ysq_ready"], 1)

        @block.scalar
        def _(act):
            chain = [0]

            def link(ins):
                chain[0] += 1
                ins.then_inc(S["act_chain"], 1)
                act.wait_ge(S["act_chain"], chain[0])

            def norm_root(n):
                if n == 0:
                    act.wait_ge(S["x_loaded"], 16)
                    act.wait_ge(S["consts_set"], 1)
                elif n % 2 == 1:
                    act.wait_ge(S["x_mixed"], n // 2 + 1)
                else:
                    act.wait_ge(S["ffn_done"], n // 2)
                for t in range(NT):
                    link(act.activation(xn[:, t, :], xs[:, t, :], ACT.Square, accum_out=ssq[:, t:t + 1]))
                act.activation(rstd[:, :], ssq[:, :], ACT.Sqrt, scale=1.0 / D, bias=cEPS[:, :]).then_inc(S["root_done"], 1)

            def norm_turned(n, row):
                for k in range(4):
                    act.wait_ge(S["normT_done"], 4 * n + k // 2 + 1)
                    act.activation(hT[:, k, :], bank[k // 2][:, (k % 2) * SEQ:(k % 2 + 1) * SEQ], ACT.Copy,
                                   scale=par[:, row + k:row + k + 1]).then_inc(S["hT_act"], 1)

            act.wait_ge(S["params_transposed"], 1)
            act.activation(par[:, :], bank[0][:, 0:N_ROWS], ACT.Copy).then_inc(S["params_ready"], 1)
            act.activation(posT[:, :], bank[0][:, 128:128 + HD], ACT.Copy).then_inc(S["params_ready"], 1)
            act.wait_ge(S["urow_done"], 1)
            act.activation(urow[:, :], bank[1][0:NH, 0:U_LEN], ACT.Copy).then_inc(S["urow_ready"], 1)
            act.wait_ge(S["params_ready"], 2)
            for w, r in ((0, R_BA), (1, R_BX)):
                link(act.activation(nba[:, w, :], par[:, r:r + 8], ACT.Copy, scale=-1.0))
            link(act.activation(sp4[:, :], par[:, R_LAM:R_LAM + 8], ACT.Exp, scale=-1.0))
            link(act.activation(sp4[:, :], sp4[:, :], ACT.Ln, bias=1.0))
            link(act.activation(sp4[:, :], sp4[:, :], ACT.Copy, scale=4.0))

            for l in range(DEPTH):
                L = l + 1
                norm_root(2 * l)
                norm_turned(2 * l, R_G1 + 8 * l)
                if l == 0:
                    for c in range(4):
                        act.wait_ge(S["flip_done"], c + 1)
                        act.activation(biasU[:, 2 * c:2 * c + 2, :], bank[4 + c][:, :].rearrange("p (a b) -> p a b", a=2), ACT.Copy)\
                            .then_inc(S["bias_ready"], 1)
                act.wait_ge(S["q_done"], 2 * l + 1)
                act.activation(tok[:, 0, 0:512], bank[4][:, :], ACT.Copy).then_inc(S["tok_act"], 1)
                act.wait_ge(S["kv_done"], 2 * l + 1)
                act.activation(tok[:, 0, 768:1280], bank[0][:, :], ACT.Copy).then_inc(S["tok_act"], 1)
                act.wait_ge(S["gates_done"], 2 * l + 1)
                act.activation(tok[:, 0, 512:768], bank[6][:, 0:256], ACT.Copy).then_inc(S["tok_act"], 1)
                act.activation(tok[:, 0, 1280:1304], bank[6][:, 256:280], ACT.Copy).then_inc(S["tok_act"], 1)
                for m in range(NC_LRU):
                    act.wait_ge(S["lrux_done"], 2 * l + m // 2 + 1)
                    act.activation(xpad[:, m, 3:3 + SEQ], bank[2 + m // 2][:, (m % 2) * SEQ:(m % 2 + 1) * SEQ], ACT.Copy)\
                        .then_inc(S["lrux_ready"], 1)
                act.wait_ge(S["qk_root_in"], L)
                act.activation(rms20, rms20, ACT.Sqrt, scale=1.0 / HD, bias=cEPS[:, :]).then_inc(S["qk_root"], 1)
                for m in range(2):
                    act.wait_ge(S["lrug_done"], 2 * l + m + 1)
                    last = act.activation(gT[:, 2 * m:2 * m + 2, :], bank[4 + m][:, :].rearrange("p (a b) -> p a b", a=2), ACT.Copy)
                    if m == 0:
                        link(last)
                    else:
                        last.then_inc(S["gate_ready"], 1)
                for b in range(2):
                    act.wait_ge(S["T_done"], 4 * l + b + 1)
                    act.activation(qT[:, 2 * b:2 * b + 2, :], bank[6 + b][:, :].rearrange("p (a b) -> p a b", a=2), ACT.Copy,
                                   scale=par[:, R_QG + l:R_QG + l + 1]).then_inc(S["qT_ready"], 1)
                act.wait_ge(S["gs_in"], L)
                act.activation(gsig, gsig, ACT.Exp, scale=-1.0).then_inc(S["gs_exp"], 1)
                act.wait_ge(S["gelu_in"], L)
                act.activation(tt, tt, ACT.Tanh, scale=0.7978845608028654).then_inc(S["gelu_th"], 1)
                act.wait_ge(S["gelu_c_in"], L)
                act.activation(hct, hc2, ACT.Tanh, scale=0.7978845608028654).then_inc(S["gelu_c_th"], 1)
                for w, (done, dst, exp, b0) in enumerate((("rgate_done", rr, "exp_r", 4), ("igate_done", ii, "exp_i", 0))):
                    act.wait_ge(S[done], L)
                    for m in range(NC_LRU):
                        last = act.activation(dst[:, m, :], bank[b0 + m // 2][:, (m % 2) * SEQ:(m % 2 + 1) * SEQ], ACT.Exp,
                                              scale=-1.0, bias=nba[:, w, l * NC_LRU + m:l * NC_LRU + m + 1])
                        if m < NC_LRU - 1:
                            link(last)
                    last.then_inc(S[exp], 1)
                act.wait_ge(S["sig_ready"], L)
                for m in range(NC_LRU):
                    last = act.activation(rr[:, m, :], rr[:, m, :], ACT.Tanh, scale=sp4[:, l * NC_LRU + m:l * NC_LRU + m + 1])
                    if m < NC_LRU - 1:
                        link(last)
                last.then_inc(S["tanh_r"], 1)
                act.wait_ge(S["kcn_in"], L)
                act.activation(kcs, kcs, ACT.Sqrt, scale=1.0 / HD, bias=cEPS[0:NG * N_CMP, :]).then_inc(S["kcn_root"], 1)
                act.wait_ge(S["tanh_r"], L)
                act.wait_ge(S["gelu_th"], L)
                act.wait_ge(S["rec_ready"], L)
                act.activation(tt, rr, ACT.Sqrt).then_inc(S["sqrt_t"], 1)
                act.wait_ge(S["cs_in"], L)
                act.activation(cS, cS, ACT.Exp).then_inc(S["cs_exp"], 1)
                for c in range(4):
                    act.wait_ge(S["cpT_done"], 4 * l + c + 1)
                    act.activation(cPT[:, 4 * c:4 * c + 4, :], bank[c % 2][0:N_CMP, :].rearrange("p (a b) -> p a b", a=4), ACT.Copy)\
                        .then_inc(S["cpT_ready"], 1)
                for i in range(NT * NH + 1):
                    if i < NT * NH:
                        W = P * (i // NH + 1)
                        n = NT * NH * l + i
                        act.wait_ge(S["s_ready"], n + 1)
                        if i >= 2:
                            act.wait_ge(S["pT_done"], n - 1)
                        for b in range(2):
                            last = act.activation(sP[:, i % 2, b * W:(b + 1) * W], sS[:, i % 2, b * W:(b + 1) * W], ACT.Exp,
                                                  bias=mx[:, 16 * (i % 2) + b:16 * (i % 2) + b + 1],
                                                  accum_out=den[:, 16 * (i % 2) + b:16 * (i % 2) + b + 1])
                            if b == 0:
                                link(last)
                        last.then_inc(S["e_ready"], 1)
                    if i >= 1:
                        k = i - 1
                        n = NT * NH * l + k
                        W = P * (k // NH + 1)
                        act.wait_ge(S["pT_done"], n + 1)
                        if k >= 2:
                            act.wait_ge(S["o_done"], n - 1)
                        act.activation(sT[:, k % 2, 0:2 * W], bank[2 + k % 2][:, 0:2 * W], ACT.Copy).then_inc(S["pT_ready"], 1)
                for t in range(NT):
                    act.wait_ge(S["o_done"], NT * NH * l + NH * (t + 1))
                    link(act.activation(oS[:, t, :], bank[4 + t][:, :], ACT.Copy))
                    act.activation(sS[:, 0, :], oS[:, t, :], ACT.Square, accum_out=nrm[:, t:t + 1]).then_inc(S["o_ready"], 1)
                act.wait_ge(S["lsum_done"], L)
                act.activation(nrm[:, 2:4], bank[1][:, 0:2], ACT.Copy).then_inc(S["mroot_in"], 1)
                act.wait_ge(S["mroot_in"], L)
                act.wait_ge(S["o_ready"], 2 * L)
                act.activation(nrm[:, 4:8], nrm[:, 0:4], ACT.Sqrt, scale=1.0 / D_LRU, bias=cEPS[:, :]).then_inc(S["mroot"], 1)
                act.wait_ge(S["ysq_ready"], L)
                for m in range(NC_LRU):
                    act.activation(mixT[:, m, :], xc[:, m, :], ACT.Copy,
                                   scale=par[:, R_OG + 8 * l + m:R_OG + 8 * l + m + 1]).then_inc(S["ymix_ready"], 1)
                for m in range(4):
                    act.wait_ge(S["oT_done"], 2 * l + m // 2 + 1)
                    act.activation(mixT[:, 4 + m, :], bank[6 + m // 2][:, (m % 2) * SEQ:(m % 2 + 1) * SEQ], ACT.Copy,
                                   scale=par[:, R_OG + 8 * l + 4 + m:R_OG + 8 * l + 5 + m]).then_inc(S["oT_ready"], 1)
                norm_root(2 * l + 1)
                norm_turned(2 * l + 1, R_G2 + 8 * l)
                if l == 0:
                    for s in range(NT * FCH):
                        act.wait_ge(S["gu_done"], s + 1)
                        if s >= 2:
                            act.wait_ge(S["hid_ready"], s - 1)
                        act.activation(sil[:, s % 2, :], bank[2 * (s % 2)][:, 0:FN], ACT.Silu).then_inc(S["silu_ready"], 1)
                else:
                    act.wait_ge(S["texp_in"], 1)
                    act.activation(wt[:, 0:2], wt[:, 0:2], ACT.Exp).then_inc(S["texp"], 1)
                    act.wait_ge(S["jobs_ready"], 1)
                    njobs = act.value_load(jobi[0:1, 0:1], min_val=NE, max_val=JOBS)
                    with act.Fori(0, njobs) as j:
                        for c in range(2):
                            act.wait_ge(S["xg_done"], 2 * j + (c + 1))
                            for k in range(4 * c, 4 * c + 4):
                                act.activation(xg[:, k, :], bank[4 + c][:, (k % 4) * P:(k % 4 + 1) * P], ACT.Copy,
                                               scale=par[:, R_G2 + 8 + k:R_G2 + 9 + k]).then_inc(S["xg_ready"], 1)
                        for s in range(FCH):
                            act.wait_ge(S["gu_done"], j * FCH + (NT * FCH + s + 1))
                            act.wait_ge(S["hid_ready"], j * FCH + (NT * FCH + s - 1))
                            act.activation(sil[:, s % 2, :], bank[2 * (s % 2)][:, 0:FN], ACT.Silu).then_inc(S["silu_ready"], 1)

        @block.vector
        def _(dve):
            chain = [0]

            def link(ins):
                chain[0] += 1
                ins.then_inc(S["dve_chain"], 1)
                dve.wait_ge(S["dve_chain"], chain[0])

            def norm(n, row):
                dve.wait_ge(S["root_done"], n + 1)
                link(dve.reciprocal(rstd[:, :], rstd[:, :]))
                for t in range(NT):
                    dve.tensor_scalar(xn[:, t, :], xs[:, t, :], rstd[:, t:t + 1], None, ALU.mult).then_inc(S["norm_ready"], 1)
                for k in range(4, 8):
                    dve.wait_ge(S["normT_done"], 4 * n + k // 2 + 1)
                    dve.tensor_scalar(hT[:, k, :], bank[k // 2][:, (k % 2) * SEQ:(k % 2 + 1) * SEQ],
                                      par[:, row + k:row + k + 1], None, ALU.mult).then_inc(S["hT_dve"], 1)

            dve.wait_ge(S["params_ready"], 2)
            for l in range(DEPTH):
                L = l + 1
                norm(2 * l, R_G1 + 8 * l)
                link(dve.memset(xpad[:, :, 0:3], 0.0))
                dve.wait_ge(S["q_done"], 2 * l + 2)
                dve.tensor_copy(tok[:, 1, 0:512], bank[5][:, :]).then_inc(S["tok_dve"], 1)
                dve.wait_ge(S["kv_done"], 2 * l + 2)
                dve.tensor_copy(tok[:, 1, 768:1280], bank[1][:, :]).then_inc(S["tok_dve"], 1)
                dve.wait_ge(S["gates_done"], 2 * l + 2)
                dve.tensor_copy(tok[:, 1, 512:768], bank[7][:, 0:256]).then_inc(S["tok_dve"], 1)
                dve.tensor_copy(tok[:, 1, 1280:1304], bank[7][:, 256:280]).then_inc(S["tok_dve"], 1)
                dve.wait_ge(S["tok_dve"], 4 * L)
                dve.wait_ge(S["tok_act"], 4 * L)
                for t in range(NT):
                    link(dve.tensor_tensor(sq[:, t, :], tok[:, t, 0:1280], tok[:, t, 0:1280], ALU.mult))
                for t in range(NT):
                    last = dve.tensor_reduce(rms20[:, t, :], sq[:, t, :].rearrange("p (a b) -> p a b", b=HD), AX, ALU.add)
                    if t == 0:
                        link(last)
                last.then_inc(S["qk_root_in"], 1)
                dve.wait_ge(S["qk_root"], L)
                link(dve.reciprocal(rms20, rms20))
                for t in range(NT):
                    link(dve.tensor_tensor(qn[:, t].rearrange("p h (g d) -> p h g d", g=NG),
                                           tok[:, t, 0:512].rearrange("p (g h d) -> p h g d", g=NG, h=HPG),
                                           rms20[:, t, 0:8].rearrange("p (g h a) -> p h g a", g=NG, a=1)
                                           .to_broadcast([P, HPG, NG, HD]), ALU.mult))
                    kk = tok[:, t, 768:1280].rearrange("p (b c g d) -> p b c g d", b=2, c=2, g=NG)[:, :, 0]
                    rk = rms20[:, t, 12:20].rearrange("p (b c g a) -> p b c g a", b=2, c=2, g=NG)[:, :, 0]
                    last = dve.tensor_tensor(kn[:, t].rearrange("p b (g d) -> p b g d", g=NG), kk,
                                             rk.to_broadcast([P, 2, NG, HD]), ALU.mult)
                    if t == 0:
                        link(last)
                last.then_inc(S["qk_ready"], 1)
                dve.tensor_tensor(gsig, tok[:, :, 1280:1304], gateb[:, l:l + 1, :].to_broadcast([P, NT, 3 * NH]),
                                  ALU.add).then_inc(S["gs_in"], 1)
                dve.wait_ge(S["lrux_ready"], 4 * L)
                for m in range(NC_LRU):
                    cw = [par[:, R_CW + 16 * l + 4 * w + m:R_CW + 16 * l + 4 * w + m + 1] for w in range(CONV)]
                    cb = par[:, R_CB + 4 * l + m:R_CB + 4 * l + m + 1]
                    link(dve.tensor_scalar(xc[:, m, :], xpad[:, m, 0:SEQ], cw[0], cb, ALU.mult, ALU.add))
                    for w in range(1, CONV):
                        last = dve.scalar_tensor_tensor(xc[:, m, :], xpad[:, m, w:w + SEQ], cw[w], xc[:, m, :], ALU.mult, ALU.add)
                        if w < CONV - 1:
                            link(last)
                    last.then_inc(S["conv_ready"], 1)
                dve.wait_ge(S["T_done"], 4 * l + 3)
                dve.tensor_scalar(kT, bank[0][:, :].rearrange("p (a b) -> p a b", a=2), par[:, R_KG + l:R_KG + l + 1], None,
                                  ALU.mult).then_inc(S["kT_ready"], 1)
                dve.wait_ge(S["T_done"], 4 * l + 4)
                for e in range(2):
                    for g in range(NG):
                        last = dve.tensor_copy(
                            kcv2[e * HD:(e + 1) * HD, :, g, :],
                            bank[1][g * HD:(g + 1) * HD, :].rearrange("p (v t e) -> p v t e", v=2, e=2)[:, :, :, e])
                        if (e, g) != (1, 1):
                            link(last)
                last.then_inc(S["kcv_ready"], 1)
                dve.wait_ge(S["kcv_ready"], L)
                for v in range(2):
                    s0 = kcv2[:, v, 0, 0:1]
                    src = bass.AP(s0.tensor, s0.offset, [list(s0.ap[0]), [1, L2], [P, NG], [CMP_STRIDE // 2, N_CMP]])
                    p0 = posT[:, (2 * l + v) * L2:(2 * l + v) * L2 + 1]
                    pv = bass.AP(p0.tensor, p0.offset, [list(p0.ap[0]), [1, L2], [0, NG], [0, N_CMP]])
                    dve.tensor_tensor(blk[:, v, :].rearrange("p (m g n) -> p m g n", m=L2, g=NG), src, pv, ALU.add)\
                       .then_inc(S["blk_ready"], 1)
                dve.wait_ge(S["gs_exp"], L)
                link(dve.tensor_scalar(gsig, gsig, 1.0, None, ALU.add))
                link(dve.reciprocal(gsig, gsig))
                dve.wait_ge(S["cmph_done"], L)
                link(dve.tensor_copy(hc, bank[2][:, 0:60]))
                link(dve.tensor_tensor(hc2, hc, hc, ALU.mult))
                link(dve.tensor_scalar(hc2, hc2, 0.044715, 1.0, ALU.mult, ALU.add))
                dve.tensor_tensor(hc2, hc2, hc, ALU.mult).then_inc(S["gelu_c_in"], 1)
                dve.wait_ge(S["gelu_c_th"], L)
                link(dve.tensor_scalar(hct, hct, 1.0, 0.5, ALU.add, ALU.mult))
                dve.tensor_tensor(hc, hc, hct, ALU.mult).then_inc(S["gelu_c_ready"], 1)
                dve.wait_ge(S["kc_done2"], L)
                nb = NG * N_CMP
                link(dve.tensor_copy(kcn[:, 0:HD], bank[2][0:nb, 64:128]))
                dve.tensor_copy(vcs, bank[2][0:N_CMP, 128:256]).then_inc(S["vc_ready"], 1)
                link(dve.tensor_tensor(kcsq, kcn[:, 0:HD], kcn[:, 0:HD], ALU.mult))
                dve.tensor_reduce(kcs, kcsq, AX, ALU.add).then_inc(S["kcn_in"], 1)
                dve.wait_ge(S["pre_sig"], L)
                link(dve.reciprocal(rr, rr))
                dve.reciprocal(ii, ii).then_inc(S["sig_ready"], 1)
                dve.wait_ge(S["kcn_root"], L)
                link(dve.reciprocal(kcs, kcs))
                link(dve.tensor_scalar(kcn[:, HD:P], kcn[:, 0:HD], kcs, None, ALU.mult))
                dve.tensor_copy(kcn[:, 0:HD], kcn[:, HD:P]).then_inc(S["kcn_ready"], 1)
                dve.wait_ge(S["pre_rec"], L)
                dve.reciprocal(aa, aa).then_inc(S["rec_ready"], 1)
                dve.wait_ge(S["kcT_done"], L)
                dve.tensor_scalar(kcT, bank[3][:, 0:nb], par[:, R_KG + l:R_KG + l + 1], None, ALU.mult).then_inc(S["kcT_ready"], 1)
                if l == 0:
                    dve.wait_ge(S["bias_ready"], 4)
                dve.wait_ge(S["cs_done"], L)
                link(dve.memset(cS, NEG))
                for t in range(NT):
                    n = CMP_SEEN[t]
                    first = CMP_BLOCK - 1 + P * (1 - t)
                    for g in range(NG):
                        c = t * HPG * 16
                        link(dve.scalar_tensor_tensor(
                            cS[:, t, g * HPG:(g + 1) * HPG, 0:n],
                            bank[g][:, c:c + HPG * 16].rearrange("p (h n) -> p h n", h=HPG)[:, :, 0:n], HD ** -0.5,
                            biasU[:, g * HPG:(g + 1) * HPG, first:first + CMP_STRIDE * (n - 1) + 1:CMP_STRIDE], ALU.mult, ALU.add))
                cSf = cS.rearrange("p t h n -> p (t h) n")
                link(dve.tensor_reduce(cmx, cSf, AX, ALU.max))
                link(dve.tensor_scalar(cmx, cmx, NEG / 10, None, ALU.max))
                dve.tensor_tensor(cSf, cSf, cmx.rearrange("p (a b) -> p a b", b=1).to_broadcast([P, NT * NH, 16]),
                                  ALU.subtract).then_inc(S["cs_in"], 1)
                dve.wait_ge(S["cs_exp"], L)
                link(dve.tensor_reduce(cden, cSf, AX, ALU.add))
                link(dve.tensor_scalar(cden, cden, 1e-30, None, ALU.max))
                link(dve.reciprocal(cden, cden))
                link(dve.tensor_tensor(cden.rearrange("p (t h) -> p t h", t=NT), cden.rearrange("p (t h) -> p t h", t=NT),
                                       gsig[:, :, 0:NH], ALU.mult))
                dve.tensor_tensor(cSf, cSf, cden.rearrange("p (a b) -> p a b", b=1).to_broadcast([P, NT * NH, 16]),
                                  ALU.mult).then_inc(S["cp_ready"], 1)
                dve.wait_ge(S["sqrt_t"], L)
                dve.wait_ge(S["mult_ready"], L)
                for m in range(NC_LRU):
                    last = dve.tensor_tensor_scan(tt[:, m, :], aa[:, m, :], ii[:, m, :], 0.0, ALU.mult, ALU.add)
                    if m < NC_LRU - 1:
                        link(last)
                last.then_inc(S["scan_ready"], 1)

                def scores(i):
                    t, h = i // NH, i % NH
                    W = P * (t + 1)
                    n = NT * NH * l + i
                    dve.wait_ge(S["s_done"], n + 1)
                    if i >= 2:
                        dve.wait_ge(S["e_ready"], n - 1)
                    s = sS[:, i % 2, 0:2 * W].rearrange("p (b k) -> p b k", b=2)
                    first = P * (1 - t)
                    link(dve.scalar_tensor_tensor(s, bank[6 + i % 2][:, 0:2 * W].rearrange("p (b k) -> p b k", b=2), HD ** -0.5,
                                                  biasU[:, h:h + 1, first:first + W].to_broadcast([P, 2, W]), ALU.mult, ALU.add))
                    m = mx[:, 16 * (i % 2):16 * (i % 2) + 2]
                    link(dve.tensor_reduce(m, s, AX, ALU.max))
                    dve.tensor_scalar(m, m, -1.0, None, ALU.mult).then_inc(S["s_ready"], 1)

                def weigh(i):
                    t, h = i // NH, i % NH
                    W = P * (t + 1)
                    dve.wait_ge(S["e_ready"], NT * NH * l + i + 1)
                    d = den[:, 16 * (i % 2):16 * (i % 2) + 2]
                    link(dve.reciprocal(d, d))
                    link(dve.tensor_tensor(d, d, gsig[:, t, NH + h:NH + h + NH + 1:NH], ALU.mult))
                    for b in range(2):
                        last = dve.tensor_scalar(sP[:, i % 2, b * W:(b + 1) * W], sP[:, i % 2, b * W:(b + 1) * W], d[:, b:b + 1],
                                                 None, ALU.mult)
                        if b == 0:
                            link(last)
                    last.then_inc(S["p_ready"], 1)

                for i in range(NT * NH + 1):
                    if i < NT * NH:
                        scores(i)
                    if i >= 1:
                        weigh(i - 1)
                dve.wait_ge(S["mroot"], L)
                link(dve.reciprocal(nrm[:, 4:8], nrm[:, 4:8]))
                for part in range(2):
                    for t in range(NT):
                        for c in range(2):
                            dve.wait_ge(S["out_done"], 8 * l + 4 * part + 2 * t + c + 1)
                            xo = xs[:, t, c * 512:(c + 1) * 512]
                            r = nrm[:, 6 + t:7 + t] if part == 0 else nrm[:, 4 + t:5 + t]
                            last = dve.scalar_tensor_tensor(xo, bank[4 * part + 2 * t + c][:, :], r, xo, ALU.mult, ALU.add)
                            if (part, t, c) != (1, 1, 1):
                                link(last)
                last.then_inc(S["x_mixed"], 1)
                dve.wait_ge(S["x_mixed"], L)
                norm(2 * l + 1, R_G2 + 8 * l)

                def hidden(s, n, q, tile):
                    dve.wait_ge(S["silu_ready"], n)
                    dve.tensor_tensor(hid[:, tile, q * FN:(q + 1) * FN], sil[:, s % 2, :], bank[1 + 2 * (s % 2)][:, 0:FN],
                                      ALU.mult).then_inc(S["hid_ready"], 1)

                if l == 0:
                    for s in range(NT * FCH + 2):
                        if s < NT * FCH:
                            if s // NT >= HALF:
                                dve.wait_ge(S["hidT_done"], s - NT * (HALF - 1) + 1)
                            hidden(s, s + 1, (s // NT) % HALF, s % NT)
                        if s >= 2:
                            k = s - 2
                            a, b = done_tiles(k // NT), done_tiles(k // NT + 1)
                            dve.wait_ge(S["hidT_done"], k + 1)
                            dve.tensor_copy(hidT[:, k % NT, a:b, :],
                                            bank[4 + k % 2][:, 0:(b - a) * P].rearrange("p (a b) -> p a b", b=P))\
                               .then_inc(S["hidT_ready"], 1)
                    for t in range(NT):
                        dve.wait_ge(S["y_done"], t + 1)
                        for c in range(2):
                            xo = xs[:, t, c * 512:(c + 1) * 512]
                            last = dve.tensor_tensor(xo, xo, bank[(6, 2)[t] + c][:, :], ALU.add)
                            if (t, c) != (1, 1):
                                link(last)
                    last.then_inc(S["ffn_done"], 1)
                    dve.wait_ge(S["ffn_done"], 1)
                    continue
                dve.wait_ge(S["log_done"], 1)
                link(dve.tensor_copy(logit, bank[4][:, 0:16].rearrange("p (a b) -> p a b", a=NT)))
                for t in range(NT):
                    link(dve.max(top8[:, t, :], logit[:, t, :]))
                    link(dve.max_index(idx8[:, t, :], top8[:, t, :], logit[:, t, :]))
                link(dve.tensor_copy(idxf, idx8[:, :, :]))
                dve.tensor_tensor(wt[:, 0:2], top8[:, :, 1], top8[:, :, 0], ALU.subtract).then_inc(S["texp_in"], 1)
                dve.wait_ge(S["texp"], 1)
                link(dve.tensor_scalar(wt[:, 2:4], wt[:, 0:2], 1.0, None, ALU.add))
                link(dve.reciprocal(wt[:, 2:4], wt[:, 2:4]))
                link(dve.tensor_tensor(wt[:, 4:6], wt[:, 0:2], wt[:, 2:4], ALU.mult))
                eid = slot_id[:, 0:NE]
                for t in range(NT):
                    link(dve.tensor_scalar(oh1[:, t, :], eid, idxf[:, t, 0:1], None, ALU.is_equal))
                    link(dve.tensor_scalar(oh2[:, t, :], eid, idxf[:, t, 1:2], None, ALU.is_equal))
                    link(dve.tensor_scalar(wexp[:, t, :], oh1[:, t, :], wt[:, 2 + t:3 + t], None, ALU.mult))
                    link(dve.scalar_tensor_tensor(wexp[:, t, :], oh2[:, t, :], wt[:, 4 + t:5 + t], wexp[:, t, :], ALU.mult, ALU.add))
                dve.tensor_tensor(memb, oh1, oh2, ALU.add).then_inc(S["pos_in"], 1)
                dve.wait_ge(S["pos_in"], 1)
                dve.wait_ge(S["pos_done"], 1)
                link(dve.tensor_copy(pos, bank[4][:, 32:48].rearrange("p (a b) -> p a b", a=NT)))
                link(dve.tensor_scalar(over, bank[4][:, 48:56], float(P), None, ALU.is_gt))
                link(dve.tensor_tensor_scan(rank, ones[:, 0:NE], over, 0.0, ALU.mult, ALU.add))
                link(dve.tensor_scalar(jobf[:, 0:1], rank[:, NE - 1:NE], float(NE), None, ALU.add))
                link(dve.tensor_copy(jobf[:, 1:NE + 1], eid))
                for t in range(NT):
                    link(dve.tensor_copy(table[:, 0:NE, t], memb[:, t, :]))
                    link(dve.tensor_copy(table[:, 0:NE, 2 + t], pos[:, t, :]))
                    link(dve.tensor_copy(table[:, 0:NE, 4 + t], wexp[:, t, :]))
                for o in range(OVER):
                    link(dve.scalar_tensor_tensor(pick, rank, float(o + 1), over, ALU.is_equal, ALU.mult))
                    link(dve.tensor_tensor_reduce(junk[:, 0, :], pick, eid, 1.0, 0.0, ALU.mult, ALU.add,
                                                  jobf[:, NE + 1 + o:NE + 2 + o]))
                    for t in range(NT):
                        link(dve.tensor_tensor_reduce(junk[:, 0, :], pick, memb[:, t, :], 1.0, 0.0, ALU.mult, ALU.add,
                                                      table[:, NE + o, t:t + 1]))
                        link(dve.tensor_tensor_reduce(junk[:, 0, :], pick, pos[:, t, :], 1.0, -float(P), ALU.mult, ALU.add,
                                                      table[:, NE + o, 2 + t:3 + t]))
                        link(dve.tensor_tensor_reduce(junk[:, 0, :], pick, wexp[:, t, :], 1.0, 0.0, ALU.mult, ALU.add,
                                                      table[:, NE + o, 4 + t:5 + t]))
                dve.tensor_copy(jobi[:, 0:JOBS + 1], jobf).then_inc(S["jobs_ready"], 1)
                dve.wait_ge(S["jobs_ready"], 1)
                njobs = dve.value_load(jobi[0:1, 0:1], min_val=NE, max_val=JOBS)
                with dve.Fori(0, njobs) as j:
                    dve.tensor_copy(job, table[:, bass.ds(j, 1), :].rearrange("p a c -> p (a c)")).then_inc(S["job_ready"], 1)
                    dve.wait_ge(S["job_ready"], j + 1)
                    for t in range(NT):
                        dve.tensor_scalar(selM[:, t, :], slot_id[:, :], job[:, 2 + t:3 + t], job[:, t:t + 1], ALU.is_equal, ALU.mult)\
                           .then_inc(S["sel_ready"], 1)
                    for t in range(NT):
                        dve.tensor_scalar(selW[:, t, :], slot_id[:, :], job[:, 2 + t:3 + t], job[:, 4 + t:5 + t], ALU.is_equal, ALU.mult)\
                           .then_inc(S["sel_ready"], 1)
                    dve.wait_ge(S["selT_done"], j + 1)
                    dve.tensor_copy(selT, bank[6][:, 0:NT * P].rearrange("p (a b) -> p a b", a=NT)).then_inc(S["selT_ready"], 1)
                    for s in range(FCH + 1):
                        if s < FCH:
                            if s >= HALF:
                                dve.wait_ge(S["hidT_done"], j * FCH + (NT * FCH + s - HALF + 2))
                            hidden(s, j * FCH + (NT * FCH + s + 1), s % HALF, 0)
                        if s >= 1:
                            k = s - 1
                            a, b = done_tiles(k), done_tiles(k + 1)
                            dve.wait_ge(S["hidT_done"], j * FCH + (NT * FCH + k + 1))
                            dve.tensor_copy(hidT[:, 0, a:b, :],
                                            bank[4 + k % 2][:, 0:(b - a) * P].rearrange("p (a b) -> p a b", b=P))\
                               .then_inc(S["hidT_ready"], 1)
                    dve.wait_ge(S["y_done"], j + 3)
                    for c in range(2):
                        dve.tensor_copy(ye[:, c * 512:(c + 1) * 512], bank[6 + c][:, :]).then_inc(S["y_ready"], 1)
                    for q in range(4):
                        t, c = q // 2, q % 2
                        dve.wait_ge(S["comb_done"], 4 * j + (q + 1))
                        xo = xs[:, t, c * 512:(c + 1) * 512]
                        dve.tensor_tensor(xo, xo, bank[(4, 5, 6, 7)[q]][:, :], ALU.add).then_inc(S["comb_ready"], 1)
                    dve.wait_ge(S["comb_ready"], 4 * j + 4)

        @block.tensor
        def _(pe):
            mm = pe.matmul

            def norm_turn(n):
                for k in range(KD):
                    for t in range(NT):
                        pe.wait_ge(S["norm_ready"], 2 * n + t + 1)
                        last = pe.transpose(bank[k // 2][:, (k % 2) * SEQ + t * P:(k % 2) * SEQ + (t + 1) * P],
                                            xn[:, t, k * P:(k + 1) * P], ident[:, :])
                    if k % 2 == 1:
                        last.then_inc(S["normT_done"], 1)

            pe.wait_ge(S["consts_set"], 1)
            pe.wait_ge(S["small_loaded"], 16 * 16)
            pe.transpose(bank[0][:, 0:N_ROWS], prow[:, :], ident[0:N_ROWS, 0:N_ROWS])
            pe.transpose(bank[0][:, 128:128 + HD], posr[:, :], ident[0:HD, 0:HD]).then_inc(S["params_transposed"], 1)
            pe.wait_ge(S["relb_loaded"], 32)
            mm(bank[1][0:NH, 0:U_LEN], relb[:, :], bucketT[:, :], start=True, stop=True).then_inc(S["urow_done"], 1)
            pe.wait_ge(S["params_ready"], 2)
            pe.wait_ge(S["urow_ready"], 1)

            for l in range(DEPTH):
                L = l + 1
                p0 = l * (MIX_PIECES + FFN_PIECES)
                norm_turn(2 * l)
                if l == 0:
                    pe.wait_ge(S["skew_loaded"], 16)
                    for c in range(4):
                        mm(bank[4 + c][:, :], flip[:, :], skew[:, c * 512:(c + 1) * 512], start=True, stop=True)\
                            .then_inc(S["flip_done"], 1)
                    pe.wait_ge(S["bias_ready"], 4)
                pe.wait_ge(S["hT_act"], 8 * l + 4)
                pe.wait_ge(S["hT_dve"], 8 * l + 4)

                def project(b, c0, w, lo, n, t):
                    for k in range(KD):
                        last = mm(bank[b + t][:, c0:c0 + n], hT[:, k, t * P:(t + 1) * P], w[:, k, lo:lo + n],
                                  start=(k == 0), stop=(k == KD - 1))
                    return last

                wait_piece(pe, p0)
                wA, wB = ring3(p0, KD, 768), ring3(p0 + 1, KD, W_B)
                for t in range(NT):
                    project(4, 0, wA, 0, 512, t).then_inc(S["q_done"], 1)
                project(6, 0, wA, 512, 256, 0)
                project(6, 0, wA, 512, 256, 1).then_inc(S["kc_done"], 1)
                wait_piece(pe, p0 + 1)
                for t in range(NT):
                    project(0, 0, wB, 0, 512, t).then_inc(S["kv_done"], 1)
                for t in range(NT):
                    project(6, 256, wB, 512, 24, t).then_inc(S["gates_done"], 1)
                for w in range(2):
                    wait_piece(pe, p0 + 2 + w)
                    if w == 1:
                        pe.wait_ge(S["tok_act"], 4 * l + 1)
                        pe.wait_ge(S["tok_dve"], 4 * l + 1)
                    wL = ring3(p0 + 2 + w, KD, 512)
                    for m in range(NC_LRU):
                        for k in range(KD):
                            last = mm(bank[2 + 2 * w + m // 2][:, (m % 2) * SEQ:(m % 2 + 1) * SEQ], wL[:, k, m * P:(m + 1) * P],
                                      hT[:, k, :], start=(k == 0), stop=(k == KD - 1))
                        if m == 1 or (m == 3):
                            last.then_inc(S["lrux_done" if w == 0 else "lrug_done"], 1)
                pe.wait_ge(S["tok_act"], 4 * L)
                pe.wait_ge(S["tok_dve"], 4 * L)
                pe.wait_ge(S["qk_ready"], L)
                for hh in range(HPG):
                    for t in range(NT):
                        last = pe.transpose(bank[6 + hh // 2][:, (hh % 2) * SEQ + t * P:(hh % 2) * SEQ + (t + 1) * P],
                                            qn[:, t, hh, :], ident[:, :])
                    if hh % 2 == 1:
                        last.then_inc(S["T_done"], 1)
                for b in range(2):
                    for t in range(NT):
                        last = pe.transpose(bank[0][:, b * SEQ + t * P:b * SEQ + (t + 1) * P], kn[:, t, b, :], ident[:, :])
                last.then_inc(S["T_done"], 1)
                for v in range(2):
                    for t in range(NT):
                        last = pe.transpose(bank[1][:, v * SEQ + t * P:v * SEQ + (t + 1) * P],
                                            tok[:, t, 512 + v * P:512 + (v + 1) * P], ident[:, :])
                last.then_inc(S["T_done"], 1)
                wait_piece(pe, p0 + 4)
                w1 = ring3(p0 + 4, 2 * L2, P)
                pe.wait_ge(S["lrux_ready"], 4 * L)
                nb = NG * N_CMP
                for v in range(2):
                    pe.wait_ge(S["blk_ready"], 2 * l + v + 1)
                    for m in range(L2):
                        last = mm(bank[2][:, v * nb:(v + 1) * nb], w1[:, v * L2 + m, :], blk[:, v, m * nb:(m + 1) * nb],
                                  start=(m == 0), stop=(m == L2 - 1))
                last.then_inc(S["cmph_done"], 1)
                pe.wait_ge(S["gate_ready"], L)
                pe.wait_ge(S["lru_w_loaded"], 16 * 4 * L)
                pe.wait_ge(S["conv_ready"], 4 * L)
                for w in range(2):
                    if w == 1:
                        pe.wait_ge(S["kT_ready"], L)
                        pe.wait_ge(S["kcv_ready"], L)
                    for m in range(NC_LRU):
                        last = mm(bank[(4, 0)[w] + m // 2][:, (m % 2) * SEQ:(m % 2 + 1) * SEQ], lruW[:, w, m, :], xc[:, m, :],
                                  start=True, stop=True)
                    last.then_inc(S[("rgate_done", "igate_done")[w]], 1)
                pe.wait_ge(S["gelu_c_ready"], L)
                mm(bank[2][0:nb, 64:128], hc[:, 0:nb], w2[:, l, 0, :], start=True, stop=True)
                for g in range(NG):
                    last = mm(bank[2][0:N_CMP, 128 + g * HD:128 + (g + 1) * HD], hc[:, nb + g * N_CMP:nb + (g + 1) * N_CMP],
                              w2[:, l, 1, :], start=True, stop=True)
                last.then_inc(S["kc_done2"], 1)
                pe.wait_ge(S["kcn_ready"], L)
                pe.transpose(bank[3][:, 0:nb], kcn, ident[0:nb, 0:nb]).then_inc(S["kcT_done"], 1)
                pe.wait_ge(S["qT_ready"], 2 * L)
                pe.wait_ge(S["kcT_ready"], L)
                pe.wait_ge(S["exp_i"], L)
                for t in range(NT):
                    for h in range(NH):
                        g, hh = h // HPG, h % HPG
                        c = (t * HPG + hh) * 16
                        last = mm(bank[g][:, c:c + N_CMP], qT[g * HD:(g + 1) * HD, hh, t * P:(t + 1) * P],
                                  kcT[g * HD:(g + 1) * HD, g * N_CMP:(g + 1) * N_CMP], start=True, stop=True)
                last.then_inc(S["cs_done"], 1)

                def score(i):
                    t, h = i // NH, i % NH
                    g, hh = h // HPG, h % HPG
                    W = P * (t + 1)
                    if i >= 2:
                        pe.wait_ge(S["s_ready"], NT * NH * l + i - 1)
                    for b in range(2):
                        last = mm(bank[6 + i % 2][:, b * W:(b + 1) * W], qT[g * HD:(g + 1) * HD, hh, t * P:(t + 1) * P],
                                  kT[g * HD:(g + 1) * HD, b, 0:W], start=True, stop=True)
                    last.then_inc(S["s_done"], 1)

                def turn(i):
                    W = P * (i // NH + 1)
                    n = NT * NH * l + i
                    pe.wait_ge(S["p_ready"], n + 1)
                    if i >= 2:
                        pe.wait_ge(S["pT_ready"], n - 1)
                    for b in range(2 * W // P):
                        last = pe.transpose(bank[2 + i % 2][:, b * P:(b + 1) * P], sP[:, i % 2, b * P:(b + 1) * P], ident[:, :])
                    last.then_inc(S["pT_done"], 1)

                def values(i):
                    t, h = i // NH, i % NH
                    g = h // HPG
                    n = NT * NH * l + i
                    pe.wait_ge(S["pT_ready"], n + 1)
                    o = bank[4 + t][:, h * HD:(h + 1) * HD]
                    mm(o, cPT[:, i, :], vcs[:, g * HD:(g + 1) * HD], start=True, stop=False)
                    for b in range(2):
                        for k in range(t + 1):
                            v = tok[:, k, 896 + 256 * b + g * HD:896 + 256 * b + (g + 1) * HD]
                            last = mm(o, sT[:, i % 2, (b * (t + 1) + k) * P:(b * (t + 1) + k + 1) * P], v,
                                      start=False, stop=(b == 1 and k == t))
                    last.then_inc(S["o_done"], 1)

                pe.wait_ge(S["kT_ready"], L)
                score(0)
                pe.wait_ge(S["cp_ready"], L)
                for c in range(4):
                    if c >= 2:
                        pe.wait_ge(S["cpT_ready"], 4 * l + c - 1)
                    for a in range(4):
                        i = 4 * c + a
                        last = pe.transpose(bank[c % 2][0:N_CMP, a * P:(a + 1) * P], cS[:, i // NH, i % NH, 0:N_CMP], ident[:, :])
                    last.then_inc(S["cpT_done"], 1)
                pe.wait_ge(S["cpT_ready"], 4 * L)
                pe.wait_ge(S["vc_ready"], L)
                pe.wait_ge(S["exp_r"], L)
                for i in range(1, NT * NH + 2):
                    if i < NT * NH:
                        score(i)
                    if i <= NT * NH:
                        turn(i - 1)
                    if i >= 2:
                        values(i - 2)
                pe.wait_ge(S["ysq_ready"], L)
                for t in range(NT):
                    for m in range(NC_LRU):
                        last = mm(bank[1][:, t:t + 1], tt[:, m, t * P:(t + 1) * P], ones[:, 0:1], start=(m == 0), stop=(m == NC_LRU - 1))
                last.then_inc(S["lsum_done"], 1)
                pe.wait_ge(S["s_ready"], NT * NH * L)
                pe.wait_ge(S["o_ready"], NT * L)
                for m in range(4):
                    for t in range(NT):
                        last = pe.transpose(bank[6 + m // 2][:, (m % 2) * SEQ + t * P:(m % 2) * SEQ + (t + 1) * P],
                                            oS[:, t, m * P:(m + 1) * P], ident[:, :])
                    if m % 2 == 1:
                        last.then_inc(S["oT_done"], 1)
                for part in range(2):
                    wait_piece(pe, p0 + 5 + part)
                    if part == 0:
                        pe.wait_ge(S["ymix_ready"], 4 * L)
                        pe.wait_ge(S["mroot_in"], L)
                        pe.wait_ge(S["pT_ready"], NT * NH * L)
                    else:
                        pe.wait_ge(S["oT_ready"], 4 * L)
                    wo = ring3(p0 + 5 + part, 4, D)
                    for t in range(NT):
                        for c in range(2):
                            for m in range(4):
                                last = mm(bank[4 * part + 2 * t + c][:, :], mixT[:, 4 * part + m, t * P:(t + 1) * P],
                                          wo[:, m, c * 512:(c + 1) * 512], start=(m == 0), stop=(m == 3))
                            last.then_inc(S["out_done"], 1)
                norm_turn(2 * l + 1)
                pe.wait_ge(S["hT_act"], 8 * l + 8)
                pe.wait_ge(S["hT_dve"], 8 * l + 8)

                def gate_up(p, q, lhs, s, last_tile):
                    lo = (q % 2) * FN
                    for w in range(2):
                        wr = ring3(p + 2 * (q // 2) + w, KD, FCOLS)
                        for k in range(KD):
                            last = mm(bank[2 * (s % 2) + w][:, 0:FN], lhs(k), wr[:, k, lo:lo + FN],
                                      start=(k == 0), stop=(k == KD - 1))
                        if w == 0 and last_tile and q % 2 == 1:
                            last.then_inc(S["gate_used"], 1)
                    last.then_inc(S["gu_done"], 1)

                def turn_hidden(q, tile, b):
                    a, z = done_tiles(q), done_tiles(q + 1)
                    for i in range(a, z):
                        lo = i * P % (HALF * FN)
                        last = pe.transpose(bank[b][:, (i - a) * P:(i - a + 1) * P], hid[:, tile, lo:lo + P], ident[:, :])
                    last.then_inc(S["hidT_done"], 1)

                if l == 0:
                    p = p0 + MIX_PIECES
                    for s in range(NT * FCH + NT):
                        q, t = s // NT, s % NT
                        if s < NT * FCH:
                            if q % 2 == 0 and t == 0:
                                wait_piece(pe, p + q)
                                wait_piece(pe, p + q + 1)
                            if s >= 2:
                                pe.wait_ge(S["hid_ready"], s - 1)
                            gate_up(p, q, lambda k: hT[:, k, t * P:(t + 1) * P], s, t == NT - 1)
                        if s >= NT:
                            k = s - NT
                            pe.wait_ge(S["hid_ready"], k + 1)
                            if k >= 2:
                                pe.wait_ge(S["hidT_ready"], k - 1)
                            turn_hidden(k // NT, k % NT, 4 + k % 2)
                    pe.wait_ge(S["hidT_ready"], NT * FCH)
                    for t in range(NT):
                        i = 0
                        for c, n in enumerate(DOWN):
                            wait_piece(pe, p + 8 + c)
                            wd = ring3(p + 8 + c, n, D)
                            for r in range(n):
                                for o in range(2):
                                    last = mm(bank[(6, 2)[t] + o][:, :], hidT[:, t, i, :], wd[:, r, o * 512:(o + 1) * 512],
                                              start=(i == 0), stop=(i == FT - 1), skip_group_check=True)
                                i += 1
                            if t == NT - 1 and c < len(DOWN) - 1:
                                last.then_inc(S["down_used"], 1)
                        last.then_inc(S["y_done"], 1)
                    continue
                for t in range(NT):
                    for k in range(KD):
                        last = mm(bank[4][:, t * NE:(t + 1) * NE], hT[:, k, t * P:(t + 1) * P], rw[:, k, :], start=(k == 0), stop=(k == KD - 1))
                last.then_inc(S["log_done"], 1)
                pe.wait_ge(S["pos_in"], 1)
                mm(bank[4][:, 32:40], before[:, :], memb[:, 0, :], start=True, stop=True)
                mm(bank[4][:, 40:48], ones[:, :], memb[:, 0, :], start=True, stop=False)
                mm(bank[4][:, 40:48], before[:, :], memb[:, 1, :], start=False, stop=True)
                mm(bank[4][:, 48:56], ones[:, :], memb[:, 0, :], start=True, stop=False)
                mm(bank[4][:, 48:56], ones[:, :], memb[:, 1, :], start=False, stop=True).then_inc(S["pos_done"], 1)
                pe.wait_ge(S["jobs_ready"], 1)
                njobs = pe.value_load(jobi[0:1, 0:1], min_val=NE, max_val=JOBS)
                p = ROUTED0
                with pe.Fori(0, njobs) as j:
                    def wait_job_piece(i):
                        n = (p + i) // SLOTS + 1
                        pe.wait_ge(loaded[(p + i) % SLOTS], j * (16 * FFN_PIECES // SLOTS) + 16 * n)

                    pe.wait_ge(S["sel_ready"], 4 * j + 2)
                    for c in range(2):
                        for k in range(4 * c, 4 * c + 4):
                            for t in range(NT):
                                last = mm(bank[4 + c][:, (k % 4) * P:(k % 4 + 1) * P], xn[:, t, k * P:(k + 1) * P], selM[:, t, :],
                                          start=(t == 0), stop=(t == NT - 1))
                        last.then_inc(S["xg_done"], 1)
                    pe.wait_ge(S["sel_ready"], 4 * j + 4)
                    for t in range(NT):
                        last = pe.transpose(bank[6][:, t * P:(t + 1) * P], selW[:, t, :], ident[:, :])
                    last.then_inc(S["selT_done"], 1)
                    pe.wait_ge(S["xg_ready"], 8 * j + 8)
                    for q in range(FCH + 1):
                        if q < FCH:
                            if q % 2 == 0:
                                wait_job_piece(q)
                                wait_job_piece(q + 1)
                            pe.wait_ge(S["hid_ready"], j * FCH + (NT * FCH + q - 1))
                            gate_up(p, q, lambda k: xg[:, k, :], q, True)
                        if q >= 1:
                            k = q - 1
                            pe.wait_ge(S["hid_ready"], j * FCH + (NT * FCH + k + 1))
                            if k >= 2:
                                pe.wait_ge(S["hidT_ready"], j * FCH + (NT * FCH + k - 1))
                            turn_hidden(k, 0, 4 + k % 2)
                    pe.wait_ge(S["selT_ready"], j + 1)
                    i = 0
                    for c, n in enumerate(DOWN):
                        wait_job_piece(8 + c)
                        wd = ring3(p + 8 + c, n, D)
                        for r in range(n):
                            for s in range(1, FCH + 1):
                                if done_tiles(s - 1) == i:
                                    pe.wait_ge(S["hidT_ready"], j * FCH + (NT * FCH + s))
                            for o in range(2):
                                last = mm(bank[6 + o][:, :], hidT[:, 0, i, :], wd[:, r, o * 512:(o + 1) * 512],
                                          start=(i == 0), stop=(i == FT - 1), skip_group_check=True)
                            i += 1
                        if c < len(DOWN) - 1:
                            last.then_inc(S["down_used"], 1)
                    last.then_inc(S["y_done"], 1)
                    pe.wait_ge(S["y_ready"], 2 * j + 2)
                    for o in range(4):
                        t, c = o // 2, o % 2
                        mm(bank[4 + o][:, :], selT[:, t, :], ye[:, c * 512:(c + 1) * 512], start=True, stop=True)\
                            .then_inc(S["comb_done"], 1)
                    pe.wait_ge(S["comb_ready"], 4 * j + 4)


_INS = ['x', 'rel_bias', 'norm1_g', 'w_in', 'conv_w', 'conv_b', 'lru_wa', 'lru_ba', 'lru_wx', 'lru_bx', 'lru_lambda',
        'q_norm_g', 'k_norm_g', 'cmp_pos', 'cmp_w1', 'cmp_w2', 'gate_b', 'out_norm_g', 'w_out', 'norm2_g',
        'ffn_w_gate', 'ffn_w_up', 'ffn_w_down', 'router_w', 'moe_w_gate', 'moe_w_up', 'moe_w_down']


def bucket_constant():
    import math
    import numpy as np
    rows = np.zeros((N_BUCKETS + 1, U_LEN), np.float32)
    exact, far = N_BUCKETS // 2, 128
    for j in range(U_LEN):
        dist = 2 * P - 1 - j
        if dist < 0:
            b = N_BUCKETS
        elif dist < exact:
            b = dist
        else:
            b = min(exact + int(np.float32(math.log(dist / exact)) / np.float32(math.log(far / exact)) * (N_BUCKETS - exact)),
                    N_BUCKETS - 1)
        rows[b, j] = 1.0
    return rows


def kernel(**inputs):
    import numpy as _np
    import concourse.bacc as _bacc
    from concourse import mybir as _mybir
    from concourse.bass_utils import run_bass_kernel_spmd as _run

    nc = _bacc.Bacc("TRN2", target_bir_lowering=False, num_devices=1)
    arrays, args = {}, []
    for name in _INS:
        a = _np.ascontiguousarray(inputs[name])
        arrays[f"in_{name}_dram"] = a
        args.append(nc.dram_tensor(f"in_{name}_dram", a.shape, _mybir.dt.from_np(a.dtype), kind="ExternalInput").ap())
    rows = bucket_constant()
    arrays["bucket_rows_dram"] = rows
    args.append(nc.dram_tensor("bucket_rows_dram", rows.shape, F32, kind="ExternalInput").ap())
    args.append(nc.dram_tensor("out_0_dram", (1, SEQ, D), F32, kind="ExternalOutput").ap())
    build(nc, *args)
    r = _run(nc, [arrays], core_ids=[0])
    return r.results[0]["out_0_dram"]
```

```python
from contextlib import ExitStack

import concourse.bass as bass
from concourse import mybir

F32 = mybir.dt.float32
F32R = mybir.dt.float32r
I32 = mybir.dt.int32
U32 = mybir.dt.uint32
ALU = mybir.AluOpType
ACT = mybir.ActivationFunctionType
AX = mybir.AxisListType.X

P = 128
D = 1024
SEQ = 256
NT = SEQ // P
KD = D // P
DEPTH = 2
D_LRU = 512
NC_LRU = D_LRU // P
HD = 64
NH = 8
NG = 2
HPG = NH // NG
CONV = 4
CMP_BLOCK, CMP_STRIDE = 32, 16
N_CMP = (SEQ - CMP_BLOCK) // CMP_STRIDE + 1
CMP_SEEN = (P // CMP_STRIDE - CMP_BLOCK // CMP_STRIDE + 1, N_CMP)
L2 = CMP_BLOCK // 2
N_BUCKETS = 32
D_FF = 2816
NE = 8
D_IN = 2 * D_LRU + NH * HD + 6 * NG * HD + 3 * NH
OFF_Q = 2 * D_LRU
OFF_KV = OFF_Q + NH * HD
W_B = D_IN - OFF_KV - 2 * P
EPS = 1e-6
NEG = -1e30
U_LEN = 3 * P

SLOTS = 3
SLOT = 6 * D
FCOLS = D_FF // 4
FN = FCOLS // 2
FCH = D_FF // FN
FT = D_FF // P
DOWN = (6, 6, 6, 4)
HALF = FCH // 2
MIX_PIECES = 7
FFN_PIECES = 8 + len(DOWN)
ARENA = 17100
ROUTED0 = 2 * MIX_PIECES + FFN_PIECES
OVER = 3
JOBS = NE + OVER
UNIT = 4 * FN
UNITS = 4 * FCH + FT
USLOTS = 3

R_G1, R_G2, R_OG = 0, 16, 32
R_CW, R_CB, R_BA, R_BX, R_LAM = 48, 80, 88, 96, 104
R_QG, R_KG, N_ROWS = 112, 114, 116


def done_tiles(c):
    return c * FN // P


def build(nc, x, rel_bias, norm1_g, w_in, conv_w, conv_b, lru_wa, lru_ba, lru_wx, lru_bx, lru_lambda,
          q_norm_g, k_norm_g, cmp_pos, cmp_w1, cmp_w2, gate_b, out_norm_g, w_out, norm2_g,
          ffn_w_gate, ffn_w_up, ffn_w_down, router_w, moe_w_gate, moe_w_up, moe_w_down,
          bucket_rows, out):
    ctx = ExitStack()
    with ctx:
        def sb(name, shape, dt=F32):
            return ctx.enter_context(nc.sbuf_tensor(name, shape, dt))

        def sem(name):
            return ctx.enter_context(nc.semaphore(name))

        ring = sb("ring", [P, SLOTS, SLOT])
        xs = sb("xs", [P, NT, D])
        xn = sb("xn", [P, NT, D])
        hT = sb("hT", [P, KD, SEQ])
        biasU = sb("biasU", [P, NH, 2 * P])
        ident = sb("ident", [P, P])
        flip = sb("flip", [P, P])
        ones = sb("ones", [P, P])
        before = sb("before", [P, P])
        slot_id = sb("slot_id", [P, P])
        prow = sb("prow", [N_ROWS, P])
        par = sb("par", [P, N_ROWS])
        posr = sb("posr", [HD, P])
        posT = sb("posT", [P, HD])
        gateb = sb("gateb", [P, DEPTH, 3 * NH])
        bucketT = sb("bucketT", [N_BUCKETS + 1, U_LEN])
        relb = sb("relb", [N_BUCKETS + 1, NH])
        urow = sb("urow", [NH, U_LEN])
        lruW = sb("lruW", [P, 2, NC_LRU, P])
        w2 = sb("w2", [P, DEPTH, 2, HD])
        rw = sb("rw", [P, KD, NE])
        nba = sb("nba", [P, 2, DEPTH * NC_LRU])
        sp4 = sb("sp4", [P, DEPTH * NC_LRU])
        cEPS = sb("cEPS", [P, 1])
        ssq = sb("ssq", [P, NT])
        rstd = sb("rstd", [P, NT])

        idx8 = sb("idx8", [P, NT, 8], U32)
        jobi = sb("jobi", [P, JOBS + 2], I32)

        arena_scope = ExitStack()
        arena = arena_scope.enter_context(nc.sbuf_tensor("arena", [P, ARENA], F32))
        at = [0]

        def mix(n, *dims):
            v = arena[:, at[0]:at[0] + n]
            at[0] += n
            assert at[0] <= ARENA
            if len(dims) == 2:
                v = v.rearrange("p (a b) -> p a b", a=dims[0])
            if len(dims) == 3:
                v = v.rearrange("p (a b c) -> p a b c", a=dims[0], b=dims[1])
            return v

        tok = mix(NT * 1304, NT, 1304)
        qn = mix(NT * 512, NT, HPG, P)
        kn = mix(NT * 256, NT, 2, P)
        sq = mix(NT * 1280, NT, 1280)
        qT = mix(HPG * SEQ, HPG, SEQ)
        kT = mix(2 * SEQ, 2, SEQ)
        kcv2 = mix(2 * NG * P, 2, NG, P)
        blk = mix(2 * L2 * NG * N_CMP, 2, L2 * NG * N_CMP)
        xpad = mix(NC_LRU * (SEQ + 4), NC_LRU, SEQ + 4)
        gT = mix(NC_LRU * SEQ, NC_LRU, SEQ)
        xc = mix(NC_LRU * SEQ, NC_LRU, SEQ)
        rr = arena[:, NT * 1304 + NT * 768:][:, 0:NC_LRU * SEQ].rearrange("p (a b) -> p a b", a=NC_LRU)
        ii = arena[:, NT * 1304 + NT * 768 + 1024:][:, 0:NC_LRU * SEQ].rearrange("p (a b) -> p a b", a=NC_LRU)
        aa = mix(NC_LRU * SEQ, NC_LRU, SEQ)
        tt = mix(NC_LRU * SEQ, NC_LRU, SEQ)
        sS = xn[:, 0, :].rearrange("p (b c) -> p b c", b=2)
        sP = xn[:, 1, :].rearrange("p (b c) -> p b c", b=2)
        skew = arena[:, at[0] - 2 * NC_LRU * SEQ:at[0]]
        sT = mix(2 * 512, 2, 512)
        cS = mix(NT * NH * 16, NT, NH, 16)
        small = mix(896)
        oS = arena[:, 0:NT * 512].rearrange("p (a b) -> p a b", a=NT)
        mixT = hT
        rms20 = small[:, 0:40].rearrange("p (a b) -> p a b", a=NT)
        gsig = small[:, 40:88].rearrange("p (a b) -> p a b", a=NT)
        hc = small[:, 88:148]
        hc2 = small[:, 148:208]
        hct = small[:, 208:268]
        kcn = small[0:NG * N_CMP, 268:396]
        kcsq = small[0:NG * N_CMP, 396:460]
        kcs = small[0:NG * N_CMP, 460:461]
        kcT = small[:, 462:492]
        vcs = small[0:N_CMP, 492:620]
        mx = small[:, 620:652]
        den = small[:, 652:684]
        cmx = small[:, 684:700]
        cden = small[:, 700:716]
        nrm = small[:, 716:724]
        cPT = hT[0:N_CMP].rearrange("p k (a q) -> p (k a) q", a=2)

        at[0] = 0
        hid = mix(NT * HALF * FN, NT, HALF * FN)
        sil = mix(2 * FN, 2, FN)
        hidT = mix(NT * FT * P, NT, FT, P)

        arena_scope.close()
        ehid = sb("ehid", [P, HALF * FN])
        esil = sb("esil", [P, 2, FN])
        ehidTh = sb("ehidTh", [P, FT, P], F32R)
        ehidTl = sb("ehidTl", [P, FT, P], F32R)
        xgh = sb("xgh", [P, KD, P], F32R)
        xgl = sb("xgl", [P, KD, P], F32R)
        wh = sb("wh", [P, USLOTS, UNIT], F32R)
        wl = sb("wl", [P, USLOTS, UNIT], F32R)
        ye = ehid[:, 0:D]
        selM = sb("selM", [P, NT, P])
        selW = sb("selW", [P, NT, P])
        selT = sb("selT", [P, NT, P])
        rt = sb("rt", [P, 280])
        logit = rt[:, 0:16].rearrange("p (a b) -> p a b", a=NT)
        top8 = rt[:, 16:32].rearrange("p (a b) -> p a b", a=NT)
        idxf = rt[:, 32:48].rearrange("p (a b) -> p a b", a=NT)
        oh1 = rt[:, 48:64].rearrange("p (a b) -> p a b", a=NT)
        oh2 = rt[:, 64:80].rearrange("p (a b) -> p a b", a=NT)
        memb = rt[:, 80:96].rearrange("p (a b) -> p a b", a=NT)
        wexp = rt[:, 96:112].rearrange("p (a b) -> p a b", a=NT)
        pos = rt[:, 112:128].rearrange("p (a b) -> p a b", a=NT)
        wt = rt[:, 128:136]
        over = rt[:, 136:144]
        rank = rt[:, 144:152]
        pick = rt[:, 152:160]
        junk = rt[:, 160:176].rearrange("p (a b) -> p a b", a=NT)
        table = rt[:, 176:176 + 6 * (JOBS + 1)].rearrange("p (j c) -> p j c", c=6)
        job = rt[:, 250:256]
        jobf = rt[:, 256:256 + JOBS + 1]

        bank = [ctx.enter_context(nc.psum_tensor(f"bank{i}", [P, 512], F32)) for i in range(8)]

        urows_dram = nc.dram_tensor("urows", (NH, U_LEN), F32, kind="Internal").ap()

        names = """small_loaded relb_loaded rows_stored skew_loaded flip_done bias_ready lru_w_loaded gate_used down_used out_stored
            x_loaded consts_set params_transposed params_ready urow_done urow_ready
            root_done norm_ready normT_done hT_act hT_dve q_done kc_done kv_done gates_done lrux_done lrug_done
            tok_act tok_dve lrux_ready gate_ready
            qk_root_in qk_root qk_ready T_done qT_ready kT_ready kcv_ready blk_ready cmph_done hc_ready gelu_c_in gelu_c_th gelu_c_ready
            kc_done2 vc_ready kcn_in kcn_root kcn_ready kcT_done kcT_ready
            conv_ready rgate_done igate_done exp_r exp_i pre_sig sig_ready tanh_r pre_rec rec_ready sqrt_t mult_ready scan_ready
            gelu_in gelu_th gelu_ready ysq_ready ymix_ready
            gs_in gs_exp gs_ready cs_done cs_in cs_exp cp_ready cpT_done cpT_ready
            s_done s_ready e_ready p_ready pT_done pT_ready o_done o_ready oT_done oT_ready lsum_done mroot_in mroot rout_ready
            out_done x_mixed
            xg_done xg_high xg_ready wh_ready wl_ready unit_used hidT_high ye_act gu_done silu_ready hid_ready hidT_done hidT_ready y_ready comb_done comb_ready sel_ready selT_done selT_ready
            log_done job_ready texp_in texp pos_in pos_done jobs_ready ffn_done
            act_chain dve_chain pool_chain""".split()
        S = {n: sem(n) for n in names}
        loaded = [sem(f"slot{i}_loaded") for i in range(SLOTS)]

        def piece_at(p):
            return ring[:, p % SLOTS, :]

        def ring3(p, a, b):
            return piece_at(p)[:, 0:a * b].rearrange("p (a b) -> p a b", a=a)

        def wait_piece(eng, p):
            eng.wait_ge(loaded[p % SLOTS], 16 * (p // SLOTS + 1))

        def last_unit(i):
            return 8 * (i // 2) + 5 + 2 * (i % 2) if i < 8 else 4 * FCH + sum(DOWN[:i - 7]) - 1

        def first_piece(u):
            if u < 4 * FCH:
                return 2 * (u // 8) + u % 8 // 2 if u % 8 in (0, 2) else None
            starts = [4 * FCH + sum(DOWN[:c]) for c in range(len(DOWN))]
            return 8 + starts.index(u) if u in starts else None

        def unit_source(u):
            if u < 4 * FCH:
                q, w, kh = u // 4, u % 4 // 2, u % 2
                piece = ring3(ROUTED0 + 2 * (q // 2) + w, KD, FCOLS)
                return piece[:, 4 * kh:4 * kh + 4, (q % 2) * FN:(q % 2 + 1) * FN]
            i, c = u - 4 * FCH, 0
            while i >= DOWN[c]:
                i, c = i - DOWN[c], c + 1
            return ring3(ROUTED0 + 8 + c, DOWN[c], D)[:, i:i + 1, :]

        def unit_in(w, u):
            if u < 4 * FCH:
                return w[:, u % USLOTS, :].rearrange("p (k n) -> p k n", k=4)
            return w[:, u % USLOTS, 0:D].rearrange("p (k n) -> p k n", k=1)

        def wait_job_piece(eng, j, i):
            eng.wait_ge(loaded[(ROUTED0 + i) % SLOTS], j * (16 * FFN_PIECES // SLOTS) + 16 * ((ROUTED0 + i) // SLOTS + 1))

        block = ctx.enter_context(nc.Block())

        @block.sync
        def _(sp):
            sp.dma_start(xs[:, :, :], x[0].rearrange("(t p) d -> p t d", p=P)).then_inc(S["x_loaded"], 16)

            def freed(p):
                l, i = divmod(p, MIX_PIECES + FFN_PIECES)
                if i < MIX_PIECES:
                    return [("kc_done", l + 1), ("gates_done", 2 * l + 2), ("lrux_done", 2 * l + 2), ("lrug_done", 2 * l + 2),
                            ("cmph_done", l + 1), ("out_done", 8 * l + 4), ("out_done", 8 * l + 8)][i]
                i -= MIX_PIECES
                if i < 8:
                    return ("gate_used", i // 2 + 1) if i % 2 == 0 else ("gu_done", NT * (i + 1))
                return ("down_used", i - 7)

            def load(p, dst, src):
                if p >= SLOTS:
                    name, count = freed(p - SLOTS)
                    sp.wait_ge(S[name], count)
                sp.dma_start(dst, src).then_inc(loaded[p % SLOTS], 16)

            def load_mix(l, p):
                wi = w_in[l].rearrange("(k p) n -> p k n", p=P)
                load(p, ring3(p, KD, 768), wi[:, :, OFF_Q:OFF_Q + 768])
                load(p + 1, ring3(p + 1, KD, W_B), wi[:, :, OFF_Q + 768:D_IN])
                load(p + 2, ring3(p + 2, KD, 512), wi[:, :, 0:D_LRU])
                load(p + 3, ring3(p + 3, KD, 512), wi[:, :, D_LRU:2 * D_LRU])
                load(p + 4, ring3(p + 4, 2 * L2, P), cmp_w1[l].rearrange("v (m e) d c -> (e d) (v m) c", e=2))
                wo = w_out[l].rearrange("(k p) n -> p k n", p=P)
                load(p + 5, ring3(p + 5, 4, D), wo[:, 0:4, :])
                load(p + 6, ring3(p + 6, 4, D), wo[:, 4:8, :])

            def ffn_piece(p, i, wg, wu, wd):
                if i < 8:
                    w = (wg, wu)[i % 2].rearrange("(k p) n -> p k n", p=P)
                    return ring3(p + i, KD, FCOLS), w[:, :, i // 2 * FCOLS:(i // 2 + 1) * FCOLS]
                n, t = DOWN[i - 8], sum(DOWN[:i - 8])
                return ring3(p + i, n, D), wd.rearrange("(t p) n -> p t n", p=P)[:, t:t + n, :]

            load_mix(0, 0)
            for i in range(FFN_PIECES):
                load(MIX_PIECES + i, *ffn_piece(MIX_PIECES, i, ffn_w_gate[0], ffn_w_up[0], ffn_w_down[0]))
            load_mix(1, MIX_PIECES + FFN_PIECES)
            for i in range(SLOTS):
                load(ROUTED0 + i, *ffn_piece(ROUTED0, i, moe_w_gate[0, 0], moe_w_up[0, 0], moe_w_down[0, 0]))
            sp.wait_ge(S["jobs_ready"], 1)
            njobs = sp.value_load(jobi[0:1, 0:1], min_val=NE, max_val=JOBS)
            def weights_of(j):
                e = sp.value_load(jobi[0:1, bass.ds(j + 1, 1)], min_val=0, max_val=NE - 1)
                first = sp.snap(e * (D * D_FF))
                row_reg = sp.to_reg(first + D)
                row = sp.snap(row_reg, min_val=D, max_val=(NE - 1) * D * D_FF + D)
                return [bass.AP(m.tensor, o, [[n, r], [1, n]]) for m, o, r, n in
                        ((moe_w_gate, row - D, D, D_FF), (moe_w_up, row - D, D, D_FF), (moe_w_down, row - D, D_FF, D))]

            def load_job(j, i, w, k):
                sp.wait_ge(S["wl_ready"], j * UNITS + (last_unit(k) + 1))
                dst, src = ffn_piece(ROUTED0, i, *w)
                sp.dma_start(dst, src).then_inc(loaded[(ROUTED0 + i) % SLOTS], 16)

            with sp.Fori(0, njobs) as j:
                w = weights_of(j)
                for i in range(SLOTS, FFN_PIECES):
                    load_job(j, i, w, i - SLOTS)
                with sp.If(j + 1 < njobs):
                    w = weights_of(j + 1)
                    for i in range(SLOTS):
                        load_job(j, i, w, FFN_PIECES - SLOTS + i)
            sp.wait_ge(S["comb_ready"], njobs * 4)
            sp.dma_start(out[0].rearrange("(t p) d -> p t d", p=P), xs[:, :, :]).then_inc(S["out_stored"], 16)
            sp.wait_ge(S["out_stored"], 16)

        @block.gpsimd
        def _(pool):
            chain = [0]

            def link(ins):
                chain[0] += 1
                ins.then_inc(S["pool_chain"], 1)
                pool.wait_ge(S["pool_chain"], chain[0])

            link(pool.memset(relb[:, :], NEG))
            pool.dma_start(relb[0:N_BUCKETS, :], rel_bias).then_inc(S["relb_loaded"], 16)
            pool.dma_start(bucketT[:, :], bucket_rows).then_inc(S["relb_loaded"], 16)
            rows = [(R_G1, norm1_g.rearrange("l (k p) -> (l k) p", p=P)), (R_G2, norm2_g.rearrange("l (k p) -> (l k) p", p=P)),
                    (R_OG, out_norm_g.rearrange("l (k p) -> (l k) p", p=P)),
                    (R_CW, conv_w.rearrange("l w (k p) -> (l w k) p", p=P)), (R_CB, conv_b.rearrange("l (k p) -> (l k) p", p=P)),
                    (R_BA, lru_ba.rearrange("l (k p) -> (l k) p", p=P)), (R_BX, lru_bx.rearrange("l (k p) -> (l k) p", p=P)),
                    (R_LAM, lru_lambda.rearrange("l (k p) -> (l k) p", p=P))]
            for r, src in rows:
                pool.dma_start(prow[r:r + src.shape[0], :], src).then_inc(S["small_loaded"], 16)
            for half in range(2):
                pool.dma_start(prow[R_QG:R_QG + 2, half * HD:(half + 1) * HD], q_norm_g).then_inc(S["small_loaded"], 16)
                pool.dma_start(prow[R_KG:R_KG + 2, half * HD:(half + 1) * HD], k_norm_g).then_inc(S["small_loaded"], 16)
            pool.dma_start(posr[:, :], cmp_pos.rearrange("l v (m e) d -> (l v m) (e d)", e=2)).then_inc(S["small_loaded"], 16)
            pool.dma_start(gateb[:, :, :], gate_b.partition_broadcast(P)).then_inc(S["small_loaded"], 16)
            pool.dma_start(w2[:, :, :, :], cmp_w2.rearrange("l v c d -> c l v d")).then_inc(S["small_loaded"], 16)
            pool.dma_start(rw[:, :, :], router_w[0].rearrange("(k p) e -> p k e", p=P)).then_inc(S["small_loaded"], 16)
            link(pool.memset(ident[:, :], 0.0))
            link(pool.affine_select(out=ident[:, :], in_=ident[:, :], compare_op=ALU.not_equal, fill=1.0, base=0,
                                    pattern=[[-1, P]], channel_multiplier=1))
            link(pool.memset(flip[:, :], 0.0))
            link(pool.affine_select(out=flip[:, :], in_=flip[:, :], compare_op=ALU.not_equal, fill=1.0, base=1 - P,
                                    pattern=[[1, P]], channel_multiplier=1))
            link(pool.memset(ones[:, :], 1.0))
            link(pool.affine_select(out=before[:, :], in_=ones[:, :], compare_op=ALU.is_gt, fill=0.0, base=0,
                                    pattern=[[1, P]], channel_multiplier=-1))
            link(pool.iota(slot_id[:, :], pattern=[[1, P]], base=0, channel_multiplier=0,
                           allow_small_or_imprecise_dtypes=True))
            link(pool.memset(cEPS[:, :], EPS))
            pool.memset(lruW[:, :, :, :], 0.0).then_inc(S["consts_set"], 1)
            pool.wait_ge(S["consts_set"], 1)
            pool.wait_ge(S["urow_ready"], 1)
            pool.dma_start(urows_dram, urow[:, :]).then_inc(S["rows_stored"], 16)
            pool.wait_ge(S["rows_stored"], 16)
            pool.dma_start(skew.rearrange("p (h i) -> p h i", h=NH), bass.AP(urows_dram.tensor, 0, [[1, P], [U_LEN, NH], [1, 2 * P]]))\
                .then_inc(S["skew_loaded"], 16)

            for l in range(DEPTH):
                L = l + 1
                if l > 0:
                    pool.wait_ge(S["igate_done"], l)
                for e in range(2):
                    for w, src in enumerate((lru_wa, lru_wx)):
                        pool.dma_start(lruW[e * HD:(e + 1) * HD, w, :, e * HD:(e + 1) * HD],
                                       src[l].rearrange("(m e) i j -> e i m j", e=2)[e]).then_inc(S["lru_w_loaded"], 16)
                pool.wait_ge(S["gate_ready"], L)
                link(pool.tensor_tensor(tt, gT, gT, ALU.mult))
                link(pool.tensor_scalar(tt, tt, 0.044715, 1.0, ALU.mult, ALU.add))
                pool.tensor_tensor(tt, tt, gT, ALU.mult).then_inc(S["gelu_in"], 1)
                pool.wait_ge(S["gelu_th"], L)
                link(pool.tensor_scalar(tt, tt, 1.0, 0.5, ALU.add, ALU.mult))
                link(pool.tensor_tensor(gT, gT, tt, ALU.mult))
                pool.wait_ge(S["exp_r"], L)
                link(pool.tensor_scalar(rr, rr, 1.0, None, ALU.add))
                pool.wait_ge(S["exp_i"], L)
                pool.tensor_scalar(ii, ii, 1.0, None, ALU.add).then_inc(S["pre_sig"], 1)
                pool.wait_ge(S["sig_ready"], L)
                link(pool.tensor_tensor(ii, ii, xc, ALU.mult))
                pool.wait_ge(S["tanh_r"], L)
                pool.tensor_scalar(aa, rr, 1.0, None, ALU.add).then_inc(S["pre_rec"], 1)
                pool.wait_ge(S["rec_ready"], L)
                link(pool.tensor_tensor(ii, ii, aa, ALU.mult))
                pool.wait_ge(S["sqrt_t"], L)
                link(pool.tensor_tensor(ii, ii, tt, ALU.mult))
                link(pool.tensor_scalar(ii, ii, 2.0, None, ALU.mult))
                link(pool.tensor_scalar(rr, rr, -1.0, 1.0, ALU.mult, ALU.add))
                pool.tensor_tensor(aa, aa, rr, ALU.mult).then_inc(S["mult_ready"], 1)
                pool.wait_ge(S["scan_ready"], L)
                link(pool.tensor_tensor(xc, gT, tt, ALU.mult))
                pool.tensor_tensor(tt, xc, xc, ALU.mult).then_inc(S["ysq_ready"], 1)

        @block.scalar
        def _(act):
            chain = [0]

            def link(ins):
                chain[0] += 1
                ins.then_inc(S["act_chain"], 1)
                act.wait_ge(S["act_chain"], chain[0])

            def norm_root(n):
                if n == 0:
                    act.wait_ge(S["x_loaded"], 16)
                    act.wait_ge(S["consts_set"], 1)
                elif n % 2 == 1:
                    act.wait_ge(S["x_mixed"], n // 2 + 1)
                else:
                    act.wait_ge(S["ffn_done"], n // 2)
                for t in range(NT):
                    link(act.activation(xn[:, t, :], xs[:, t, :], ACT.Square, accum_out=ssq[:, t:t + 1]))
                act.activation(rstd[:, :], ssq[:, :], ACT.Sqrt, scale=1.0 / D, bias=cEPS[:, :]).then_inc(S["root_done"], 1)

            def norm_turned(n, row):
                for k in range(4):
                    act.wait_ge(S["normT_done"], 4 * n + k // 2 + 1)
                    act.activation(hT[:, k, :], bank[k // 2][:, (k % 2) * SEQ:(k % 2 + 1) * SEQ], ACT.Copy,
                                   scale=par[:, row + k:row + k + 1]).then_inc(S["hT_act"], 1)

            act.wait_ge(S["params_transposed"], 1)
            act.activation(par[:, :], bank[0][:, 0:N_ROWS], ACT.Copy).then_inc(S["params_ready"], 1)
            act.activation(posT[:, :], bank[0][:, 128:128 + HD], ACT.Copy).then_inc(S["params_ready"], 1)
            act.wait_ge(S["urow_done"], 1)
            act.activation(urow[:, :], bank[1][0:NH, 0:U_LEN], ACT.Copy).then_inc(S["urow_ready"], 1)
            act.wait_ge(S["params_ready"], 2)
            for w, r in ((0, R_BA), (1, R_BX)):
                link(act.activation(nba[:, w, :], par[:, r:r + 8], ACT.Copy, scale=-1.0))
            link(act.activation(sp4[:, :], par[:, R_LAM:R_LAM + 8], ACT.Exp, scale=-1.0))
            link(act.activation(sp4[:, :], sp4[:, :], ACT.Ln, bias=1.0))
            link(act.activation(sp4[:, :], sp4[:, :], ACT.Copy, scale=4.0))

            for l in range(DEPTH):
                L = l + 1
                norm_root(2 * l)
                norm_turned(2 * l, R_G1 + 8 * l)
                if l == 0:
                    for c in range(4):
                        act.wait_ge(S["flip_done"], c + 1)
                        act.activation(biasU[:, 2 * c:2 * c + 2, :], bank[4 + c][:, :].rearrange("p (a b) -> p a b", a=2), ACT.Copy)\
                            .then_inc(S["bias_ready"], 1)
                act.wait_ge(S["q_done"], 2 * l + 1)
                act.activation(tok[:, 0, 0:512], bank[4][:, :], ACT.Copy).then_inc(S["tok_act"], 1)
                act.wait_ge(S["kv_done"], 2 * l + 1)
                act.activation(tok[:, 0, 768:1280], bank[0][:, :], ACT.Copy).then_inc(S["tok_act"], 1)
                act.wait_ge(S["gates_done"], 2 * l + 1)
                act.activation(tok[:, 0, 512:768], bank[6][:, 0:256], ACT.Copy).then_inc(S["tok_act"], 1)
                act.activation(tok[:, 0, 1280:1304], bank[6][:, 256:280], ACT.Copy).then_inc(S["tok_act"], 1)
                for m in range(NC_LRU):
                    act.wait_ge(S["lrux_done"], 2 * l + m // 2 + 1)
                    act.activation(xpad[:, m, 3:3 + SEQ], bank[2 + m // 2][:, (m % 2) * SEQ:(m % 2 + 1) * SEQ], ACT.Copy)\
                        .then_inc(S["lrux_ready"], 1)
                act.wait_ge(S["qk_root_in"], L)
                act.activation(rms20, rms20, ACT.Sqrt, scale=1.0 / HD, bias=cEPS[:, :]).then_inc(S["qk_root"], 1)
                for m in range(2):
                    act.wait_ge(S["lrug_done"], 2 * l + m + 1)
                    last = act.activation(gT[:, 2 * m:2 * m + 2, :], bank[4 + m][:, :].rearrange("p (a b) -> p a b", a=2), ACT.Copy)
                    if m == 0:
                        link(last)
                    else:
                        last.then_inc(S["gate_ready"], 1)
                for b in range(2):
                    act.wait_ge(S["T_done"], 4 * l + b + 1)
                    act.activation(qT[:, 2 * b:2 * b + 2, :], bank[6 + b][:, :].rearrange("p (a b) -> p a b", a=2), ACT.Copy,
                                   scale=par[:, R_QG + l:R_QG + l + 1]).then_inc(S["qT_ready"], 1)
                act.wait_ge(S["gs_in"], L)
                act.activation(gsig, gsig, ACT.Exp, scale=-1.0).then_inc(S["gs_exp"], 1)
                act.wait_ge(S["gelu_in"], L)
                act.activation(tt, tt, ACT.Tanh, scale=0.7978845608028654).then_inc(S["gelu_th"], 1)
                act.wait_ge(S["gelu_c_in"], L)
                act.activation(hct, hc2, ACT.Tanh, scale=0.7978845608028654).then_inc(S["gelu_c_th"], 1)
                for w, (done, dst, exp, b0) in enumerate((("rgate_done", rr, "exp_r", 4), ("igate_done", ii, "exp_i", 0))):
                    act.wait_ge(S[done], L)
                    for m in range(NC_LRU):
                        last = act.activation(dst[:, m, :], bank[b0 + m // 2][:, (m % 2) * SEQ:(m % 2 + 1) * SEQ], ACT.Exp,
                                              scale=-1.0, bias=nba[:, w, l * NC_LRU + m:l * NC_LRU + m + 1])
                        if m < NC_LRU - 1:
                            link(last)
                    last.then_inc(S[exp], 1)
                act.wait_ge(S["sig_ready"], L)
                for m in range(NC_LRU):
                    last = act.activation(rr[:, m, :], rr[:, m, :], ACT.Tanh, scale=sp4[:, l * NC_LRU + m:l * NC_LRU + m + 1])
                    if m < NC_LRU - 1:
                        link(last)
                last.then_inc(S["tanh_r"], 1)
                act.wait_ge(S["kcn_in"], L)
                act.activation(kcs, kcs, ACT.Sqrt, scale=1.0 / HD, bias=cEPS[0:NG * N_CMP, :]).then_inc(S["kcn_root"], 1)
                act.wait_ge(S["tanh_r"], L)
                act.wait_ge(S["gelu_th"], L)
                act.wait_ge(S["rec_ready"], L)
                act.activation(tt, rr, ACT.Sqrt).then_inc(S["sqrt_t"], 1)
                act.wait_ge(S["cs_in"], L)
                act.activation(cS, cS, ACT.Exp).then_inc(S["cs_exp"], 1)
                for c in range(4):
                    act.wait_ge(S["cpT_done"], 4 * l + c + 1)
                    act.activation(cPT[:, 4 * c:4 * c + 4, :], bank[c % 2][0:N_CMP, :].rearrange("p (a b) -> p a b", a=4), ACT.Copy)\
                        .then_inc(S["cpT_ready"], 1)
                for i in range(NT * NH + 1):
                    if i < NT * NH:
                        W = P * (i // NH + 1)
                        n = NT * NH * l + i
                        act.wait_ge(S["s_ready"], n + 1)
                        if i >= 2:
                            act.wait_ge(S["pT_done"], n - 1)
                        for b in range(2):
                            last = act.activation(sP[:, i % 2, b * W:(b + 1) * W], sS[:, i % 2, b * W:(b + 1) * W], ACT.Exp,
                                                  bias=mx[:, 16 * (i % 2) + b:16 * (i % 2) + b + 1],
                                                  accum_out=den[:, 16 * (i % 2) + b:16 * (i % 2) + b + 1])
                            if b == 0:
                                link(last)
                        last.then_inc(S["e_ready"], 1)
                    if i >= 1:
                        k = i - 1
                        n = NT * NH * l + k
                        W = P * (k // NH + 1)
                        act.wait_ge(S["pT_done"], n + 1)
                        if k >= 2:
                            act.wait_ge(S["o_done"], n - 1)
                        act.activation(sT[:, k % 2, 0:2 * W], bank[2 + k % 2][:, 0:2 * W], ACT.Copy).then_inc(S["pT_ready"], 1)
                for t in range(NT):
                    act.wait_ge(S["o_done"], NT * NH * l + NH * (t + 1))
                    link(act.activation(oS[:, t, :], bank[4 + t][:, :], ACT.Copy))
                    act.activation(sS[:, 0, :], oS[:, t, :], ACT.Square, accum_out=nrm[:, t:t + 1]).then_inc(S["o_ready"], 1)
                act.wait_ge(S["lsum_done"], L)
                act.activation(nrm[:, 2:4], bank[1][:, 0:2], ACT.Copy).then_inc(S["mroot_in"], 1)
                act.wait_ge(S["mroot_in"], L)
                act.wait_ge(S["o_ready"], 2 * L)
                act.activation(nrm[:, 4:8], nrm[:, 0:4], ACT.Sqrt, scale=1.0 / D_LRU, bias=cEPS[:, :]).then_inc(S["mroot"], 1)
                act.wait_ge(S["ysq_ready"], L)
                for m in range(NC_LRU):
                    act.activation(mixT[:, m, :], xc[:, m, :], ACT.Copy,
                                   scale=par[:, R_OG + 8 * l + m:R_OG + 8 * l + m + 1]).then_inc(S["ymix_ready"], 1)
                for m in range(4):
                    act.wait_ge(S["oT_done"], 2 * l + m // 2 + 1)
                    act.activation(mixT[:, 4 + m, :], bank[6 + m // 2][:, (m % 2) * SEQ:(m % 2 + 1) * SEQ], ACT.Copy,
                                   scale=par[:, R_OG + 8 * l + 4 + m:R_OG + 8 * l + 5 + m]).then_inc(S["oT_ready"], 1)
                norm_root(2 * l + 1)
                norm_turned(2 * l + 1, R_G2 + 8 * l)
                if l == 0:
                    for s in range(NT * FCH):
                        act.wait_ge(S["gu_done"], s + 1)
                        if s >= 2:
                            act.wait_ge(S["hid_ready"], s - 1)
                        act.activation(sil[:, s % 2, :], bank[2 * (s % 2)][:, 0:FN], ACT.Silu).then_inc(S["silu_ready"], 1)
                else:
                    act.wait_ge(S["texp_in"], 1)
                    act.activation(wt[:, 0:2], wt[:, 0:2], ACT.Exp).then_inc(S["texp"], 1)
                    act.wait_ge(S["jobs_ready"], 1)
                    njobs = act.value_load(jobi[0:1, 0:1], min_val=NE, max_val=JOBS)

                    def high(j, u, first=False):
                        if first_piece(u) is not None:
                            wait_job_piece(act, j, first_piece(u))
                        if not first:
                            act.wait_ge(S["unit_used"], j * UNITS + (u - USLOTS + 1))
                        act.activation(unit_in(wh, u), unit_source(u), ACT.Copy).then_inc(S["wh_ready"], 1)

                    def tokens_high(j):
                        for c in range(2):
                            act.wait_ge(S["xg_done"], 2 * j + (c + 1))
                            for k in range(4 * c, 4 * c + 4):
                                act.activation(xgh[:, k, :], bank[4 + c][:, (k % 4) * P:(k % 4 + 1) * P], ACT.Copy,
                                               scale=par[:, R_G2 + 8 + k:R_G2 + 9 + k]).then_inc(S["xg_high"], 1)

                    def turned_high(j, k):
                        a, b = done_tiles(k), done_tiles(k + 1)
                        act.wait_ge(S["hidT_done"], j * FCH + (NT * FCH + k + 1))
                        act.activation(ehidTh[:, a:b, :], bank[4 + k % 2][:, 0:(b - a) * P].rearrange("p (a b) -> p a b", b=P),
                                       ACT.Copy).then_inc(S["hidT_high"], 1)

                    high(0, 0, True)
                    high(0, 1, True)
                    tokens_high(0)
                    high(0, 2, True)
                    with act.Fori(0, njobs) as j:
                        for u in range(USLOTS, UNITS):
                            q = (u - 6) // 4
                            if u % 4 == 2 and u >= 6 and q < FCH:
                                act.wait_ge(S["unit_used"], j * UNITS + (4 * q + 4))
                                act.wait_ge(S["hid_ready"], j * FCH + (NT * FCH + q - 1))
                                act.activation(esil[:, q % 2, :], bank[2 * (q % 2)][:, 0:FN], ACT.Silu).then_inc(S["silu_ready"], 1)
                                if q >= 1:
                                    turned_high(j, q - 1)
                            if u == 4 * FCH + 5:
                                turned_high(j, FCH - 1)
                            high(j, u)
                        act.wait_ge(S["unit_used"], j * UNITS + UNITS)
                        act.activation(ye[:, 512:1024], bank[7][:, :], ACT.Copy).then_inc(S["ye_act"], 1)
                        with act.If(j + 1 < njobs):
                            high(j + 1, 0)
                            high(j + 1, 1)
                            tokens_high(j + 1)
                            high(j + 1, 2)

        @block.vector
        def _(dve):
            chain = [0]

            def link(ins):
                chain[0] += 1
                ins.then_inc(S["dve_chain"], 1)
                dve.wait_ge(S["dve_chain"], chain[0])

            def norm(n, row):
                dve.wait_ge(S["root_done"], n + 1)
                link(dve.reciprocal(rstd[:, :], rstd[:, :]))
                for t in range(NT):
                    dve.tensor_scalar(xn[:, t, :], xs[:, t, :], rstd[:, t:t + 1], None, ALU.mult).then_inc(S["norm_ready"], 1)
                for k in range(4, 8):
                    dve.wait_ge(S["normT_done"], 4 * n + k // 2 + 1)
                    dve.tensor_scalar(hT[:, k, :], bank[k // 2][:, (k % 2) * SEQ:(k % 2 + 1) * SEQ],
                                      par[:, row + k:row + k + 1], None, ALU.mult).then_inc(S["hT_dve"], 1)

            dve.wait_ge(S["params_ready"], 2)
            for l in range(DEPTH):
                L = l + 1
                norm(2 * l, R_G1 + 8 * l)
                link(dve.memset(xpad[:, :, 0:3], 0.0))
                dve.wait_ge(S["q_done"], 2 * l + 2)
                dve.tensor_copy(tok[:, 1, 0:512], bank[5][:, :]).then_inc(S["tok_dve"], 1)
                dve.wait_ge(S["kv_done"], 2 * l + 2)
                dve.tensor_copy(tok[:, 1, 768:1280], bank[1][:, :]).then_inc(S["tok_dve"], 1)
                dve.wait_ge(S["gates_done"], 2 * l + 2)
                dve.tensor_copy(tok[:, 1, 512:768], bank[7][:, 0:256]).then_inc(S["tok_dve"], 1)
                dve.tensor_copy(tok[:, 1, 1280:1304], bank[7][:, 256:280]).then_inc(S["tok_dve"], 1)
                dve.wait_ge(S["tok_dve"], 4 * L)
                dve.wait_ge(S["tok_act"], 4 * L)
                for t in range(NT):
                    link(dve.tensor_tensor(sq[:, t, :], tok[:, t, 0:1280], tok[:, t, 0:1280], ALU.mult))
                for t in range(NT):
                    last = dve.tensor_reduce(rms20[:, t, :], sq[:, t, :].rearrange("p (a b) -> p a b", b=HD), AX, ALU.add)
                    if t == 0:
                        link(last)
                last.then_inc(S["qk_root_in"], 1)
                dve.wait_ge(S["qk_root"], L)
                link(dve.reciprocal(rms20, rms20))
                for t in range(NT):
                    link(dve.tensor_tensor(qn[:, t].rearrange("p h (g d) -> p h g d", g=NG),
                                           tok[:, t, 0:512].rearrange("p (g h d) -> p h g d", g=NG, h=HPG),
                                           rms20[:, t, 0:8].rearrange("p (g h a) -> p h g a", g=NG, a=1)
                                           .to_broadcast([P, HPG, NG, HD]), ALU.mult))
                    kk = tok[:, t, 768:1280].rearrange("p (b c g d) -> p b c g d", b=2, c=2, g=NG)[:, :, 0]
                    rk = rms20[:, t, 12:20].rearrange("p (b c g a) -> p b c g a", b=2, c=2, g=NG)[:, :, 0]
                    last = dve.tensor_tensor(kn[:, t].rearrange("p b (g d) -> p b g d", g=NG), kk,
                                             rk.to_broadcast([P, 2, NG, HD]), ALU.mult)
                    if t == 0:
                        link(last)
                last.then_inc(S["qk_ready"], 1)
                dve.tensor_tensor(gsig, tok[:, :, 1280:1304], gateb[:, l:l + 1, :].to_broadcast([P, NT, 3 * NH]),
                                  ALU.add).then_inc(S["gs_in"], 1)
                dve.wait_ge(S["lrux_ready"], 4 * L)
                for m in range(NC_LRU):
                    cw = [par[:, R_CW + 16 * l + 4 * w + m:R_CW + 16 * l + 4 * w + m + 1] for w in range(CONV)]
                    cb = par[:, R_CB + 4 * l + m:R_CB + 4 * l + m + 1]
                    link(dve.tensor_scalar(xc[:, m, :], xpad[:, m, 0:SEQ], cw[0], cb, ALU.mult, ALU.add))
                    for w in range(1, CONV):
                        last = dve.scalar_tensor_tensor(xc[:, m, :], xpad[:, m, w:w + SEQ], cw[w], xc[:, m, :], ALU.mult, ALU.add)
                        if w < CONV - 1:
                            link(last)
                    last.then_inc(S["conv_ready"], 1)
                dve.wait_ge(S["T_done"], 4 * l + 3)
                dve.tensor_scalar(kT, bank[0][:, :].rearrange("p (a b) -> p a b", a=2), par[:, R_KG + l:R_KG + l + 1], None,
                                  ALU.mult).then_inc(S["kT_ready"], 1)
                dve.wait_ge(S["T_done"], 4 * l + 4)
                for e in range(2):
                    for g in range(NG):
                        last = dve.tensor_copy(
                            kcv2[e * HD:(e + 1) * HD, :, g, :],
                            bank[1][g * HD:(g + 1) * HD, :].rearrange("p (v t e) -> p v t e", v=2, e=2)[:, :, :, e])
                        if (e, g) != (1, 1):
                            link(last)
                last.then_inc(S["kcv_ready"], 1)
                dve.wait_ge(S["kcv_ready"], L)
                for v in range(2):
                    s0 = kcv2[:, v, 0, 0:1]
                    src = bass.AP(s0.tensor, s0.offset, [list(s0.ap[0]), [1, L2], [P, NG], [CMP_STRIDE // 2, N_CMP]])
                    p0 = posT[:, (2 * l + v) * L2:(2 * l + v) * L2 + 1]
                    pv = bass.AP(p0.tensor, p0.offset, [list(p0.ap[0]), [1, L2], [0, NG], [0, N_CMP]])
                    dve.tensor_tensor(blk[:, v, :].rearrange("p (m g n) -> p m g n", m=L2, g=NG), src, pv, ALU.add)\
                       .then_inc(S["blk_ready"], 1)
                dve.wait_ge(S["gs_exp"], L)
                link(dve.tensor_scalar(gsig, gsig, 1.0, None, ALU.add))
                link(dve.reciprocal(gsig, gsig))
                dve.wait_ge(S["cmph_done"], L)
                link(dve.tensor_copy(hc, bank[2][:, 0:60]))
                link(dve.tensor_tensor(hc2, hc, hc, ALU.mult))
                link(dve.tensor_scalar(hc2, hc2, 0.044715, 1.0, ALU.mult, ALU.add))
                dve.tensor_tensor(hc2, hc2, hc, ALU.mult).then_inc(S["gelu_c_in"], 1)
                dve.wait_ge(S["gelu_c_th"], L)
                link(dve.tensor_scalar(hct, hct, 1.0, 0.5, ALU.add, ALU.mult))
                dve.tensor_tensor(hc, hc, hct, ALU.mult).then_inc(S["gelu_c_ready"], 1)
                dve.wait_ge(S["kc_done2"], L)
                nb = NG * N_CMP
                link(dve.tensor_copy(kcn[:, 0:HD], bank[2][0:nb, 64:128]))
                dve.tensor_copy(vcs, bank[2][0:N_CMP, 128:256]).then_inc(S["vc_ready"], 1)
                link(dve.tensor_tensor(kcsq, kcn[:, 0:HD], kcn[:, 0:HD], ALU.mult))
                dve.tensor_reduce(kcs, kcsq, AX, ALU.add).then_inc(S["kcn_in"], 1)
                dve.wait_ge(S["pre_sig"], L)
                link(dve.reciprocal(rr, rr))
                dve.reciprocal(ii, ii).then_inc(S["sig_ready"], 1)
                dve.wait_ge(S["kcn_root"], L)
                link(dve.reciprocal(kcs, kcs))
                link(dve.tensor_scalar(kcn[:, HD:P], kcn[:, 0:HD], kcs, None, ALU.mult))
                dve.tensor_copy(kcn[:, 0:HD], kcn[:, HD:P]).then_inc(S["kcn_ready"], 1)
                dve.wait_ge(S["pre_rec"], L)
                dve.reciprocal(aa, aa).then_inc(S["rec_ready"], 1)
                dve.wait_ge(S["kcT_done"], L)
                dve.tensor_scalar(kcT, bank[3][:, 0:nb], par[:, R_KG + l:R_KG + l + 1], None, ALU.mult).then_inc(S["kcT_ready"], 1)
                if l == 0:
                    dve.wait_ge(S["bias_ready"], 4)
                dve.wait_ge(S["cs_done"], L)
                link(dve.memset(cS, NEG))
                for t in range(NT):
                    n = CMP_SEEN[t]
                    first = CMP_BLOCK - 1 + P * (1 - t)
                    for g in range(NG):
                        c = t * HPG * 16
                        link(dve.scalar_tensor_tensor(
                            cS[:, t, g * HPG:(g + 1) * HPG, 0:n],
                            bank[g][:, c:c + HPG * 16].rearrange("p (h n) -> p h n", h=HPG)[:, :, 0:n], HD ** -0.5,
                            biasU[:, g * HPG:(g + 1) * HPG, first:first + CMP_STRIDE * (n - 1) + 1:CMP_STRIDE], ALU.mult, ALU.add))
                cSf = cS.rearrange("p t h n -> p (t h) n")
                link(dve.tensor_reduce(cmx, cSf, AX, ALU.max))
                link(dve.tensor_scalar(cmx, cmx, NEG / 10, None, ALU.max))
                dve.tensor_tensor(cSf, cSf, cmx.rearrange("p (a b) -> p a b", b=1).to_broadcast([P, NT * NH, 16]),
                                  ALU.subtract).then_inc(S["cs_in"], 1)
                dve.wait_ge(S["cs_exp"], L)
                link(dve.tensor_reduce(cden, cSf, AX, ALU.add))
                link(dve.tensor_scalar(cden, cden, 1e-30, None, ALU.max))
                link(dve.reciprocal(cden, cden))
                link(dve.tensor_tensor(cden.rearrange("p (t h) -> p t h", t=NT), cden.rearrange("p (t h) -> p t h", t=NT),
                                       gsig[:, :, 0:NH], ALU.mult))
                dve.tensor_tensor(cSf, cSf, cden.rearrange("p (a b) -> p a b", b=1).to_broadcast([P, NT * NH, 16]),
                                  ALU.mult).then_inc(S["cp_ready"], 1)
                dve.wait_ge(S["sqrt_t"], L)
                dve.wait_ge(S["mult_ready"], L)
                for m in range(NC_LRU):
                    last = dve.tensor_tensor_scan(tt[:, m, :], aa[:, m, :], ii[:, m, :], 0.0, ALU.mult, ALU.add)
                    if m < NC_LRU - 1:
                        link(last)
                last.then_inc(S["scan_ready"], 1)

                def scores(i):
                    t, h = i // NH, i % NH
                    W = P * (t + 1)
                    n = NT * NH * l + i
                    dve.wait_ge(S["s_done"], n + 1)
                    if i >= 2:
                        dve.wait_ge(S["e_ready"], n - 1)
                    s = sS[:, i % 2, 0:2 * W].rearrange("p (b k) -> p b k", b=2)
                    first = P * (1 - t)
                    link(dve.scalar_tensor_tensor(s, bank[6 + i % 2][:, 0:2 * W].rearrange("p (b k) -> p b k", b=2), HD ** -0.5,
                                                  biasU[:, h:h + 1, first:first + W].to_broadcast([P, 2, W]), ALU.mult, ALU.add))
                    m = mx[:, 16 * (i % 2):16 * (i % 2) + 2]
                    link(dve.tensor_reduce(m, s, AX, ALU.max))
                    dve.tensor_scalar(m, m, -1.0, None, ALU.mult).then_inc(S["s_ready"], 1)

                def weigh(i):
                    t, h = i // NH, i % NH
                    W = P * (t + 1)
                    dve.wait_ge(S["e_ready"], NT * NH * l + i + 1)
                    d = den[:, 16 * (i % 2):16 * (i % 2) + 2]
                    link(dve.reciprocal(d, d))
                    link(dve.tensor_tensor(d, d, gsig[:, t, NH + h:NH + h + NH + 1:NH], ALU.mult))
                    for b in range(2):
                        last = dve.tensor_scalar(sP[:, i % 2, b * W:(b + 1) * W], sP[:, i % 2, b * W:(b + 1) * W], d[:, b:b + 1],
                                                 None, ALU.mult)
                        if b == 0:
                            link(last)
                    last.then_inc(S["p_ready"], 1)

                for i in range(NT * NH + 1):
                    if i < NT * NH:
                        scores(i)
                    if i >= 1:
                        weigh(i - 1)
                dve.wait_ge(S["mroot"], L)
                link(dve.reciprocal(nrm[:, 4:8], nrm[:, 4:8]))
                for part in range(2):
                    for t in range(NT):
                        for c in range(2):
                            dve.wait_ge(S["out_done"], 8 * l + 4 * part + 2 * t + c + 1)
                            xo = xs[:, t, c * 512:(c + 1) * 512]
                            r = nrm[:, 6 + t:7 + t] if part == 0 else nrm[:, 4 + t:5 + t]
                            last = dve.scalar_tensor_tensor(xo, bank[4 * part + 2 * t + c][:, :], r, xo, ALU.mult, ALU.add)
                            if (part, t, c) != (1, 1, 1):
                                link(last)
                last.then_inc(S["x_mixed"], 1)
                dve.wait_ge(S["x_mixed"], L)
                norm(2 * l + 1, R_G2 + 8 * l)

                def hidden(s, n, q, tile):
                    dve.wait_ge(S["silu_ready"], n)
                    dve.tensor_tensor(hid[:, tile, q * FN:(q + 1) * FN], sil[:, s % 2, :], bank[1 + 2 * (s % 2)][:, 0:FN],
                                      ALU.mult).then_inc(S["hid_ready"], 1)

                if l == 0:
                    for s in range(NT * FCH + 2):
                        if s < NT * FCH:
                            if s // NT >= HALF:
                                dve.wait_ge(S["hidT_done"], s - NT * (HALF - 1) + 1)
                            hidden(s, s + 1, (s // NT) % HALF, s % NT)
                        if s >= 2:
                            k = s - 2
                            a, b = done_tiles(k // NT), done_tiles(k // NT + 1)
                            dve.wait_ge(S["hidT_done"], k + 1)
                            dve.tensor_copy(hidT[:, k % NT, a:b, :],
                                            bank[4 + k % 2][:, 0:(b - a) * P].rearrange("p (a b) -> p a b", b=P))\
                               .then_inc(S["hidT_ready"], 1)
                    for t in range(NT):
                        dve.wait_ge(S["down_used"], len(DOWN))
                        for c in range(2):
                            xo = xs[:, t, c * 512:(c + 1) * 512]
                            last = dve.tensor_tensor(xo, xo, bank[(6, 2)[t] + c][:, :], ALU.add)
                            if (t, c) != (1, 1):
                                link(last)
                    last.then_inc(S["ffn_done"], 1)
                    dve.wait_ge(S["ffn_done"], 1)
                    continue
                dve.wait_ge(S["log_done"], 1)
                link(dve.tensor_copy(logit, bank[4][:, 0:16].rearrange("p (a b) -> p a b", a=NT)))
                for t in range(NT):
                    link(dve.max(top8[:, t, :], logit[:, t, :]))
                    link(dve.max_index(idx8[:, t, :], top8[:, t, :], logit[:, t, :]))
                link(dve.tensor_copy(idxf, idx8[:, :, :]))
                dve.tensor_tensor(wt[:, 0:2], top8[:, :, 1], top8[:, :, 0], ALU.subtract).then_inc(S["texp_in"], 1)
                dve.wait_ge(S["texp"], 1)
                link(dve.tensor_scalar(wt[:, 2:4], wt[:, 0:2], 1.0, None, ALU.add))
                link(dve.reciprocal(wt[:, 2:4], wt[:, 2:4]))
                link(dve.tensor_tensor(wt[:, 4:6], wt[:, 0:2], wt[:, 2:4], ALU.mult))
                eid = slot_id[:, 0:NE]
                for t in range(NT):
                    link(dve.tensor_scalar(oh1[:, t, :], eid, idxf[:, t, 0:1], None, ALU.is_equal))
                    link(dve.tensor_scalar(oh2[:, t, :], eid, idxf[:, t, 1:2], None, ALU.is_equal))
                    link(dve.tensor_scalar(wexp[:, t, :], oh1[:, t, :], wt[:, 2 + t:3 + t], None, ALU.mult))
                    link(dve.scalar_tensor_tensor(wexp[:, t, :], oh2[:, t, :], wt[:, 4 + t:5 + t], wexp[:, t, :], ALU.mult, ALU.add))
                dve.tensor_tensor(memb, oh1, oh2, ALU.add).then_inc(S["pos_in"], 1)
                dve.wait_ge(S["pos_in"], 1)
                dve.wait_ge(S["pos_done"], 1)
                link(dve.tensor_copy(pos, bank[4][:, 32:48].rearrange("p (a b) -> p a b", a=NT)))
                link(dve.tensor_scalar(over, bank[4][:, 48:56], float(P), None, ALU.is_gt))
                link(dve.tensor_tensor_scan(rank, ones[:, 0:NE], over, 0.0, ALU.mult, ALU.add))
                link(dve.tensor_scalar(jobf[:, 0:1], rank[:, NE - 1:NE], float(NE), None, ALU.add))
                link(dve.tensor_copy(jobf[:, 1:NE + 1], eid))
                for t in range(NT):
                    link(dve.tensor_copy(table[:, 0:NE, t], memb[:, t, :]))
                    link(dve.tensor_copy(table[:, 0:NE, 2 + t], pos[:, t, :]))
                    link(dve.tensor_copy(table[:, 0:NE, 4 + t], wexp[:, t, :]))
                for o in range(OVER):
                    link(dve.scalar_tensor_tensor(pick, rank, float(o + 1), over, ALU.is_equal, ALU.mult))
                    link(dve.tensor_tensor_reduce(junk[:, 0, :], pick, eid, 1.0, 0.0, ALU.mult, ALU.add,
                                                  jobf[:, NE + 1 + o:NE + 2 + o]))
                    for t in range(NT):
                        link(dve.tensor_tensor_reduce(junk[:, 0, :], pick, memb[:, t, :], 1.0, 0.0, ALU.mult, ALU.add,
                                                      table[:, NE + o, t:t + 1]))
                        link(dve.tensor_tensor_reduce(junk[:, 0, :], pick, pos[:, t, :], 1.0, -float(P), ALU.mult, ALU.add,
                                                      table[:, NE + o, 2 + t:3 + t]))
                        link(dve.tensor_tensor_reduce(junk[:, 0, :], pick, wexp[:, t, :], 1.0, 0.0, ALU.mult, ALU.add,
                                                      table[:, NE + o, 4 + t:5 + t]))
                dve.tensor_copy(jobi[:, 0:JOBS + 1], jobf).then_inc(S["jobs_ready"], 1)
                dve.wait_ge(S["jobs_ready"], 1)
                njobs = dve.value_load(jobi[0:1, 0:1], min_val=NE, max_val=JOBS)

                def rest(j, u, first=False):
                    if not first:
                        dve.wait_ge(S["unit_used"], j * UNITS + (u - USLOTS + 1))
                    dve.wait_ge(S["wh_ready"], j * UNITS + (u + 1))
                    dve.tensor_tensor(unit_in(wl, u), unit_source(u), unit_in(wh, u).bitcast(F32), ALU.subtract)\
                       .then_inc(S["wl_ready"], 1)

                def tokens_rest(j):
                    for k in range(KD):
                        dve.wait_ge(S["xg_high"], 8 * j + 4 * (k // 4 + 1))
                        dve.scalar_tensor_tensor(xgl[:, k, :], bank[4 + k // 4][:, (k % 4) * P:(k % 4 + 1) * P],
                                                 par[:, R_G2 + 8 + k:R_G2 + 9 + k], xgh[:, k, :].bitcast(F32),
                                                 ALU.mult, ALU.subtract).then_inc(S["xg_ready"], 1)

                def turned_rest(j, k):
                    a, b = done_tiles(k), done_tiles(k + 1)
                    dve.wait_ge(S["hidT_high"], j * FCH + (k + 1))
                    dve.tensor_tensor(ehidTl[:, a:b, :], bank[4 + k % 2][:, 0:(b - a) * P].rearrange("p (a b) -> p a b", b=P),
                                      ehidTh[:, a:b, :].bitcast(F32), ALU.subtract).then_inc(S["hidT_ready"], 1)

                def select(j):
                    for t in range(NT):
                        dve.tensor_scalar(selM[:, t, :], slot_id[:, :], job[:, 2 + t:3 + t], job[:, t:t + 1], ALU.is_equal, ALU.mult)\
                           .then_inc(S["sel_ready"], 1)
                    for t in range(NT):
                        dve.tensor_scalar(selW[:, t, :], slot_id[:, :], job[:, 2 + t:3 + t], job[:, 4 + t:5 + t], ALU.is_equal, ALU.mult)\
                           .then_inc(S["sel_ready"], 1)

                def selection_turned(j):
                    dve.wait_ge(S["selT_done"], j + 1)
                    dve.tensor_copy(selT[:, :, :], bank[6][:, 0:NT * P].rearrange("p (a b) -> p a b", a=NT)).then_inc(S["selT_ready"], 1)

                dve.tensor_copy(job, table[:, 0, :]).then_inc(S["job_ready"], 1)
                dve.wait_ge(S["job_ready"], 1)
                select(0)
                rest(0, 0, True)
                rest(0, 1, True)
                tokens_rest(0)
                selection_turned(0)
                rest(0, 2, True)
                with dve.Fori(0, njobs) as j:
                    for u in range(USLOTS, UNITS):
                        q = (u - 6) // 4
                        if u % 4 == 2 and u >= 6 and q < FCH:
                            if q >= HALF:
                                dve.wait_ge(S["hidT_done"], j * FCH + (NT * FCH + q - HALF + 2))
                            dve.wait_ge(S["silu_ready"], j * FCH + (NT * FCH + q + 1))
                            dve.tensor_tensor(ehid[:, q % HALF * FN:(q % HALF + 1) * FN], esil[:, q % 2, :],
                                              bank[1 + 2 * (q % 2)][:, 0:FN], ALU.mult).then_inc(S["hid_ready"], 1)
                            if q >= 1:
                                turned_rest(j, q - 1)
                        if u == 4 * FCH + 5:
                            turned_rest(j, FCH - 1)
                        if u == 4 * FCH + 8:
                            with dve.If(j + 1 < njobs):
                                dve.tensor_copy(job, table[:, bass.ds(j + 1, 1), :].rearrange("p a c -> p (a c)"))\
                                   .then_inc(S["job_ready"], 1)
                                dve.wait_ge(S["job_ready"], j + 2)
                                select(j + 1)
                        rest(j, u)
                    dve.wait_ge(S["unit_used"], j * UNITS + UNITS)
                    dve.tensor_copy(ye[:, 0:512], bank[6][:, :]).then_inc(S["y_ready"], 1)
                    with dve.If(j + 1 < njobs):
                        rest(j + 1, 0)
                        rest(j + 1, 1)
                        tokens_rest(j + 1)
                    for q in range(4):
                        t, c = q // 2, q % 2
                        dve.wait_ge(S["comb_done"], 4 * j + (q + 1))
                        xo = xs[:, t, c * 512:(c + 1) * 512]
                        dve.tensor_tensor(xo, xo, bank[q][:, :], ALU.add).then_inc(S["comb_ready"], 1)
                    with dve.If(j + 1 < njobs):
                        selection_turned(j + 1)
                        rest(j + 1, 2)
                    dve.wait_ge(S["comb_ready"], 4 * j + 4)

        @block.tensor
        def _(pe):
            mm = pe.matmul

            def norm_turn(n):
                for k in range(KD):
                    for t in range(NT):
                        pe.wait_ge(S["norm_ready"], 2 * n + t + 1)
                        last = pe.transpose(bank[k // 2][:, (k % 2) * SEQ + t * P:(k % 2) * SEQ + (t + 1) * P],
                                            xn[:, t, k * P:(k + 1) * P], ident[:, :])
                    if k % 2 == 1:
                        last.then_inc(S["normT_done"], 1)

            pe.wait_ge(S["consts_set"], 1)
            pe.wait_ge(S["small_loaded"], 16 * 16)
            pe.transpose(bank[0][:, 0:N_ROWS], prow[:, :], ident[0:N_ROWS, 0:N_ROWS])
            pe.transpose(bank[0][:, 128:128 + HD], posr[:, :], ident[0:HD, 0:HD]).then_inc(S["params_transposed"], 1)
            pe.wait_ge(S["relb_loaded"], 32)
            mm(bank[1][0:NH, 0:U_LEN], relb[:, :], bucketT[:, :], start=True, stop=True).then_inc(S["urow_done"], 1)
            pe.wait_ge(S["params_ready"], 2)
            pe.wait_ge(S["urow_ready"], 1)

            for l in range(DEPTH):
                L = l + 1
                p0 = l * (MIX_PIECES + FFN_PIECES)
                norm_turn(2 * l)
                if l == 0:
                    pe.wait_ge(S["skew_loaded"], 16)
                    for c in range(4):
                        mm(bank[4 + c][:, :], flip[:, :], skew[:, c * 512:(c + 1) * 512], start=True, stop=True)\
                            .then_inc(S["flip_done"], 1)
                    pe.wait_ge(S["bias_ready"], 4)
                pe.wait_ge(S["hT_act"], 8 * l + 4)
                pe.wait_ge(S["hT_dve"], 8 * l + 4)

                def project(b, c0, w, lo, n, t):
                    for k in range(KD):
                        last = mm(bank[b + t][:, c0:c0 + n], hT[:, k, t * P:(t + 1) * P], w[:, k, lo:lo + n],
                                  start=(k == 0), stop=(k == KD - 1))
                    return last

                wait_piece(pe, p0)
                wA, wB = ring3(p0, KD, 768), ring3(p0 + 1, KD, W_B)
                for t in range(NT):
                    project(4, 0, wA, 0, 512, t).then_inc(S["q_done"], 1)
                project(6, 0, wA, 512, 256, 0)
                project(6, 0, wA, 512, 256, 1).then_inc(S["kc_done"], 1)
                wait_piece(pe, p0 + 1)
                for t in range(NT):
                    project(0, 0, wB, 0, 512, t).then_inc(S["kv_done"], 1)
                for t in range(NT):
                    project(6, 256, wB, 512, 24, t).then_inc(S["gates_done"], 1)
                for w in range(2):
                    wait_piece(pe, p0 + 2 + w)
                    if w == 1:
                        pe.wait_ge(S["tok_act"], 4 * l + 1)
                        pe.wait_ge(S["tok_dve"], 4 * l + 1)
                    wL = ring3(p0 + 2 + w, KD, 512)
                    for m in range(NC_LRU):
                        for k in range(KD):
                            last = mm(bank[2 + 2 * w + m // 2][:, (m % 2) * SEQ:(m % 2 + 1) * SEQ], wL[:, k, m * P:(m + 1) * P],
                                      hT[:, k, :], start=(k == 0), stop=(k == KD - 1))
                        if m == 1 or (m == 3):
                            last.then_inc(S["lrux_done" if w == 0 else "lrug_done"], 1)
                pe.wait_ge(S["tok_act"], 4 * L)
                pe.wait_ge(S["tok_dve"], 4 * L)
                pe.wait_ge(S["qk_ready"], L)
                for hh in range(HPG):
                    for t in range(NT):
                        last = pe.transpose(bank[6 + hh // 2][:, (hh % 2) * SEQ + t * P:(hh % 2) * SEQ + (t + 1) * P],
                                            qn[:, t, hh, :], ident[:, :])
                    if hh % 2 == 1:
                        last.then_inc(S["T_done"], 1)
                for b in range(2):
                    for t in range(NT):
                        last = pe.transpose(bank[0][:, b * SEQ + t * P:b * SEQ + (t + 1) * P], kn[:, t, b, :], ident[:, :])
                last.then_inc(S["T_done"], 1)
                for v in range(2):
                    for t in range(NT):
                        last = pe.transpose(bank[1][:, v * SEQ + t * P:v * SEQ + (t + 1) * P],
                                            tok[:, t, 512 + v * P:512 + (v + 1) * P], ident[:, :])
                last.then_inc(S["T_done"], 1)
                wait_piece(pe, p0 + 4)
                w1 = ring3(p0 + 4, 2 * L2, P)
                pe.wait_ge(S["lrux_ready"], 4 * L)
                nb = NG * N_CMP
                for v in range(2):
                    pe.wait_ge(S["blk_ready"], 2 * l + v + 1)
                    for m in range(L2):
                        last = mm(bank[2][:, v * nb:(v + 1) * nb], w1[:, v * L2 + m, :], blk[:, v, m * nb:(m + 1) * nb],
                                  start=(m == 0), stop=(m == L2 - 1))
                last.then_inc(S["cmph_done"], 1)
                pe.wait_ge(S["gate_ready"], L)
                pe.wait_ge(S["lru_w_loaded"], 16 * 4 * L)
                pe.wait_ge(S["conv_ready"], 4 * L)
                for w in range(2):
                    if w == 1:
                        pe.wait_ge(S["kT_ready"], L)
                        pe.wait_ge(S["kcv_ready"], L)
                    for m in range(NC_LRU):
                        last = mm(bank[(4, 0)[w] + m // 2][:, (m % 2) * SEQ:(m % 2 + 1) * SEQ], lruW[:, w, m, :], xc[:, m, :],
                                  start=True, stop=True)
                    last.then_inc(S[("rgate_done", "igate_done")[w]], 1)
                pe.wait_ge(S["gelu_c_ready"], L)
                mm(bank[2][0:nb, 64:128], hc[:, 0:nb], w2[:, l, 0, :], start=True, stop=True)
                for g in range(NG):
                    last = mm(bank[2][0:N_CMP, 128 + g * HD:128 + (g + 1) * HD], hc[:, nb + g * N_CMP:nb + (g + 1) * N_CMP],
                              w2[:, l, 1, :], start=True, stop=True)
                last.then_inc(S["kc_done2"], 1)
                pe.wait_ge(S["kcn_ready"], L)
                pe.transpose(bank[3][:, 0:nb], kcn, ident[0:nb, 0:nb]).then_inc(S["kcT_done"], 1)
                pe.wait_ge(S["qT_ready"], 2 * L)
                pe.wait_ge(S["kcT_ready"], L)
                pe.wait_ge(S["exp_i"], L)
                for t in range(NT):
                    for h in range(NH):
                        g, hh = h // HPG, h % HPG
                        c = (t * HPG + hh) * 16
                        last = mm(bank[g][:, c:c + N_CMP], qT[g * HD:(g + 1) * HD, hh, t * P:(t + 1) * P],
                                  kcT[g * HD:(g + 1) * HD, g * N_CMP:(g + 1) * N_CMP], start=True, stop=True)
                last.then_inc(S["cs_done"], 1)

                def score(i):
                    t, h = i // NH, i % NH
                    g, hh = h // HPG, h % HPG
                    W = P * (t + 1)
                    if i >= 2:
                        pe.wait_ge(S["s_ready"], NT * NH * l + i - 1)
                    for b in range(2):
                        last = mm(bank[6 + i % 2][:, b * W:(b + 1) * W], qT[g * HD:(g + 1) * HD, hh, t * P:(t + 1) * P],
                                  kT[g * HD:(g + 1) * HD, b, 0:W], start=True, stop=True)
                    last.then_inc(S["s_done"], 1)

                def turn(i):
                    W = P * (i // NH + 1)
                    n = NT * NH * l + i
                    pe.wait_ge(S["p_ready"], n + 1)
                    if i >= 2:
                        pe.wait_ge(S["pT_ready"], n - 1)
                    for b in range(2 * W // P):
                        last = pe.transpose(bank[2 + i % 2][:, b * P:(b + 1) * P], sP[:, i % 2, b * P:(b + 1) * P], ident[:, :])
                    last.then_inc(S["pT_done"], 1)

                def values(i):
                    t, h = i // NH, i % NH
                    g = h // HPG
                    n = NT * NH * l + i
                    pe.wait_ge(S["pT_ready"], n + 1)
                    o = bank[4 + t][:, h * HD:(h + 1) * HD]
                    mm(o, cPT[:, i, :], vcs[:, g * HD:(g + 1) * HD], start=True, stop=False)
                    for b in range(2):
                        for k in range(t + 1):
                            v = tok[:, k, 896 + 256 * b + g * HD:896 + 256 * b + (g + 1) * HD]
                            last = mm(o, sT[:, i % 2, (b * (t + 1) + k) * P:(b * (t + 1) + k + 1) * P], v,
                                      start=False, stop=(b == 1 and k == t))
                    last.then_inc(S["o_done"], 1)

                pe.wait_ge(S["kT_ready"], L)
                score(0)
                pe.wait_ge(S["cp_ready"], L)
                for c in range(4):
                    if c >= 2:
                        pe.wait_ge(S["cpT_ready"], 4 * l + c - 1)
                    for a in range(4):
                        i = 4 * c + a
                        last = pe.transpose(bank[c % 2][0:N_CMP, a * P:(a + 1) * P], cS[:, i // NH, i % NH, 0:N_CMP], ident[:, :])
                    last.then_inc(S["cpT_done"], 1)
                pe.wait_ge(S["cpT_ready"], 4 * L)
                pe.wait_ge(S["vc_ready"], L)
                pe.wait_ge(S["exp_r"], L)
                for i in range(1, NT * NH + 2):
                    if i < NT * NH:
                        score(i)
                    if i <= NT * NH:
                        turn(i - 1)
                    if i >= 2:
                        values(i - 2)
                pe.wait_ge(S["ysq_ready"], L)
                for t in range(NT):
                    for m in range(NC_LRU):
                        last = mm(bank[1][:, t:t + 1], tt[:, m, t * P:(t + 1) * P], ones[:, 0:1], start=(m == 0), stop=(m == NC_LRU - 1))
                last.then_inc(S["lsum_done"], 1)
                pe.wait_ge(S["s_ready"], NT * NH * L)
                pe.wait_ge(S["o_ready"], NT * L)
                for m in range(4):
                    for t in range(NT):
                        last = pe.transpose(bank[6 + m // 2][:, (m % 2) * SEQ + t * P:(m % 2) * SEQ + (t + 1) * P],
                                            oS[:, t, m * P:(m + 1) * P], ident[:, :])
                    if m % 2 == 1:
                        last.then_inc(S["oT_done"], 1)
                for part in range(2):
                    wait_piece(pe, p0 + 5 + part)
                    if part == 0:
                        pe.wait_ge(S["ymix_ready"], 4 * L)
                        pe.wait_ge(S["mroot_in"], L)
                        pe.wait_ge(S["pT_ready"], NT * NH * L)
                    else:
                        pe.wait_ge(S["oT_ready"], 4 * L)
                    wo = ring3(p0 + 5 + part, 4, D)
                    for t in range(NT):
                        for c in range(2):
                            for m in range(4):
                                last = mm(bank[4 * part + 2 * t + c][:, :], mixT[:, 4 * part + m, t * P:(t + 1) * P],
                                          wo[:, m, c * 512:(c + 1) * 512], start=(m == 0), stop=(m == 3))
                            last.then_inc(S["out_done"], 1)
                norm_turn(2 * l + 1)
                pe.wait_ge(S["hT_act"], 8 * l + 8)
                pe.wait_ge(S["hT_dve"], 8 * l + 8)

                def gate_up(p, q, lhs, s, last_tile):
                    lo = (q % 2) * FN
                    for w in range(2):
                        wr = ring3(p + 2 * (q // 2) + w, KD, FCOLS)
                        for k in range(KD):
                            last = mm(bank[2 * (s % 2) + w][:, 0:FN], lhs(k), wr[:, k, lo:lo + FN],
                                      start=(k == 0), stop=(k == KD - 1))
                        if w == 0 and last_tile and q % 2 == 1:
                            last.then_inc(S["gate_used"], 1)
                    last.then_inc(S["gu_done"], 1)

                def turn_hidden(q, tile, b):
                    a, z = done_tiles(q), done_tiles(q + 1)
                    for i in range(a, z):
                        lo = i * P % (HALF * FN)
                        last = pe.transpose(bank[b][:, (i - a) * P:(i - a + 1) * P], hid[:, tile, lo:lo + P], ident[:, :])
                    last.then_inc(S["hidT_done"], 1)

                if l == 0:
                    p = p0 + MIX_PIECES
                    for s in range(NT * FCH + NT):
                        q, t = s // NT, s % NT
                        if s < NT * FCH:
                            if q % 2 == 0 and t == 0:
                                wait_piece(pe, p + q)
                                wait_piece(pe, p + q + 1)
                            if s >= 2:
                                pe.wait_ge(S["hid_ready"], s - 1)
                            gate_up(p, q, lambda k: hT[:, k, t * P:(t + 1) * P], s, t == NT - 1)
                        if s >= NT:
                            k = s - NT
                            pe.wait_ge(S["hid_ready"], k + 1)
                            if k >= 2:
                                pe.wait_ge(S["hidT_ready"], k - 1)
                            turn_hidden(k // NT, k % NT, 4 + k % 2)
                    pe.wait_ge(S["hidT_ready"], NT * FCH)
                    i = 0
                    for c, n in enumerate(DOWN):
                        wait_piece(pe, p + 8 + c)
                        wd = ring3(p + 8 + c, n, D)
                        for r in range(n):
                            for t in range(NT):
                                for o in range(2):
                                    last = mm(bank[(6, 2)[t] + o][:, :], hidT[:, t, i, :], wd[:, r, o * 512:(o + 1) * 512],
                                              start=(i == 0), stop=(i == FT - 1), skip_group_check=True)
                            i += 1
                        last.then_inc(S["down_used"], 1)
                    continue
                for t in range(NT):
                    for k in range(KD):
                        last = mm(bank[4][:, t * NE:(t + 1) * NE], hT[:, k, t * P:(t + 1) * P], rw[:, k, :], start=(k == 0), stop=(k == KD - 1))
                last.then_inc(S["log_done"], 1)
                pe.wait_ge(S["pos_in"], 1)
                mm(bank[4][:, 32:40], before[:, :], memb[:, 0, :], start=True, stop=True)
                mm(bank[4][:, 40:48], ones[:, :], memb[:, 0, :], start=True, stop=False)
                mm(bank[4][:, 40:48], before[:, :], memb[:, 1, :], start=False, stop=True)
                mm(bank[4][:, 48:56], ones[:, :], memb[:, 0, :], start=True, stop=False)
                mm(bank[4][:, 48:56], ones[:, :], memb[:, 1, :], start=False, stop=True).then_inc(S["pos_done"], 1)
                pe.wait_ge(S["jobs_ready"], 1)
                njobs = pe.value_load(jobi[0:1, 0:1], min_val=NE, max_val=JOBS)

                def gather(j):
                    pe.wait_ge(S["sel_ready"], 4 * j + 2)
                    for c in range(2):
                        for k in range(4 * c, 4 * c + 4):
                            for t in range(NT):
                                last = mm(bank[4 + c][:, (k % 4) * P:(k % 4 + 1) * P], xn[:, t, k * P:(k + 1) * P], selM[:, t, :],
                                          start=(t == 0), stop=(t == NT - 1))
                        last.then_inc(S["xg_done"], 1)

                def turn_selection(j):
                    pe.wait_ge(S["sel_ready"], 4 * j + 4)
                    for t in range(NT):
                        last = pe.transpose(bank[6][:, t * P:(t + 1) * P], selW[:, t, :], ident[:, :])
                    last.then_inc(S["selT_done"], 1)

                def split_product(j, u, outs, high, rest, start, stop):
                    h, low = unit_in(wh, u), unit_in(wl, u)
                    pe.wait_ge(S["wh_ready"], j * UNITS + (u + 1))
                    for k, o, lo, hi in outs:
                        mm(o, high(k), h[:, k, lo:hi], start=start and k == 0, stop=False, skip_group_check=True)
                        mm(o, rest(k), h[:, k, lo:hi], start=False, stop=False, skip_group_check=True)
                    pe.wait_ge(S["wl_ready"], j * UNITS + (u + 1))
                    for k, o, lo, hi in outs:
                        last = mm(o, high(k), low[:, k, lo:hi], start=False, stop=stop and k == h.shape[1] - 1, skip_group_check=True)
                    last.then_inc(S["unit_used"], 1)

                def turn_expert_hidden(k):
                    a, z = done_tiles(k), done_tiles(k + 1)
                    for i in range(a, z):
                        lo = i * P % (HALF * FN)
                        last = pe.transpose(bank[4 + k % 2][:, (i - a) * P:(i - a + 1) * P], ehid[:, lo:lo + P], ident[:, :])
                    last.then_inc(S["hidT_done"], 1)

                gather(0)
                turn_selection(0)
                pe.wait_ge(S["xg_ready"], 8)
                with pe.Fori(0, njobs) as j:
                    for q in range(FCH):
                        pe.wait_ge(S["hid_ready"], j * FCH + (NT * FCH + q - 1))
                        for w in range(2):
                            for kh in range(2):
                                split_product(j, 4 * q + 2 * w + kh,
                                                     [(k, bank[2 * (q % 2) + w][:, 0:FN], 0, FN) for k in range(4)],
                                                     lambda k: xgh[:, 4 * kh + k, :], lambda k: xgl[:, 4 * kh + k, :],
                                                     kh == 0, kh == 1)
                        if q >= 1:
                            pe.wait_ge(S["hid_ready"], j * FCH + (NT * FCH + q))
                            if q >= 3:
                                pe.wait_ge(S["hidT_ready"], j * FCH + (NT * FCH + q - 2))
                            turn_expert_hidden(q - 1)
                    for i in range(FT):
                        for s in range(1, FCH + 1):
                            if done_tiles(s - 1) == i:
                                pe.wait_ge(S["hidT_ready"], j * FCH + (NT * FCH + s))
                        split_product(j, 4 * FCH + i, [(0, bank[6 + o][:, :], o * 512, (o + 1) * 512) for o in range(2)],
                                             lambda k: ehidTh[:, i, :], lambda k: ehidTl[:, i, :], i == 0, i == FT - 1)
                        if i == 1:
                            pe.wait_ge(S["hid_ready"], j * FCH + (NT * FCH + FCH))
                            pe.wait_ge(S["hidT_ready"], j * FCH + (NT * FCH + FCH - 2))
                            turn_expert_hidden(FCH - 1)
                    with pe.If(j + 1 < njobs):
                        gather(j + 1)
                    pe.wait_ge(S["y_ready"], j + 1)
                    pe.wait_ge(S["ye_act"], j + 1)
                    pe.wait_ge(S["selT_ready"], j + 1)
                    for o in range(4):
                        t, c = o // 2, o % 2
                        mm(bank[o][:, :], selT[:, t, :], ye[:, c * 512:(c + 1) * 512], start=True, stop=True)\
                            .then_inc(S["comb_done"], 1)
                    with pe.If(j + 1 < njobs):
                        turn_selection(j + 1)
                        pe.wait_ge(S["xg_ready"], 8 * j + 16)
                    pe.wait_ge(S["comb_ready"], 4 * j + 4)


_INS = ['x', 'rel_bias', 'norm1_g', 'w_in', 'conv_w', 'conv_b', 'lru_wa', 'lru_ba', 'lru_wx', 'lru_bx', 'lru_lambda',
        'q_norm_g', 'k_norm_g', 'cmp_pos', 'cmp_w1', 'cmp_w2', 'gate_b', 'out_norm_g', 'w_out', 'norm2_g',
        'ffn_w_gate', 'ffn_w_up', 'ffn_w_down', 'router_w', 'moe_w_gate', 'moe_w_up', 'moe_w_down']


def bucket_constant():
    import math
    import numpy as np
    rows = np.zeros((N_BUCKETS + 1, U_LEN), np.float32)
    exact, far = N_BUCKETS // 2, 128
    for j in range(U_LEN):
        dist = 2 * P - 1 - j
        if dist < 0:
            b = N_BUCKETS
        elif dist < exact:
            b = dist
        else:
            b = min(exact + int(np.float32(math.log(dist / exact)) / np.float32(math.log(far / exact)) * (N_BUCKETS - exact)),
                    N_BUCKETS - 1)
        rows[b, j] = 1.0
    return rows


def kernel(**inputs):
    import numpy as _np
    import concourse.bacc as _bacc
    from concourse import mybir as _mybir
    from concourse.bass_utils import run_bass_kernel_spmd as _run

    nc = _bacc.Bacc("TRN2", target_bir_lowering=False, num_devices=1)
    arrays, args = {}, []
    for name in _INS:
        a = _np.ascontiguousarray(inputs[name])
        arrays[f"in_{name}_dram"] = a
        args.append(nc.dram_tensor(f"in_{name}_dram", a.shape, _mybir.dt.from_np(a.dtype), kind="ExternalInput").ap())
    rows = bucket_constant()
    arrays["bucket_rows_dram"] = rows
    args.append(nc.dram_tensor("bucket_rows_dram", rows.shape, F32, kind="ExternalInput").ap())
    args.append(nc.dram_tensor("out_0_dram", (1, SEQ, D), F32, kind="ExternalOutput").ap())
    build(nc, *args)
    r = _run(nc, [arrays], core_ids=[0])
    return r.results[0]["out_0_dram"]
```

```python
from contextlib import ExitStack

import concourse.bass as bass
from concourse import mybir

F32 = mybir.dt.float32
F32R = mybir.dt.float32r
I32 = mybir.dt.int32
U32 = mybir.dt.uint32
ALU = mybir.AluOpType
ACT = mybir.ActivationFunctionType
AX = mybir.AxisListType.X

P = 128
D = 1024
SEQ = 256
NT = SEQ // P
KD = D // P
DEPTH = 2
D_LRU = 512
NC_LRU = D_LRU // P
HD = 64
NH = 8
NG = 2
HPG = NH // NG
CONV = 4
CMP_BLOCK, CMP_STRIDE = 32, 16
N_CMP = (SEQ - CMP_BLOCK) // CMP_STRIDE + 1
CMP_SEEN = (P // CMP_STRIDE - CMP_BLOCK // CMP_STRIDE + 1, N_CMP)
L2 = CMP_BLOCK // 2
N_BUCKETS = 32
D_FF = 2816
NE = 8
D_IN = 2 * D_LRU + NH * HD + 6 * NG * HD + 3 * NH
OFF_Q = 2 * D_LRU
OFF_KV = OFF_Q + NH * HD
W_B = D_IN - OFF_KV - 2 * P
EPS = 1e-6
NEG = -1e30
U_LEN = 3 * P

SLOTS = 3
SLOT = 6 * D
FN = D_FF // 8
FCH = D_FF // FN
FT = D_FF // P
HALF = FCH // 2
MIX_PIECES = 7
FFN_PIECES = FT // 2
ARENA = 17100
ROUTED0 = 2 * MIX_PIECES + FFN_PIECES
OVER = 3
JOBS = NE + OVER
UNIT = 4 * FN
UNITS = 4 * FCH + FT
USLOTS = 3
EDOWN = (3, 3, 3, 3, 3, 3, 2, 2)
DUNITS = [(g, u) for s in range(FFN_PIECES + 1)
          for g, us in ((s, range(4)), (s - 1, (4, 5))) if 0 <= g < FFN_PIECES for u in us]
EXPERT_PIECES = 2 * FCH + len(EDOWN)
HALVES = 2 * SLOTS
HALF_SLOT = SLOT // 2

R_G1, R_G2, R_OG = 0, 16, 32
R_CW, R_CB, R_BA, R_BX, R_LAM = 48, 80, 88, 96, 104
R_QG, R_KG, N_ROWS = 112, 114, 116


def done_tiles(c):
    return c * FN // P


def build(nc, x, rel_bias, norm1_g, w_in, conv_w, conv_b, lru_wa, lru_ba, lru_wx, lru_bx, lru_lambda,
          q_norm_g, k_norm_g, cmp_pos, cmp_w1, cmp_w2, gate_b, out_norm_g, w_out, norm2_g,
          ffn_w_gate, ffn_w_up, ffn_w_down, router_w, moe_w_gate, moe_w_up, moe_w_down,
          bucket_rows, out):
    ctx = ExitStack()
    with ctx:
        def sb(name, shape, dt=F32):
            return ctx.enter_context(nc.sbuf_tensor(name, shape, dt))

        def sem(name):
            return ctx.enter_context(nc.semaphore(name))

        ring = sb("ring", [P, SLOTS, SLOT])
        xs = sb("xs", [P, NT, D])
        xn = sb("xn", [P, NT, D])
        hT = sb("hT", [P, KD, SEQ])
        biasU = sb("biasU", [P, NH, 2 * P])
        ident = sb("ident", [P, P])
        flip = sb("flip", [P, P])
        ones = sb("ones", [P, P])
        before = sb("before", [P, P])
        slot_id = sb("slot_id", [P, P])
        prow = sb("prow", [N_ROWS, P])
        par = sb("par", [P, N_ROWS])
        posr = sb("posr", [HD, P])
        posT = sb("posT", [P, HD])
        gateb = sb("gateb", [P, DEPTH, 3 * NH])
        bucketT = sb("bucketT", [N_BUCKETS + 1, U_LEN])
        relb = sb("relb", [N_BUCKETS + 1, NH])
        urow = sb("urow", [NH, U_LEN])
        lruW = sb("lruW", [P, 2, NC_LRU, P])
        w2 = sb("w2", [P, DEPTH, 2, HD])
        rw = sb("rw", [P, KD, NE])
        hba = sb("hba", [P, 2, DEPTH * NC_LRU])
        nsp4 = sb("nsp4", [P, DEPTH * NC_LRU])
        sp2 = sb("sp2", [P, DEPTH * NC_LRU])
        cEPS = sb("cEPS", [P, 1])
        ssq = sb("ssq", [P, NT])
        rstd = sb("rstd", [P, NT])

        idx8 = sb("idx8", [P, NT, 8], U32)
        jobi = sb("jobi", [P, JOBS + 2], I32)

        arena_scope = ExitStack()
        arena = arena_scope.enter_context(nc.sbuf_tensor("arena", [P, ARENA], F32))
        at = [0]

        def mix(n, *dims):
            v = arena[:, at[0]:at[0] + n]
            at[0] += n
            assert at[0] <= ARENA
            if len(dims) == 2:
                v = v.rearrange("p (a b) -> p a b", a=dims[0])
            if len(dims) == 3:
                v = v.rearrange("p (a b c) -> p a b c", a=dims[0], b=dims[1])
            return v

        tok = mix(NT * 1304, NT, 1304)
        qn = mix(NT * 512, NT, HPG, P)
        kn = mix(NT * 256, NT, 2, P)
        sq = mix(NT * 1280, NT, 1280)
        qT = mix(HPG * SEQ, HPG, SEQ)
        kT = mix(2 * SEQ, 2, SEQ)
        kcv2 = mix(2 * NG * P, 2, NG, P)
        blk = mix(2 * L2 * NG * N_CMP, 2, L2 * NG * N_CMP)
        xpad = mix(NC_LRU * (SEQ + 4), NC_LRU, SEQ + 4)
        gT = mix(NC_LRU * SEQ, NC_LRU, SEQ)
        xc = mix(NC_LRU * SEQ, NC_LRU, SEQ)
        rr = arena[:, NT * 1304 + NT * 768:][:, 0:NC_LRU * SEQ].rearrange("p (a b) -> p a b", a=NC_LRU)
        ii = arena[:, NT * 1304 + NT * 768 + 1024:][:, 0:NC_LRU * SEQ].rearrange("p (a b) -> p a b", a=NC_LRU)
        aa = mix(NC_LRU * SEQ, NC_LRU, SEQ)
        tt = mix(NC_LRU * SEQ, NC_LRU, SEQ)
        sS = xn[:, 0, :].rearrange("p (b c) -> p b c", b=2)
        sP = xn[:, 1, :].rearrange("p (b c) -> p b c", b=2)
        skew = arena[:, at[0] - 2 * NC_LRU * SEQ:at[0]]
        sT = mix(2 * 512, 2, 512)
        cS = mix(NT * NH * 16, NT, NH, 16)
        small = mix(896)
        oS = arena[:, 0:NT * 512].rearrange("p (a b) -> p a b", a=NT)
        mixT = hT
        rms20 = small[:, 0:40].rearrange("p (a b) -> p a b", a=NT)
        gsig = small[:, 40:88].rearrange("p (a b) -> p a b", a=NT)
        hc = small[:, 88:148]
        hc2 = small[:, 148:208]
        hct = small[:, 208:268]
        kcn = small[0:NG * N_CMP, 268:396]
        kcsq = small[0:NG * N_CMP, 396:460]
        kcs = small[0:NG * N_CMP, 460:461]
        kcT = small[:, 462:492]
        vcs = small[0:N_CMP, 492:620]
        mx = small[:, 620:652]
        den = small[:, 652:684]
        cmx = small[:, 684:700]
        cden = small[:, 700:716]
        nrm = small[:, 716:724]
        cPT = hT[0:N_CMP].rearrange("p k (a q) -> p (k a) q", a=2)

        arena_scope.close()
        ehid = sb("ehid", [P, HALF * FN])
        esil = sb("esil", [P, 2, FN])
        ehidTh = sb("ehidTh", [P, FT, P], F32R)
        ehidTl = sb("ehidTl", [P, FT, P], F32R)
        xgh = sb("xgh", [P, KD, P], F32R)
        xgl = sb("xgl", [P, KD, P], F32R)
        wh = sb("wh", [P, USLOTS, UNIT], F32R)
        wl = sb("wl", [P, USLOTS, UNIT], F32R)
        ye = ehid[:, 0:D]
        selM = sb("selM", [P, NT, P])
        selW = sb("selW", [P, NT, P])
        selT = sb("selT", [P, NT, P])
        rt = sb("rt", [P, 280])
        dxh = ehidTh.rearrange("p a b -> p (a b)")[:, 0:KD * SEQ].rearrange("p (k t) -> p k t", k=KD)
        dxl = ehidTl.rearrange("p a b -> p (a b)")[:, 0:KD * SEQ].rearrange("p (k t) -> p k t", k=KD)
        dhh = xgh.rearrange("p a b -> p (a b)").rearrange("p (i t) -> p i t", i=4)
        dhl = xgl.rearrange("p a b -> p (a b)").rearrange("p (i t) -> p i t", i=4)
        logit = rt[:, 0:16].rearrange("p (a b) -> p a b", a=NT)
        top8 = rt[:, 16:32].rearrange("p (a b) -> p a b", a=NT)
        idxf = rt[:, 32:48].rearrange("p (a b) -> p a b", a=NT)
        oh1 = rt[:, 48:64].rearrange("p (a b) -> p a b", a=NT)
        oh2 = rt[:, 64:80].rearrange("p (a b) -> p a b", a=NT)
        memb = rt[:, 80:96].rearrange("p (a b) -> p a b", a=NT)
        wexp = rt[:, 96:112].rearrange("p (a b) -> p a b", a=NT)
        pos = rt[:, 112:128].rearrange("p (a b) -> p a b", a=NT)
        wt = rt[:, 128:136]
        over = rt[:, 136:144]
        rank = rt[:, 144:152]
        pick = rt[:, 152:160]
        junk = rt[:, 160:176].rearrange("p (a b) -> p a b", a=NT)
        table = rt[:, 176:176 + 6 * (JOBS + 1)].rearrange("p (j c) -> p j c", c=6)
        job = rt[:, 250:256]
        jobf = rt[:, 256:256 + JOBS + 1]

        bank = [ctx.enter_context(nc.psum_tensor(f"bank{i}", [P, 512], F32)) for i in range(8)]

        urows_dram = nc.dram_tensor("urows", (NH, U_LEN), F32, kind="Internal").ap()

        names = """small_loaded params_loaded relb_loaded rows_stored skew_loaded flip_done bias_ready lru_w_loaded out_stored
            x_loaded consts_set params_transposed params_ready urow_done urow_ready
            root_done norm_ready normT_done hT_act hT_dve q_done kc_done kv_done gates_done lrux_done lrug_done
            tok_act tok_dve lrux_ready gate_ready
            qk_root_in qk_root qk_ready T_done qT_ready kT_ready kcv_ready blk_ready cmph_done gelu_c_in gelu_c_th gelu_c_ready
            kc_done2 vc_ready kcn_in kcn_root kcn_ready kcT_done kcT_ready
            conv_ready rgate_done igate_done rtanh_ready itanh_ready decay_ready sqrt_t mult_ready scan_ready
            gelu_in gelu_th ysq_ready ymix_ready
            gs_in gs_exp cs_done cs_in cs_exp cp_ready cpT_done cpT_ready
            s_done s_ready e_ready p_ready pT_done pT_ready o_done o_ready oT_done oT_ready lsum_done mroot_in mroot 
            out_done x_mixed
            dx_high dx_ready dwh_ready dwl_ready dunit_used dhid_high dhid_rest xg_done xg_high xg_ready wh_ready wl_ready unit_used hidT_high ye_act silu_ready hid_ready hidT_done hidT_ready y_ready comb_done comb_ready sel_ready selT_done selT_ready
            log_done job_ready texp_in texp pos_in pos_done jobs_ready ffn_done
            act_chain dve_chain pool_chain""".split()
        S = {n: sem(n) for n in names}
        loaded = [sem(f"slot{i}_loaded") for i in range(SLOTS)]
        half_loaded = [sem(f"half{i}_loaded") for i in range(HALVES)]

        def piece_at(p):
            return ring[:, p % SLOTS, :]

        def ring3(p, a, b):
            return piece_at(p)[:, 0:a * b].rearrange("p (a b) -> p a b", a=a)

        def wait_piece(eng, p):
            eng.wait_ge(loaded[p % SLOTS], sum(48 if MIX_PIECES <= q < MIX_PIECES + FFN_PIECES else 16
                                               for q in range(p % SLOTS, p + 1, SLOTS)))

        def dense_parts(g):
            v = piece_at(MIX_PIECES + g)
            return [v[:, i * 2 * D:(i + 1) * 2 * D].rearrange("p (k n) -> p k n", k=k) for i, k in enumerate((KD, KD, 2))]

        def dense_source(g, u):
            part = dense_parts(g)[u // 2]
            return part[:, 4 * (u % 2):4 * (u % 2) + 4, :] if u < 4 else part[:, u - 4:u - 3, :]

        def dense_in(w, n):
            return w[:, n % USLOTS, 0:D].rearrange("p (k n) -> p k n", k=4 if DUNITS[n][1] < 4 else 1)

        def expert_half(i):
            return (2 * ROUTED0 + i) % HALVES

        def expert_piece(i):
            h = expert_half(i)
            v = ring[:, h // 2, h % 2 * HALF_SLOT:(h % 2 + 1) * HALF_SLOT]
            k, n = (KD, FN) if i < 2 * FCH else (EDOWN[i - 2 * FCH], D)
            return v[:, 0:k * n].rearrange("p (k n) -> p k n", k=k)

        def last_unit(i):
            return 2 * i + 1 if i < 2 * FCH else 4 * FCH + sum(EDOWN[:i - 2 * FCH + 1]) - 1

        def first_piece(u):
            if u < 4 * FCH:
                return u // 2 if u % 2 == 0 else None
            starts = [4 * FCH + sum(EDOWN[:c]) for c in range(len(EDOWN))]
            return 2 * FCH + starts.index(u) if u in starts else None

        def unit_source(u):
            if u < 4 * FCH:
                return expert_piece(u // 2)[:, 4 * (u % 2):4 * (u % 2) + 4, :]
            i, c = u - 4 * FCH, 0
            while i >= EDOWN[c]:
                i, c = i - EDOWN[c], c + 1
            return expert_piece(2 * FCH + c)[:, i:i + 1, :]

        def unit_in(w, u):
            if u < 4 * FCH:
                return w[:, u % USLOTS, :].rearrange("p (k n) -> p k n", k=4)
            return w[:, u % USLOTS, 0:D].rearrange("p (k n) -> p k n", k=1)

        def wait_job_piece(eng, j, i):
            eng.wait_ge(half_loaded[expert_half(i)], j * (16 * EXPERT_PIECES // HALVES) + 16 * (i // HALVES + 1))

        block = ctx.enter_context(nc.Block())

        @block.sync
        def _(sp):
            sp.dma_start(xs[:, :, :], x[0].rearrange("(t p) d -> p t d", p=P)).then_inc(S["x_loaded"], 16)

            def freed(p):
                l, i = divmod(p, MIX_PIECES + FFN_PIECES)
                if i < MIX_PIECES:
                    return [("kc_done", l + 1), ("gates_done", 2 * l + 2), ("lrux_done", 2 * l + 2), ("lrug_done", 2 * l + 2),
                            ("cmph_done", l + 1), ("out_done", 8 * l + 4), ("out_done", 8 * l + 8)][i]
                i -= MIX_PIECES
                return ("dwl_ready", DUNITS.index((i, 5)) + 1)

            def load(p, dst, src):
                if p >= SLOTS:
                    name, count = freed(p - SLOTS)
                    sp.wait_ge(S[name], count)
                sp.dma_start(dst, src).then_inc(loaded[p % SLOTS], 16)

            def load_mix(l, p):
                wi = w_in[l].rearrange("(k p) n -> p k n", p=P)
                load(p, ring3(p, KD, 768), wi[:, :, OFF_Q:OFF_Q + 768])
                load(p + 1, ring3(p + 1, KD, W_B), wi[:, :, OFF_Q + 768:D_IN])
                load(p + 2, ring3(p + 2, KD, 512), wi[:, :, 0:D_LRU])
                load(p + 3, ring3(p + 3, KD, 512), wi[:, :, D_LRU:2 * D_LRU])
                load(p + 4, ring3(p + 4, 2 * L2, P), cmp_w1[l].rearrange("v (m e) d c -> (e d) (v m) c", e=2))
                wo = w_out[l].rearrange("(k p) n -> p k n", p=P)
                load(p + 5, ring3(p + 5, 4, D), wo[:, 0:4, :])
                load(p + 6, ring3(p + 6, 4, D), wo[:, 4:8, :])

            sp.wait_ge(S["params_loaded"], 16 * 13)
            load_mix(0, 0)
            for g in range(FFN_PIECES):
                name, count = freed(MIX_PIECES + g - SLOTS)
                sp.wait_ge(S[name], count)
                srcs = [w[0].rearrange("(k p) n -> p k n", p=P)[:, :, 2 * g * P:2 * (g + 1) * P] for w in (ffn_w_gate, ffn_w_up)]
                srcs.append(ffn_w_down[0].rearrange("(t p) n -> p t n", p=P)[:, 2 * g:2 * g + 2, :])
                for dst, src in zip(dense_parts(g), srcs):
                    sp.dma_start(dst, src).then_inc(loaded[(MIX_PIECES + g) % SLOTS], 16)
            load_mix(1, MIX_PIECES + FFN_PIECES)
            def expert_source(i, wg, wu, wd):
                if i < 2 * FCH:
                    return (wg, wu)[i % 2].rearrange("(k p) n -> p k n", p=P)[:, :, i // 2 * FN:(i // 2 + 1) * FN]
                c = i - 2 * FCH
                t = sum(EDOWN[:c])
                return wd.rearrange("(t p) n -> p t n", p=P)[:, t:t + EDOWN[c], :]

            for i in range(HALVES):
                if i % 2 == 0:
                    name, count = freed(ROUTED0 + i // 2 - SLOTS)
                    sp.wait_ge(S[name], count)
                sp.dma_start(expert_piece(i), expert_source(i, moe_w_gate[0, 0], moe_w_up[0, 0], moe_w_down[0, 0]))\
                    .then_inc(half_loaded[expert_half(i)], 16)
            sp.wait_ge(S["jobs_ready"], 1)
            njobs = sp.value_load(jobi[0:1, 0:1], min_val=NE, max_val=JOBS)
            def weights_of(j):
                e = sp.value_load(jobi[0:1, bass.ds(j + 1, 1)], min_val=0, max_val=NE - 1)
                first = sp.snap(e * (D * D_FF))
                row_reg = sp.to_reg(first + D)
                row = sp.snap(row_reg, min_val=D, max_val=(NE - 1) * D * D_FF + D)
                return [bass.AP(m.tensor, o, [[n, r], [1, n]]) for m, o, r, n in
                        ((moe_w_gate, row - D, D, D_FF), (moe_w_up, row - D, D, D_FF), (moe_w_down, row - D, D_FF, D))]

            def load_job(j, i, w, k):
                sp.wait_ge(S["wl_ready"], j * UNITS + (last_unit(k) + 1))
                sp.dma_start(expert_piece(i), expert_source(i, *w)).then_inc(half_loaded[expert_half(i)], 16)

            with sp.Fori(0, njobs) as j:
                w = weights_of(j)
                for i in range(HALVES, EXPERT_PIECES):
                    load_job(j, i, w, i - HALVES)
                with sp.If(j + 1 < njobs):
                    w = weights_of(j + 1)
                    for i in range(HALVES):
                        load_job(j, i, w, EXPERT_PIECES - HALVES + i)
            sp.wait_ge(S["comb_ready"], njobs * 4)
            sp.dma_start(out[0].rearrange("(t p) d -> p t d", p=P), xs[:, :, :]).then_inc(S["out_stored"], 16)
            sp.wait_ge(S["out_stored"], 16)

        @block.gpsimd
        def _(pool):
            chain = [0]

            def link(ins):
                chain[0] += 1
                ins.then_inc(S["pool_chain"], 1)
                pool.wait_ge(S["pool_chain"], chain[0])

            link(pool.memset(relb[:, :], NEG))
            pool.dma_start(relb[0:N_BUCKETS, :], rel_bias).then_inc(S["relb_loaded"], 16)
            pool.dma_start(bucketT[:, :], bucket_rows).then_inc(S["relb_loaded"], 16)
            link(pool.memset(ident[:, :], 0.0))
            link(pool.affine_select(out=ident[:, :], in_=ident[:, :], compare_op=ALU.not_equal, fill=1.0, base=0,
                                    pattern=[[-1, P]], channel_multiplier=1))
            link(pool.memset(flip[:, :], 0.0))
            link(pool.affine_select(out=flip[:, :], in_=flip[:, :], compare_op=ALU.not_equal, fill=1.0, base=1 - P,
                                    pattern=[[1, P]], channel_multiplier=1))
            link(pool.memset(ones[:, :], 1.0))
            link(pool.affine_select(out=before[:, :], in_=ones[:, :], compare_op=ALU.is_gt, fill=0.0, base=0,
                                    pattern=[[1, P]], channel_multiplier=-1))
            link(pool.iota(slot_id[:, :], pattern=[[1, P]], base=0, channel_multiplier=0,
                           allow_small_or_imprecise_dtypes=True))
            link(pool.memset(cEPS[:, :], EPS))
            pool.memset(lruW[:, :, :, :], 0.0).then_inc(S["consts_set"], 1)
            pool.wait_ge(S["consts_set"], 1)
            pool.wait_ge(S["urow_ready"], 1)
            pool.dma_start(urows_dram, urow[:, :]).then_inc(S["rows_stored"], 16)
            pool.wait_ge(S["rows_stored"], 16)
            pool.dma_start(skew.rearrange("p (h i) -> p h i", h=NH), bass.AP(urows_dram.tensor, 0, [[1, P], [U_LEN, NH], [1, 2 * P]]))\
                .then_inc(S["skew_loaded"], 16)

            for l in range(DEPTH):
                L = l + 1
                if l > 0:
                    pool.wait_ge(S["igate_done"], l)
                for e in range(2):
                    for w, src in enumerate((lru_wa, lru_wx)):
                        pool.dma_start(lruW[e * HD:(e + 1) * HD, w, :, e * HD:(e + 1) * HD],
                                       src[l].rearrange("(m e) i j -> e i m j", e=2)[e]).then_inc(S["lru_w_loaded"], 16)
                pool.wait_ge(S["gate_ready"], L)
                link(pool.tensor_tensor(tt, gT, gT, ALU.mult))
                link(pool.tensor_scalar(tt, tt, 0.044715, 1.0, ALU.mult, ALU.add))
                pool.tensor_tensor(tt, tt, gT, ALU.mult).then_inc(S["gelu_in"], 1)
                pool.wait_ge(S["gelu_th"], L)
                link(pool.tensor_scalar(tt, tt, 1.0, 0.5, ALU.add, ALU.mult))
                link(pool.tensor_tensor(gT, gT, tt, ALU.mult))
                pool.wait_ge(S["itanh_ready"], L)
                link(pool.tensor_scalar(ii, ii, 1.0, 0.5, ALU.add, ALU.mult))
                link(pool.tensor_tensor(ii, ii, xc, ALU.mult))
                pool.wait_ge(S["decay_ready"], L)
                link(pool.tensor_scalar(tt, aa, 1.0, None, ALU.add))
                link(pool.tensor_tensor(ii, ii, tt, ALU.mult))
                pool.wait_ge(S["sqrt_t"], L)
                pool.tensor_tensor(ii, ii, rr, ALU.mult).then_inc(S["mult_ready"], 1)
                pool.wait_ge(S["scan_ready"], L)
                link(pool.tensor_tensor(xc, gT, tt, ALU.mult))
                pool.tensor_tensor(tt, xc, xc, ALU.mult).then_inc(S["ysq_ready"], 1)

        @block.scalar
        def _(act):
            chain = [0]

            def link(ins):
                chain[0] += 1
                ins.then_inc(S["act_chain"], 1)
                act.wait_ge(S["act_chain"], chain[0])

            def norm_root(n):
                if n == 0:
                    act.wait_ge(S["x_loaded"], 16)
                    act.wait_ge(S["consts_set"], 1)
                for t in range(NT):
                    if n % 2 == 1:
                        act.wait_ge(S["x_mixed"], NT * (n // 2) + t + 1)
                    elif n > 0:
                        act.wait_ge(S["ffn_done"], t + 1)
                    link(act.activation(xn[:, t, :], xs[:, t, :], ACT.Square, accum_out=ssq[:, t:t + 1]))
                act.activation(rstd[:, :], ssq[:, :], ACT.Sqrt, scale=1.0 / D, bias=cEPS[:, :]).then_inc(S["root_done"], 1)

            def norm_turned(n, row):
                for k in range(4):
                    act.wait_ge(S["normT_done"], 4 * n + k // 2 + 1)
                    act.activation(hT[:, k, :], bank[k // 2][:, (k % 2) * SEQ:(k % 2 + 1) * SEQ], ACT.Copy,
                                   scale=par[:, row + k:row + k + 1]).then_inc(S["hT_act"], 1)

            rows = [(R_G1, norm1_g.rearrange("l (k p) -> (l k) p", p=P)), (R_G2, norm2_g.rearrange("l (k p) -> (l k) p", p=P)),
                    (R_OG, out_norm_g.rearrange("l (k p) -> (l k) p", p=P)),
                    (R_CW, conv_w.rearrange("l w (k p) -> (l w k) p", p=P)), (R_CB, conv_b.rearrange("l (k p) -> (l k) p", p=P)),
                    (R_BA, lru_ba.rearrange("l (k p) -> (l k) p", p=P)), (R_BX, lru_bx.rearrange("l (k p) -> (l k) p", p=P)),
                    (R_LAM, lru_lambda.rearrange("l (k p) -> (l k) p", p=P))]
            for r, src in rows:
                act.dma_start(prow[r:r + src.shape[0], :], src).then_inc(S["params_loaded"], 16)
            for half in range(2):
                act.dma_start(prow[R_QG:R_QG + 2, half * HD:(half + 1) * HD], q_norm_g).then_inc(S["params_loaded"], 16)
                act.dma_start(prow[R_KG:R_KG + 2, half * HD:(half + 1) * HD], k_norm_g).then_inc(S["params_loaded"], 16)
            act.dma_start(posr[:, :], cmp_pos.rearrange("l v (m e) d -> (l v m) (e d)", e=2)).then_inc(S["params_loaded"], 16)
            act.dma_start(gateb[:, :, :], gate_b.partition_broadcast(P)).then_inc(S["small_loaded"], 16)
            act.dma_start(w2[:, :, :, :], cmp_w2.rearrange("l v c d -> c l v d")).then_inc(S["small_loaded"], 16)
            act.dma_start(rw[:, :, :], router_w[0].rearrange("(k p) e -> p k e", p=P)).then_inc(S["small_loaded"], 16)
            norm_root(0)
            act.wait_ge(S["params_transposed"], 1)
            act.activation(par[:, :], bank[0][:, 0:N_ROWS], ACT.Copy).then_inc(S["params_ready"], 1)
            act.activation(posT[:, :], bank[0][:, 128:128 + HD], ACT.Copy).then_inc(S["params_ready"], 1)
            act.wait_ge(S["urow_done"], 1)
            act.activation(urow[:, :], bank[1][0:NH, 0:U_LEN], ACT.Copy).then_inc(S["urow_ready"], 1)
            act.wait_ge(S["params_ready"], 2)
            for w, r in ((0, R_BA), (1, R_BX)):
                link(act.activation(hba[:, w, :], par[:, r:r + 8], ACT.Copy, scale=0.5))
            link(act.activation(sp2[:, :], par[:, R_LAM:R_LAM + 8], ACT.Exp, scale=-1.0))
            link(act.activation(sp2[:, :], sp2[:, :], ACT.Ln, bias=1.0))
            link(act.activation(nsp4[:, :], sp2[:, :], ACT.Copy, scale=-4.0))
            link(act.activation(sp2[:, :], sp2[:, :], ACT.Copy, scale=2.0))

            for l in range(DEPTH):
                L = l + 1
                if l > 0:
                    norm_root(2 * l)
                norm_turned(2 * l, R_G1 + 8 * l)
                act.wait_ge(S["q_done"], 2 * l + 1)
                act.activation(tok[:, 0, 0:512], bank[4][:, :], ACT.Copy).then_inc(S["tok_act"], 1)
                act.wait_ge(S["kv_done"], 2 * l + 1)
                act.activation(tok[:, 0, 768:1280], bank[0][:, :], ACT.Copy).then_inc(S["tok_act"], 1)
                act.wait_ge(S["gates_done"], 2 * l + 1)
                act.activation(tok[:, 0, 512:768], bank[6][:, 0:256], ACT.Copy).then_inc(S["tok_act"], 1)
                act.activation(tok[:, 0, 1280:1304], bank[6][:, 256:280], ACT.Copy).then_inc(S["tok_act"], 1)
                if l == 0:
                    for c in range(4):
                        act.wait_ge(S["flip_done"], c + 1)
                        act.activation(biasU[:, 2 * c:2 * c + 2, :], bank[2 + c][:, :].rearrange("p (a b) -> p a b", a=2), ACT.Copy)\
                            .then_inc(S["bias_ready"], 1)
                for m in range(NC_LRU):
                    act.wait_ge(S["lrux_done"], 2 * l + m // 2 + 1)
                    act.activation(xpad[:, m, 3:3 + SEQ], bank[2 + m // 2][:, (m % 2) * SEQ:(m % 2 + 1) * SEQ], ACT.Copy)\
                        .then_inc(S["lrux_ready"], 1)
                act.wait_ge(S["qk_root_in"], L)
                act.activation(rms20, rms20, ACT.Sqrt, scale=1.0 / HD, bias=cEPS[:, :]).then_inc(S["qk_root"], 1)
                for m in range(2):
                    act.wait_ge(S["lrug_done"], 2 * l + m + 1)
                    last = act.activation(gT[:, 2 * m:2 * m + 2, :], bank[4 + m][:, :].rearrange("p (a b) -> p a b", a=2), ACT.Copy)
                    if m == 0:
                        link(last)
                    else:
                        last.then_inc(S["gate_ready"], 1)
                for b in range(2):
                    act.wait_ge(S["T_done"], 4 * l + b + 1)
                    act.activation(qT[:, 2 * b:2 * b + 2, :], bank[6 + b][:, :].rearrange("p (a b) -> p a b", a=2), ACT.Copy,
                                   scale=par[:, R_QG + l:R_QG + l + 1]).then_inc(S["qT_ready"], 1)
                act.wait_ge(S["gs_in"], L)
                act.activation(gsig, gsig, ACT.Exp, scale=-1.0).then_inc(S["gs_exp"], 1)
                act.wait_ge(S["gelu_in"], L)
                act.activation(tt, tt, ACT.Tanh, scale=0.7978845608028654).then_inc(S["gelu_th"], 1)
                act.wait_ge(S["gelu_c_in"], L)
                act.activation(hct, hc2, ACT.Tanh, scale=0.7978845608028654).then_inc(S["gelu_c_th"], 1)
                for w, (done, dst, ready, b0) in enumerate((("rgate_done", rr, "rtanh_ready", 4), ("igate_done", ii, "itanh_ready", 0))):
                    act.wait_ge(S[done], L)
                    for m in range(NC_LRU):
                        last = act.activation(dst[:, m, :], bank[b0 + m // 2][:, (m % 2) * SEQ:(m % 2 + 1) * SEQ], ACT.Tanh,
                                              scale=0.5, bias=hba[:, w, l * NC_LRU + m:l * NC_LRU + m + 1])
                        if m < NC_LRU - 1:
                            link(last)
                    last.then_inc(S[ready], 1)
                act.wait_ge(S["kcn_in"], L)
                act.activation(kcs, kcs, ACT.Sqrt, scale=1.0 / HD, bias=cEPS[0:NG * N_CMP, :]).then_inc(S["kcn_root"], 1)
                act.wait_ge(S["rtanh_ready"], L)
                for m in range(NC_LRU):
                    c = l * NC_LRU + m
                    last = act.activation(aa[:, m, :], rr[:, m, :], ACT.Exp, scale=nsp4[:, c:c + 1], bias=nsp4[:, c:c + 1])
                    if m < NC_LRU - 1:
                        link(last)
                last.then_inc(S["decay_ready"], 1)
                act.wait_ge(S["decay_ready"], L)
                for m in range(NC_LRU):
                    c = l * NC_LRU + m
                    link(act.activation(rr[:, m, :], rr[:, m, :], ACT.Tanh, scale=sp2[:, c:c + 1], bias=sp2[:, c:c + 1]))
                act.activation(rr, rr, ACT.Sqrt).then_inc(S["sqrt_t"], 1)
                act.wait_ge(S["cs_in"], L)
                act.activation(cS, cS, ACT.Exp).then_inc(S["cs_exp"], 1)
                for c in range(4):
                    act.wait_ge(S["cpT_done"], 4 * l + c + 1)
                    act.activation(cPT[:, 4 * c:4 * c + 4, :], bank[c % 2][0:N_CMP, :].rearrange("p (a b) -> p a b", a=4), ACT.Copy)\
                        .then_inc(S["cpT_ready"], 1)
                for i in range(NT * NH + 1):
                    if i < NT * NH:
                        W = P * (i // NH + 1)
                        n = NT * NH * l + i
                        act.wait_ge(S["s_ready"], n + 1)
                        if i >= 2:
                            act.wait_ge(S["pT_done"], n - 1)
                        for b in range(2):
                            last = act.activation(sP[:, i % 2, b * W:(b + 1) * W], sS[:, i % 2, b * W:(b + 1) * W], ACT.Exp,
                                                  bias=mx[:, 16 * (i % 2) + b:16 * (i % 2) + b + 1],
                                                  accum_out=den[:, 16 * (i % 2) + b:16 * (i % 2) + b + 1])
                            if b == 0:
                                link(last)
                        last.then_inc(S["e_ready"], 1)
                    if i >= 1:
                        k = i - 1
                        n = NT * NH * l + k
                        W = P * (k // NH + 1)
                        act.wait_ge(S["pT_done"], n + 1)
                        if k >= 2:
                            act.wait_ge(S["o_done"], n - 1)
                        act.activation(sT[:, k % 2, 0:2 * W], bank[2 + k % 2][:, 0:2 * W], ACT.Copy).then_inc(S["pT_ready"], 1)
                for t in range(NT):
                    act.wait_ge(S["o_done"], NT * NH * l + NH * (t + 1))
                    link(act.activation(oS[:, t, :], bank[4 + t][:, :], ACT.Copy))
                    act.activation(sS[:, 0, :], oS[:, t, :], ACT.Square, accum_out=nrm[:, t:t + 1]).then_inc(S["o_ready"], 1)
                act.wait_ge(S["lsum_done"], L)
                act.activation(nrm[:, 2:4], bank[1][:, 0:2], ACT.Copy).then_inc(S["mroot_in"], 1)
                act.wait_ge(S["mroot_in"], L)
                act.wait_ge(S["o_ready"], 2 * L)
                act.activation(nrm[:, 4:8], nrm[:, 0:4], ACT.Sqrt, scale=1.0 / D_LRU, bias=cEPS[:, :]).then_inc(S["mroot"], 1)
                act.wait_ge(S["ysq_ready"], L)
                for m in range(NC_LRU):
                    act.activation(mixT[:, m, :], xc[:, m, :], ACT.Copy,
                                   scale=par[:, R_OG + 8 * l + m:R_OG + 8 * l + m + 1]).then_inc(S["ymix_ready"], 1)
                for m in range(4):
                    act.wait_ge(S["oT_done"], 2 * l + m // 2 + 1)
                    act.activation(mixT[:, 4 + m, :], bank[6 + m // 2][:, (m % 2) * SEQ:(m % 2 + 1) * SEQ], ACT.Copy,
                                   scale=par[:, R_OG + 8 * l + 4 + m:R_OG + 8 * l + 5 + m]).then_inc(S["oT_ready"], 1)
                norm_root(2 * l + 1)
                if l > 0:
                    norm_turned(2 * l + 1, R_G2 + 8 * l)
                if l == 0:
                    def dense_high(n):
                        g, u = DUNITS[n]
                        if u == 0:
                            wait_piece(act, MIX_PIECES + g)
                        if n >= USLOTS:
                            act.wait_ge(S["dunit_used"], n - USLOTS + 1)
                        act.activation(dense_in(wh, n), dense_source(g, u), ACT.Copy).then_inc(S["dwh_ready"], 1)

                    for n in range(USLOTS):
                        dense_high(n)
                    for k in range(KD):
                        act.wait_ge(S["normT_done"], 4 + k // 2 + 1)
                        act.activation(dxh[:, k, :], bank[k // 2][:, (k % 2) * SEQ:(k % 2 + 1) * SEQ], ACT.Copy,
                                       scale=par[:, R_G2 + k:R_G2 + k + 1]).then_inc(S["dx_high"], 1)
                    for n in range(USLOTS, len(DUNITS)):
                        g, u = DUNITS[n]
                        last_piece = (g, u) == (FFN_PIECES - 1, 4)
                        done = g - 1 if u < 4 else g
                        if done >= 0 and (u == 1 or last_piece):
                            act.wait_ge(S["dunit_used"], DUNITS.index((done, 3)) + 1)
                            for r in range(2):
                                act.activation(esil[:, r, 0:SEQ], bank[(2 * done + r) % 4][:, 0:SEQ], ACT.Silu)\
                                   .then_inc(S["silu_ready"], 1)
                        if done >= 0 and (u == 2 or last_piece):
                            for i in (2 * done, 2 * done + 1):
                                act.wait_ge(S["hid_ready"], i + 1)
                                act.activation(dhh[:, i % 4, :], ehid[:, i % 2 * SEQ:(i % 2 + 1) * SEQ], ACT.Copy)\
                                   .then_inc(S["dhid_high"], 1)
                        dense_high(n)
                else:
                    act.wait_ge(S["texp_in"], 1)
                    act.activation(wt[:, 0:2], wt[:, 0:2], ACT.Exp).then_inc(S["texp"], 1)

                    def high(j, u, first=False):
                        if first_piece(u) is not None:
                            wait_job_piece(act, j, first_piece(u))
                        if not first:
                            act.wait_ge(S["unit_used"], j * UNITS + (u - USLOTS + 1))
                        act.activation(unit_in(wh, u), unit_source(u), ACT.Copy).then_inc(S["wh_ready"], 1)

                    def tokens_high(j):
                        for c in range(2):
                            act.wait_ge(S["xg_done"], 2 * j + (c + 1))
                            for k in range(4 * c, 4 * c + 4):
                                act.activation(xgh[:, k, :], bank[4 + c][:, (k % 4) * P:(k % 4 + 1) * P], ACT.Copy,
                                               scale=par[:, R_G2 + 8 + k:R_G2 + 9 + k]).then_inc(S["xg_high"], 1)

                    def turned_high(j, k):
                        a, b = done_tiles(k), done_tiles(k + 1)
                        act.wait_ge(S["hidT_done"], j * FCH + (k + 1))
                        act.activation(ehidTh[:, a:b, :], bank[4 + k % 2][:, 0:(b - a) * P].rearrange("p (a b) -> p a b", b=P),
                                       ACT.Copy).then_inc(S["hidT_high"], 1)

                    high(0, 0, True)
                    high(0, 1, True)
                    tokens_high(0)
                    high(0, 2, True)
                    act.wait_ge(S["jobs_ready"], 1)
                    njobs = act.value_load(jobi[0:1, 0:1], min_val=NE, max_val=JOBS)
                    with act.Fori(0, njobs) as j:
                        for u in range(USLOTS, UNITS):
                            q = (u - 6) // 4
                            if u % 4 == 2 and u >= 6 and q < FCH:
                                act.wait_ge(S["unit_used"], j * UNITS + (4 * q + 4))
                                act.wait_ge(S["hid_ready"], j * FCH + (FT + q - 1))
                                act.activation(esil[:, q % 2, :], bank[2 * (q % 2)][:, 0:FN], ACT.Silu).then_inc(S["silu_ready"], 1)
                                if q >= 1:
                                    turned_high(j, q - 1)
                            if u == 4 * FCH + 5:
                                turned_high(j, FCH - 1)
                            high(j, u)
                        act.wait_ge(S["unit_used"], j * UNITS + UNITS)
                        act.activation(ye[:, 512:1024], bank[7][:, :], ACT.Copy).then_inc(S["ye_act"], 1)
                        with act.If(j + 1 < njobs):
                            high(j + 1, 0)
                            high(j + 1, 1)
                            tokens_high(j + 1)
                            high(j + 1, 2)

        @block.vector
        def _(dve):
            chain = [0]

            def link(ins):
                chain[0] += 1
                ins.then_inc(S["dve_chain"], 1)
                dve.wait_ge(S["dve_chain"], chain[0])

            def norm(n, row):
                dve.wait_ge(S["root_done"], n + 1)
                link(dve.reciprocal(rstd[:, :], rstd[:, :]))
                for t in range(NT):
                    dve.tensor_scalar(xn[:, t, :], xs[:, t, :], rstd[:, t:t + 1], None, ALU.mult).then_inc(S["norm_ready"], 1)
                if n == 0:
                    dve.wait_ge(S["params_ready"], 2)
                if n == 1:
                    for k in range(KD):
                        dve.wait_ge(S["dx_high"], 2 * (k // 2 + 1))
                        dve.scalar_tensor_tensor(dxl[:, k, :], bank[k // 2][:, (k % 2) * SEQ:(k % 2 + 1) * SEQ],
                                                 par[:, row + k:row + k + 1], dxh[:, k, :].bitcast(F32),
                                                 ALU.mult, ALU.subtract).then_inc(S["dx_ready"], 1)
                    return
                for k in range(4, 8):
                    dve.wait_ge(S["normT_done"], 4 * n + k // 2 + 1)
                    dve.tensor_scalar(hT[:, k, :], bank[k // 2][:, (k % 2) * SEQ:(k % 2 + 1) * SEQ],
                                      par[:, row + k:row + k + 1], None, ALU.mult).then_inc(S["hT_dve"], 1)

            for l in range(DEPTH):
                L = l + 1
                norm(2 * l, R_G1 + 8 * l)
                link(dve.memset(xpad[:, :, 0:3], 0.0))
                dve.wait_ge(S["q_done"], 2 * l + 2)
                dve.tensor_copy(tok[:, 1, 0:512], bank[5][:, :]).then_inc(S["tok_dve"], 1)
                dve.wait_ge(S["kv_done"], 2 * l + 2)
                dve.tensor_copy(tok[:, 1, 768:1280], bank[1][:, :]).then_inc(S["tok_dve"], 1)
                dve.wait_ge(S["gates_done"], 2 * l + 2)
                dve.tensor_copy(tok[:, 1, 512:768], bank[7][:, 0:256]).then_inc(S["tok_dve"], 1)
                dve.tensor_copy(tok[:, 1, 1280:1304], bank[7][:, 256:280]).then_inc(S["tok_dve"], 1)
                dve.wait_ge(S["tok_dve"], 4 * L)
                dve.wait_ge(S["tok_act"], 4 * L)
                for t in range(NT):
                    link(dve.tensor_tensor(sq[:, t, :], tok[:, t, 0:1280], tok[:, t, 0:1280], ALU.mult))
                for t in range(NT):
                    last = dve.tensor_reduce(rms20[:, t, :], sq[:, t, :].rearrange("p (a b) -> p a b", b=HD), AX, ALU.add)
                    if t == 0:
                        link(last)
                last.then_inc(S["qk_root_in"], 1)
                dve.wait_ge(S["qk_root"], L)
                link(dve.reciprocal(rms20, rms20))
                for t in range(NT):
                    link(dve.tensor_tensor(qn[:, t].rearrange("p h (g d) -> p h g d", g=NG),
                                           tok[:, t, 0:512].rearrange("p (g h d) -> p h g d", g=NG, h=HPG),
                                           rms20[:, t, 0:8].rearrange("p (g h a) -> p h g a", g=NG, a=1)
                                           .to_broadcast([P, HPG, NG, HD]), ALU.mult))
                    kk = tok[:, t, 768:1280].rearrange("p (b c g d) -> p b c g d", b=2, c=2, g=NG)[:, :, 0]
                    rk = rms20[:, t, 12:20].rearrange("p (b c g a) -> p b c g a", b=2, c=2, g=NG)[:, :, 0]
                    last = dve.tensor_tensor(kn[:, t].rearrange("p b (g d) -> p b g d", g=NG), kk,
                                             rk.to_broadcast([P, 2, NG, HD]), ALU.mult)
                    if t == 0:
                        link(last)
                last.then_inc(S["qk_ready"], 1)
                dve.wait_ge(S["small_loaded"], 16 * 3)
                dve.tensor_tensor(gsig, tok[:, :, 1280:1304], gateb[:, l:l + 1, :].to_broadcast([P, NT, 3 * NH]),
                                  ALU.add).then_inc(S["gs_in"], 1)
                dve.wait_ge(S["lrux_ready"], 4 * L)
                for m in range(NC_LRU):
                    cw = [par[:, R_CW + 16 * l + 4 * w + m:R_CW + 16 * l + 4 * w + m + 1] for w in range(CONV)]
                    cb = par[:, R_CB + 4 * l + m:R_CB + 4 * l + m + 1]
                    link(dve.tensor_scalar(xc[:, m, :], xpad[:, m, 0:SEQ], cw[0], cb, ALU.mult, ALU.add))
                    for w in range(1, CONV):
                        last = dve.scalar_tensor_tensor(xc[:, m, :], xpad[:, m, w:w + SEQ], cw[w], xc[:, m, :], ALU.mult, ALU.add)
                        if w < CONV - 1:
                            link(last)
                    last.then_inc(S["conv_ready"], 1)
                dve.wait_ge(S["T_done"], 4 * l + 3)
                dve.tensor_scalar(kT, bank[0][:, :].rearrange("p (a b) -> p a b", a=2), par[:, R_KG + l:R_KG + l + 1], None,
                                  ALU.mult).then_inc(S["kT_ready"], 1)
                dve.wait_ge(S["T_done"], 4 * l + 4)
                for e in range(2):
                    for g in range(NG):
                        last = dve.tensor_copy(
                            kcv2[e * HD:(e + 1) * HD, :, g, :],
                            bank[1][g * HD:(g + 1) * HD, :].rearrange("p (v t e) -> p v t e", v=2, e=2)[:, :, :, e])
                        if (e, g) != (1, 1):
                            link(last)
                last.then_inc(S["kcv_ready"], 1)
                dve.wait_ge(S["kcv_ready"], L)
                for v in range(2):
                    s0 = kcv2[:, v, 0, 0:1]
                    src = bass.AP(s0.tensor, s0.offset, [list(s0.ap[0]), [1, L2], [P, NG], [CMP_STRIDE // 2, N_CMP]])
                    p0 = posT[:, (2 * l + v) * L2:(2 * l + v) * L2 + 1]
                    pv = bass.AP(p0.tensor, p0.offset, [list(p0.ap[0]), [1, L2], [0, NG], [0, N_CMP]])
                    dve.tensor_tensor(blk[:, v, :].rearrange("p (m g n) -> p m g n", m=L2, g=NG), src, pv, ALU.add)\
                       .then_inc(S["blk_ready"], 1)
                dve.wait_ge(S["gs_exp"], L)
                link(dve.tensor_scalar(gsig, gsig, 1.0, None, ALU.add))
                link(dve.reciprocal(gsig, gsig))
                dve.wait_ge(S["cmph_done"], L)
                link(dve.tensor_copy(hc, bank[2][:, 0:60]))
                link(dve.tensor_tensor(hc2, hc, hc, ALU.mult))
                link(dve.tensor_scalar(hc2, hc2, 0.044715, 1.0, ALU.mult, ALU.add))
                dve.tensor_tensor(hc2, hc2, hc, ALU.mult).then_inc(S["gelu_c_in"], 1)
                dve.wait_ge(S["gelu_c_th"], L)
                link(dve.tensor_scalar(hct, hct, 1.0, 0.5, ALU.add, ALU.mult))
                dve.tensor_tensor(hc, hc, hct, ALU.mult).then_inc(S["gelu_c_ready"], 1)
                dve.wait_ge(S["kc_done2"], L)
                nb = NG * N_CMP
                link(dve.tensor_copy(kcn[:, 0:HD], bank[2][0:nb, 64:128]))
                dve.tensor_copy(vcs, bank[2][0:N_CMP, 128:256]).then_inc(S["vc_ready"], 1)
                link(dve.tensor_tensor(kcsq, kcn[:, 0:HD], kcn[:, 0:HD], ALU.mult))
                dve.tensor_reduce(kcs, kcsq, AX, ALU.add).then_inc(S["kcn_in"], 1)
                dve.wait_ge(S["kcn_root"], L)
                link(dve.reciprocal(kcs, kcs))
                link(dve.tensor_scalar(kcn[:, HD:P], kcn[:, 0:HD], kcs, None, ALU.mult))
                dve.tensor_copy(kcn[:, 0:HD], kcn[:, HD:P]).then_inc(S["kcn_ready"], 1)
                dve.wait_ge(S["kcT_done"], L)
                dve.tensor_scalar(kcT, bank[3][:, 0:nb], par[:, R_KG + l:R_KG + l + 1], None, ALU.mult).then_inc(S["kcT_ready"], 1)
                if l == 0:
                    dve.wait_ge(S["bias_ready"], 4)
                dve.wait_ge(S["cs_done"], L)
                link(dve.memset(cS, NEG))
                for t in range(NT):
                    n = CMP_SEEN[t]
                    first = CMP_BLOCK - 1 + P * (1 - t)
                    for g in range(NG):
                        c = t * HPG * 16
                        link(dve.scalar_tensor_tensor(
                            cS[:, t, g * HPG:(g + 1) * HPG, 0:n],
                            bank[g][:, c:c + HPG * 16].rearrange("p (h n) -> p h n", h=HPG)[:, :, 0:n], HD ** -0.5,
                            biasU[:, g * HPG:(g + 1) * HPG, first:first + CMP_STRIDE * (n - 1) + 1:CMP_STRIDE], ALU.mult, ALU.add))
                cSf = cS.rearrange("p t h n -> p (t h) n")
                link(dve.tensor_reduce(cmx, cSf, AX, ALU.max))
                link(dve.tensor_scalar(cmx, cmx, NEG / 10, None, ALU.max))
                dve.tensor_tensor(cSf, cSf, cmx.rearrange("p (a b) -> p a b", b=1).to_broadcast([P, NT * NH, 16]),
                                  ALU.subtract).then_inc(S["cs_in"], 1)
                dve.wait_ge(S["cs_exp"], L)
                link(dve.tensor_reduce(cden, cSf, AX, ALU.add))
                link(dve.tensor_scalar(cden, cden, 1e-30, None, ALU.max))
                link(dve.reciprocal(cden, cden))
                link(dve.tensor_tensor(cden.rearrange("p (t h) -> p t h", t=NT), cden.rearrange("p (t h) -> p t h", t=NT),
                                       gsig[:, :, 0:NH], ALU.mult))
                dve.tensor_tensor(cSf, cSf, cden.rearrange("p (a b) -> p a b", b=1).to_broadcast([P, NT * NH, 16]),
                                  ALU.mult).then_inc(S["cp_ready"], 1)
                def scores(i):
                    t, h = i // NH, i % NH
                    W = P * (t + 1)
                    n = NT * NH * l + i
                    dve.wait_ge(S["s_done"], n + 1)
                    if i >= 2:
                        dve.wait_ge(S["e_ready"], n - 1)
                    s = sS[:, i % 2, 0:2 * W].rearrange("p (b k) -> p b k", b=2)
                    first = P * (1 - t)
                    link(dve.scalar_tensor_tensor(s, bank[6 + i % 2][:, 0:2 * W].rearrange("p (b k) -> p b k", b=2), HD ** -0.5,
                                                  biasU[:, h:h + 1, first:first + W].to_broadcast([P, 2, W]), ALU.mult, ALU.add))
                    m = mx[:, 16 * (i % 2):16 * (i % 2) + 2]
                    link(dve.tensor_reduce(m, s, AX, ALU.max))
                    dve.tensor_scalar(m, m, -1.0, None, ALU.mult).then_inc(S["s_ready"], 1)

                def weigh(i):
                    t, h = i // NH, i % NH
                    W = P * (t + 1)
                    dve.wait_ge(S["e_ready"], NT * NH * l + i + 1)
                    d = den[:, 16 * (i % 2):16 * (i % 2) + 2]
                    link(dve.reciprocal(d, d))
                    link(dve.tensor_tensor(d, d, gsig[:, t, NH + h:NH + h + NH + 1:NH], ALU.mult))
                    for b in range(2):
                        last = dve.tensor_scalar(sP[:, i % 2, b * W:(b + 1) * W], sP[:, i % 2, b * W:(b + 1) * W], d[:, b:b + 1],
                                                 None, ALU.mult)
                        if b == 0:
                            link(last)
                    last.then_inc(S["p_ready"], 1)

                for i in range(NT * NH + 1):
                    if i == NH // 2:
                        dve.wait_ge(S["mult_ready"], L)
                        for m in range(NC_LRU):
                            last = dve.tensor_tensor_scan(tt[:, m, :], aa[:, m, :], ii[:, m, :], 0.0, ALU.mult, ALU.add)
                            if m < NC_LRU - 1:
                                link(last)
                        last.then_inc(S["scan_ready"], 1)
                    if i < NT * NH:
                        scores(i)
                    if i >= 1:
                        weigh(i - 1)
                dve.wait_ge(S["mroot"], L)
                link(dve.reciprocal(nrm[:, 4:8], nrm[:, 4:8]))
                for part in range(2):
                    for t in range(NT):
                        for c in range(2):
                            dve.wait_ge(S["out_done"], 8 * l + 4 * part + 2 * t + c + 1)
                            xo = xs[:, t, c * 512:(c + 1) * 512]
                            r = nrm[:, 6 + t:7 + t] if part == 0 else nrm[:, 4 + t:5 + t]
                            last = dve.scalar_tensor_tensor(xo, bank[4 * part + 2 * t + c][:, :], r, xo, ALU.mult, ALU.add)
                            if (part, c) == (1, 1):
                                last.then_inc(S["x_mixed"], 1)
                            else:
                                link(last)
                dve.wait_ge(S["x_mixed"], NT * L)
                norm(2 * l + 1, R_G2 + 8 * l)

                if l == 0:
                    for n, (g, u) in enumerate(DUNITS):
                        last_piece = (g, u) == (FFN_PIECES - 1, 4)
                        done = g - 1 if u < 4 else g
                        if done >= 0 and (u == 1 or last_piece):
                            for i in (2 * done, 2 * done + 1):
                                dve.wait_ge(S["silu_ready"], i + 1)
                                dve.tensor_tensor(ehid[:, i % 2 * SEQ:(i % 2 + 1) * SEQ], esil[:, i % 2, 0:SEQ],
                                                  bank[i % 4][:, SEQ:2 * SEQ], ALU.mult).then_inc(S["hid_ready"], 1)
                        if done >= 0 and (u == 2 or last_piece):
                            for i in (2 * done, 2 * done + 1):
                                dve.wait_ge(S["dhid_high"], i + 1)
                                dve.tensor_tensor(dhl[:, i % 4, :], ehid[:, i % 2 * SEQ:(i % 2 + 1) * SEQ],
                                                  dhh[:, i % 4, :].bitcast(F32), ALU.subtract).then_inc(S["dhid_rest"], 1)
                        if n >= USLOTS:
                            dve.wait_ge(S["dunit_used"], n - USLOTS + 1)
                        dve.wait_ge(S["dwh_ready"], n + 1)
                        dve.tensor_tensor(dense_in(wl, n), dense_source(g, u), dense_in(wh, n).bitcast(F32), ALU.subtract)\
                           .then_inc(S["dwl_ready"], 1)
                    dve.wait_ge(S["dunit_used"], len(DUNITS))
                    for t in range(NT):
                        for c in range(2):
                            xo = xs[:, t, c * 512:(c + 1) * 512]
                            last = dve.tensor_tensor(xo, xo, bank[4 + 2 * t + c][:, :], ALU.add)
                            if c == 0:
                                link(last)
                        last.then_inc(S["ffn_done"], 1)
                    dve.wait_ge(S["ffn_done"], NT)
                    continue
                dve.wait_ge(S["log_done"], 1)
                link(dve.tensor_copy(logit, bank[4][:, 0:16].rearrange("p (a b) -> p a b", a=NT)))
                for t in range(NT):
                    link(dve.max(top8[:, t, :], logit[:, t, :]))
                    link(dve.max_index(idx8[:, t, :], top8[:, t, :], logit[:, t, :]))
                link(dve.tensor_copy(idxf, idx8[:, :, :]))
                dve.tensor_tensor(wt[:, 0:2], top8[:, :, 1], top8[:, :, 0], ALU.subtract).then_inc(S["texp_in"], 1)
                dve.wait_ge(S["texp"], 1)
                link(dve.tensor_scalar(wt[:, 2:4], wt[:, 0:2], 1.0, None, ALU.add))
                link(dve.reciprocal(wt[:, 2:4], wt[:, 2:4]))
                link(dve.tensor_tensor(wt[:, 4:6], wt[:, 0:2], wt[:, 2:4], ALU.mult))
                eid = slot_id[:, 0:NE]
                for t in range(NT):
                    link(dve.tensor_scalar(oh1[:, t, :], eid, idxf[:, t, 0:1], None, ALU.is_equal))
                    link(dve.tensor_scalar(oh2[:, t, :], eid, idxf[:, t, 1:2], None, ALU.is_equal))
                    link(dve.tensor_scalar(wexp[:, t, :], oh1[:, t, :], wt[:, 2 + t:3 + t], None, ALU.mult))
                    link(dve.scalar_tensor_tensor(wexp[:, t, :], oh2[:, t, :], wt[:, 4 + t:5 + t], wexp[:, t, :], ALU.mult, ALU.add))
                dve.tensor_tensor(memb, oh1, oh2, ALU.add).then_inc(S["pos_in"], 1)
                dve.wait_ge(S["pos_in"], 1)
                dve.wait_ge(S["pos_done"], 1)
                link(dve.tensor_copy(pos, bank[4][:, 32:48].rearrange("p (a b) -> p a b", a=NT)))
                link(dve.tensor_scalar(over, bank[4][:, 48:56], float(P), None, ALU.is_gt))
                link(dve.tensor_tensor_scan(rank, ones[:, 0:NE], over, 0.0, ALU.mult, ALU.add))
                link(dve.tensor_scalar(jobf[:, 0:1], rank[:, NE - 1:NE], float(NE), None, ALU.add))
                link(dve.tensor_copy(jobf[:, 1:NE + 1], eid))
                for t in range(NT):
                    link(dve.tensor_copy(table[:, 0:NE, t], memb[:, t, :]))
                    link(dve.tensor_copy(table[:, 0:NE, 2 + t], pos[:, t, :]))
                    link(dve.tensor_copy(table[:, 0:NE, 4 + t], wexp[:, t, :]))

                def rest(j, u, first=False):
                    if not first:
                        dve.wait_ge(S["unit_used"], j * UNITS + (u - USLOTS + 1))
                    dve.wait_ge(S["wh_ready"], j * UNITS + (u + 1))
                    dve.tensor_tensor(unit_in(wl, u), unit_source(u), unit_in(wh, u).bitcast(F32), ALU.subtract)\
                       .then_inc(S["wl_ready"], 1)

                def tokens_rest(j):
                    for k in range(KD):
                        dve.wait_ge(S["xg_high"], 8 * j + 4 * (k // 4 + 1))
                        dve.scalar_tensor_tensor(xgl[:, k, :], bank[4 + k // 4][:, (k % 4) * P:(k % 4 + 1) * P],
                                                 par[:, R_G2 + 8 + k:R_G2 + 9 + k], xgh[:, k, :].bitcast(F32),
                                                 ALU.mult, ALU.subtract).then_inc(S["xg_ready"], 1)

                def turned_rest(j, k):
                    a, b = done_tiles(k), done_tiles(k + 1)
                    dve.wait_ge(S["hidT_high"], j * FCH + (k + 1))
                    dve.tensor_tensor(ehidTl[:, a:b, :], bank[4 + k % 2][:, 0:(b - a) * P].rearrange("p (a b) -> p a b", b=P),
                                      ehidTh[:, a:b, :].bitcast(F32), ALU.subtract).then_inc(S["hidT_ready"], 1)

                def select(j):
                    for t in range(NT):
                        dve.tensor_scalar(selM[:, t, :], slot_id[:, :], job[:, 2 + t:3 + t], job[:, t:t + 1], ALU.is_equal, ALU.mult)\
                           .then_inc(S["sel_ready"], 1)
                    for t in range(NT):
                        dve.tensor_scalar(selW[:, t, :], slot_id[:, :], job[:, 2 + t:3 + t], job[:, 4 + t:5 + t], ALU.is_equal, ALU.mult)\
                           .then_inc(S["sel_ready"], 1)

                def selection_turned(j):
                    dve.wait_ge(S["selT_done"], j + 1)
                    dve.tensor_copy(selT[:, :, :], bank[6][:, 0:NT * P].rearrange("p (a b) -> p a b", a=NT)).then_inc(S["selT_ready"], 1)

                dve.tensor_copy(job, table[:, 0, :]).then_inc(S["job_ready"], 1)
                dve.wait_ge(S["job_ready"], 1)
                select(0)
                for o in range(OVER):
                    link(dve.scalar_tensor_tensor(pick, rank, float(o + 1), over, ALU.is_equal, ALU.mult))
                    link(dve.tensor_tensor_reduce(junk[:, 0, :], pick, eid, 1.0, 0.0, ALU.mult, ALU.add,
                                                  jobf[:, NE + 1 + o:NE + 2 + o]))
                    for t in range(NT):
                        link(dve.tensor_tensor_reduce(junk[:, 0, :], pick, memb[:, t, :], 1.0, 0.0, ALU.mult, ALU.add,
                                                      table[:, NE + o, t:t + 1]))
                        link(dve.tensor_tensor_reduce(junk[:, 0, :], pick, pos[:, t, :], 1.0, -float(P), ALU.mult, ALU.add,
                                                      table[:, NE + o, 2 + t:3 + t]))
                        link(dve.tensor_tensor_reduce(junk[:, 0, :], pick, wexp[:, t, :], 1.0, 0.0, ALU.mult, ALU.add,
                                                      table[:, NE + o, 4 + t:5 + t]))
                dve.tensor_copy(jobi[:, 0:JOBS + 1], jobf).then_inc(S["jobs_ready"], 1)
                dve.wait_ge(S["jobs_ready"], 1)
                njobs = dve.value_load(jobi[0:1, 0:1], min_val=NE, max_val=JOBS)
                rest(0, 0, True)
                tokens_rest(0)
                rest(0, 1, True)
                rest(0, 2, True)
                with dve.Fori(0, njobs) as j:
                    for u in range(USLOTS, UNITS):
                        q = (u - 6) // 4
                        if u % 4 == 2 and u >= 6 and q < FCH:
                            if q >= HALF:
                                dve.wait_ge(S["hidT_done"], j * FCH + (q - HALF + 2))
                            dve.wait_ge(S["silu_ready"], j * FCH + (FT + q + 1))
                            dve.tensor_tensor(ehid[:, q % HALF * FN:(q % HALF + 1) * FN], esil[:, q % 2, :],
                                              bank[1 + 2 * (q % 2)][:, 0:FN], ALU.mult).then_inc(S["hid_ready"], 1)
                            if q >= 1:
                                turned_rest(j, q - 1)
                        if u == 4 * FCH + 5:
                            turned_rest(j, FCH - 1)
                        if u == 16:
                            selection_turned(j)
                        if u == 4 * FCH + 8:
                            with dve.If(j + 1 < njobs):
                                dve.tensor_copy(job, table[:, bass.ds(j + 1, 1), :].rearrange("p a c -> p (a c)"))\
                                   .then_inc(S["job_ready"], 1)
                                dve.wait_ge(S["job_ready"], j + 2)
                                select(j + 1)
                        rest(j, u)
                    dve.wait_ge(S["unit_used"], j * UNITS + UNITS)
                    dve.tensor_copy(ye[:, 0:512], bank[6][:, :]).then_inc(S["y_ready"], 1)
                    with dve.If(j + 1 < njobs):
                        rest(j + 1, 0)
                        tokens_rest(j + 1)
                    for q in range(4):
                        t, c = q // 2, q % 2
                        dve.wait_ge(S["comb_done"], 4 * j + (q + 1))
                        xo = xs[:, t, c * 512:(c + 1) * 512]
                        dve.tensor_tensor(xo, xo, bank[q][:, :], ALU.add).then_inc(S["comb_ready"], 1)
                    with dve.If(j + 1 < njobs):
                        rest(j + 1, 1)
                        rest(j + 1, 2)
                    dve.wait_ge(S["comb_ready"], 4 * j + 4)

        @block.tensor
        def _(pe):
            mm = pe.matmul

            def norm_turn(n):
                for k in range(KD):
                    for t in range(NT):
                        pe.wait_ge(S["norm_ready"], 2 * n + t + 1)
                        last = pe.transpose(bank[k // 2][:, (k % 2) * SEQ + t * P:(k % 2) * SEQ + (t + 1) * P],
                                            xn[:, t, k * P:(k + 1) * P], ident[:, :])
                    if k % 2 == 1:
                        last.then_inc(S["normT_done"], 1)

            pe.wait_ge(S["consts_set"], 1)
            pe.wait_ge(S["params_loaded"], 16 * 13)
            pe.transpose(bank[0][:, 0:N_ROWS], prow[:, :], ident[0:N_ROWS, 0:N_ROWS])
            pe.transpose(bank[0][:, 128:128 + HD], posr[:, :], ident[0:HD, 0:HD]).then_inc(S["params_transposed"], 1)
            pe.wait_ge(S["relb_loaded"], 32)
            mm(bank[1][0:NH, 0:U_LEN], relb[:, :], bucketT[:, :], start=True, stop=True).then_inc(S["urow_done"], 1)
            pe.wait_ge(S["params_ready"], 2)
            pe.wait_ge(S["urow_ready"], 1)

            for l in range(DEPTH):
                L = l + 1
                p0 = l * (MIX_PIECES + FFN_PIECES)
                norm_turn(2 * l)
                pe.wait_ge(S["hT_act"], 4 * l + 4)
                pe.wait_ge(S["hT_dve"], 4 * l + 4)

                def project(b, c0, w, lo, n, t):
                    for k in range(KD):
                        last = mm(bank[b + t][:, c0:c0 + n], hT[:, k, t * P:(t + 1) * P], w[:, k, lo:lo + n],
                                  start=(k == 0), stop=(k == KD - 1))
                    return last

                wait_piece(pe, p0)
                wA, wB = ring3(p0, KD, 768), ring3(p0 + 1, KD, W_B)
                for t in range(NT):
                    project(4, 0, wA, 0, 512, t).then_inc(S["q_done"], 1)
                project(6, 0, wA, 512, 256, 0)
                project(6, 0, wA, 512, 256, 1).then_inc(S["kc_done"], 1)
                wait_piece(pe, p0 + 1)
                for t in range(NT):
                    project(0, 0, wB, 0, 512, t).then_inc(S["kv_done"], 1)
                for t in range(NT):
                    project(6, 256, wB, 512, 24, t).then_inc(S["gates_done"], 1)
                if l == 0:
                    pe.wait_ge(S["skew_loaded"], 16)
                    pe.wait_ge(S["tok_act"], 1)
                    pe.wait_ge(S["tok_dve"], 1)
                    for c in range(4):
                        mm(bank[2 + c][:, :], flip[:, :], skew[:, c * 512:(c + 1) * 512], start=True, stop=True)\
                            .then_inc(S["flip_done"], 1)
                for w in range(2):
                    wait_piece(pe, p0 + 2 + w)
                    if l == 0:
                        pe.wait_ge(S["bias_ready"], 2 * w + 2)
                    if w == 1:
                        pe.wait_ge(S["tok_act"], 4 * l + 1)
                        pe.wait_ge(S["tok_dve"], 4 * l + 1)
                    wL = ring3(p0 + 2 + w, KD, 512)
                    for m in range(NC_LRU):
                        for k in range(KD):
                            last = mm(bank[2 + 2 * w + m // 2][:, (m % 2) * SEQ:(m % 2 + 1) * SEQ], wL[:, k, m * P:(m + 1) * P],
                                      hT[:, k, :], start=(k == 0), stop=(k == KD - 1))
                        if m == 1 or (m == 3):
                            last.then_inc(S["lrux_done" if w == 0 else "lrug_done"], 1)
                pe.wait_ge(S["tok_act"], 4 * L)
                pe.wait_ge(S["tok_dve"], 4 * L)
                pe.wait_ge(S["qk_ready"], L)
                for hh in range(HPG):
                    for t in range(NT):
                        last = pe.transpose(bank[6 + hh // 2][:, (hh % 2) * SEQ + t * P:(hh % 2) * SEQ + (t + 1) * P],
                                            qn[:, t, hh, :], ident[:, :])
                    if hh % 2 == 1:
                        last.then_inc(S["T_done"], 1)
                for b in range(2):
                    for t in range(NT):
                        last = pe.transpose(bank[0][:, b * SEQ + t * P:b * SEQ + (t + 1) * P], kn[:, t, b, :], ident[:, :])
                last.then_inc(S["T_done"], 1)
                for v in range(2):
                    for t in range(NT):
                        last = pe.transpose(bank[1][:, v * SEQ + t * P:v * SEQ + (t + 1) * P],
                                            tok[:, t, 512 + v * P:512 + (v + 1) * P], ident[:, :])
                last.then_inc(S["T_done"], 1)
                wait_piece(pe, p0 + 4)
                w1 = ring3(p0 + 4, 2 * L2, P)
                pe.wait_ge(S["lrux_ready"], 4 * L)
                nb = NG * N_CMP
                for v in range(2):
                    pe.wait_ge(S["blk_ready"], 2 * l + v + 1)
                    for m in range(L2):
                        last = mm(bank[2][:, v * nb:(v + 1) * nb], w1[:, v * L2 + m, :], blk[:, v, m * nb:(m + 1) * nb],
                                  start=(m == 0), stop=(m == L2 - 1))
                last.then_inc(S["cmph_done"], 1)
                pe.wait_ge(S["gate_ready"], L)
                pe.wait_ge(S["lru_w_loaded"], 16 * 4 * L)
                pe.wait_ge(S["conv_ready"], 4 * L)
                for w in range(2):
                    if w == 1:
                        pe.wait_ge(S["kT_ready"], L)
                        pe.wait_ge(S["kcv_ready"], L)
                    for m in range(NC_LRU):
                        last = mm(bank[(4, 0)[w] + m // 2][:, (m % 2) * SEQ:(m % 2 + 1) * SEQ], lruW[:, w, m, :], xc[:, m, :],
                                  start=True, stop=True)
                    last.then_inc(S[("rgate_done", "igate_done")[w]], 1)
                pe.wait_ge(S["gelu_c_ready"], L)
                mm(bank[2][0:nb, 64:128], hc[:, 0:nb], w2[:, l, 0, :], start=True, stop=True)
                for g in range(NG):
                    last = mm(bank[2][0:N_CMP, 128 + g * HD:128 + (g + 1) * HD], hc[:, nb + g * N_CMP:nb + (g + 1) * N_CMP],
                              w2[:, l, 1, :], start=True, stop=True)
                last.then_inc(S["kc_done2"], 1)
                pe.wait_ge(S["kcn_ready"], L)
                pe.transpose(bank[3][:, 0:nb], kcn, ident[0:nb, 0:nb]).then_inc(S["kcT_done"], 1)
                pe.wait_ge(S["qT_ready"], 2 * L)
                pe.wait_ge(S["kcT_ready"], L)
                pe.wait_ge(S["itanh_ready"], L)
                for t in range(NT):
                    for h in range(NH):
                        g, hh = h // HPG, h % HPG
                        c = (t * HPG + hh) * 16
                        last = mm(bank[g][:, c:c + N_CMP], qT[g * HD:(g + 1) * HD, hh, t * P:(t + 1) * P],
                                  kcT[g * HD:(g + 1) * HD, g * N_CMP:(g + 1) * N_CMP], start=True, stop=True)
                last.then_inc(S["cs_done"], 1)

                def score(i):
                    t, h = i // NH, i % NH
                    g, hh = h // HPG, h % HPG
                    W = P * (t + 1)
                    if i >= 2:
                        pe.wait_ge(S["s_ready"], NT * NH * l + i - 1)
                    for b in range(2):
                        last = mm(bank[6 + i % 2][:, b * W:(b + 1) * W], qT[g * HD:(g + 1) * HD, hh, t * P:(t + 1) * P],
                                  kT[g * HD:(g + 1) * HD, b, 0:W], start=True, stop=True)
                    last.then_inc(S["s_done"], 1)

                def turn(i):
                    W = P * (i // NH + 1)
                    n = NT * NH * l + i
                    pe.wait_ge(S["p_ready"], n + 1)
                    if i >= 2:
                        pe.wait_ge(S["pT_ready"], n - 1)
                    for b in range(2 * W // P):
                        last = pe.transpose(bank[2 + i % 2][:, b * P:(b + 1) * P], sP[:, i % 2, b * P:(b + 1) * P], ident[:, :])
                    last.then_inc(S["pT_done"], 1)

                def values(i):
                    t, h = i // NH, i % NH
                    g = h // HPG
                    n = NT * NH * l + i
                    pe.wait_ge(S["pT_ready"], n + 1)
                    o = bank[4 + t][:, h * HD:(h + 1) * HD]
                    mm(o, cPT[:, i, :], vcs[:, g * HD:(g + 1) * HD], start=True, stop=False)
                    for b in range(2):
                        for k in range(t + 1):
                            v = tok[:, k, 896 + 256 * b + g * HD:896 + 256 * b + (g + 1) * HD]
                            last = mm(o, sT[:, i % 2, (b * (t + 1) + k) * P:(b * (t + 1) + k + 1) * P], v,
                                      start=False, stop=(b == 1 and k == t))
                    last.then_inc(S["o_done"], 1)

                pe.wait_ge(S["kT_ready"], L)
                score(0)
                pe.wait_ge(S["cp_ready"], L)
                for c in range(4):
                    if c >= 2:
                        pe.wait_ge(S["cpT_ready"], 4 * l + c - 1)
                    for a in range(4):
                        i = 4 * c + a
                        last = pe.transpose(bank[c % 2][0:N_CMP, a * P:(a + 1) * P], cS[:, i // NH, i % NH, 0:N_CMP], ident[:, :])
                    last.then_inc(S["cpT_done"], 1)
                pe.wait_ge(S["cpT_ready"], 4 * L)
                pe.wait_ge(S["vc_ready"], L)
                pe.wait_ge(S["rtanh_ready"], L)
                score(1)
                for i in range(1, NT * NH + 2):
                    if i + 1 < NT * NH:
                        score(i + 1)
                    if i <= NT * NH:
                        turn(i - 1)
                    if i >= 2:
                        values(i - 2)
                pe.wait_ge(S["ysq_ready"], L)
                for t in range(NT):
                    for m in range(NC_LRU):
                        last = mm(bank[1][:, t:t + 1], tt[:, m, t * P:(t + 1) * P], ones[:, 0:1], start=(m == 0), stop=(m == NC_LRU - 1))
                last.then_inc(S["lsum_done"], 1)
                pe.wait_ge(S["s_ready"], NT * NH * L)
                pe.wait_ge(S["o_ready"], NT * L)
                for m in range(4):
                    for t in range(NT):
                        last = pe.transpose(bank[6 + m // 2][:, (m % 2) * SEQ + t * P:(m % 2) * SEQ + (t + 1) * P],
                                            oS[:, t, m * P:(m + 1) * P], ident[:, :])
                    if m % 2 == 1:
                        last.then_inc(S["oT_done"], 1)
                for part in range(2):
                    wait_piece(pe, p0 + 5 + part)
                    if part == 0:
                        pe.wait_ge(S["ymix_ready"], 4 * L)
                        pe.wait_ge(S["mroot_in"], L)
                        pe.wait_ge(S["pT_ready"], NT * NH * L)
                    else:
                        pe.wait_ge(S["oT_ready"], 4 * L)
                    wo = ring3(p0 + 5 + part, 4, D)
                    for t in range(NT):
                        for c in range(2):
                            for m in range(4):
                                last = mm(bank[4 * part + 2 * t + c][:, :], mixT[:, 4 * part + m, t * P:(t + 1) * P],
                                          wo[:, m, c * 512:(c + 1) * 512], start=(m == 0), stop=(m == 3))
                            last.then_inc(S["out_done"], 1)
                norm_turn(2 * l + 1)
                if l == 0:
                    pe.wait_ge(S["dx_ready"], KD)
                    for n, (g, u) in enumerate(DUNITS):
                        if u < 4:
                            w, kh = u // 2, u % 2
                            outs = [(bank[(2 * g + r) % 4][:, w * SEQ:(w + 1) * SEQ], r, k) for r in range(2) for k in range(4)]
                            pe.wait_ge(S["dwh_ready"], n + 1)
                            for o, r, k in outs:
                                h = dense_in(wh, n)[:, k, r * P:(r + 1) * P]
                                mm(o, h, dxh[:, 4 * kh + k, :], start=(kh == 0 and k == 0), stop=False, skip_group_check=True)
                                mm(o, h, dxl[:, 4 * kh + k, :], start=False, stop=False, skip_group_check=True)
                            pe.wait_ge(S["dwl_ready"], n + 1)
                            for o, r, k in outs:
                                last = mm(o, dense_in(wl, n)[:, k, r * P:(r + 1) * P], dxh[:, 4 * kh + k, :], start=False,
                                          stop=(kh == 1 and k == 3), skip_group_check=True)
                        else:
                            i = 2 * g + u - 4
                            pe.wait_ge(S["dhid_rest"], i + 1)
                            pe.wait_ge(S["dwh_ready"], n + 1)
                            pe.wait_ge(S["dwl_ready"], n + 1)
                            for t in range(NT):
                                for a, b in ((dhh, wh), (dhh, wl), (dhl, wh)):
                                    for c in range(2):
                                        last = mm(bank[4 + 2 * t + c][:, :], a[:, i % 4, t * P:(t + 1) * P],
                                                  dense_in(b, n)[:, 0, c * 512:(c + 1) * 512], start=(i == 0 and a is dhh and b is wh),
                                                  stop=(i == FT - 1 and a is dhl), skip_group_check=True)
                        last.then_inc(S["dunit_used"], 1)
                    continue
                pe.wait_ge(S["hT_act"], 12)
                pe.wait_ge(S["hT_dve"], 12)
                for t in range(NT):
                    for k in range(KD):
                        last = mm(bank[4][:, t * NE:(t + 1) * NE], hT[:, k, t * P:(t + 1) * P], rw[:, k, :], start=(k == 0), stop=(k == KD - 1))
                last.then_inc(S["log_done"], 1)
                pe.wait_ge(S["pos_in"], 1)
                mm(bank[4][:, 32:40], before[:, :], memb[:, 0, :], start=True, stop=True)
                mm(bank[4][:, 40:48], ones[:, :], memb[:, 0, :], start=True, stop=False)
                mm(bank[4][:, 40:48], before[:, :], memb[:, 1, :], start=False, stop=True)
                mm(bank[4][:, 48:56], ones[:, :], memb[:, 0, :], start=True, stop=False)
                mm(bank[4][:, 48:56], ones[:, :], memb[:, 1, :], start=False, stop=True).then_inc(S["pos_done"], 1)

                def gather(j):
                    pe.wait_ge(S["sel_ready"], 4 * j + 2)
                    for c in range(2):
                        for k in range(4 * c, 4 * c + 4):
                            for t in range(NT):
                                last = mm(bank[4 + c][:, (k % 4) * P:(k % 4 + 1) * P], xn[:, t, k * P:(k + 1) * P], selM[:, t, :],
                                          start=(t == 0), stop=(t == NT - 1))
                        last.then_inc(S["xg_done"], 1)

                def turn_selection(j):
                    pe.wait_ge(S["sel_ready"], 4 * j + 4)
                    for t in range(NT):
                        last = pe.transpose(bank[6][:, t * P:(t + 1) * P], selW[:, t, :], ident[:, :])
                    last.then_inc(S["selT_done"], 1)

                def split_product(j, u, outs, high, rest, start, stop):
                    h, low = unit_in(wh, u), unit_in(wl, u)
                    pe.wait_ge(S["wh_ready"], j * UNITS + (u + 1))
                    for k, o, lo, hi in outs:
                        mm(o, high(k), h[:, k, lo:hi], start=start and k == 0, stop=False, skip_group_check=True)
                        mm(o, rest(k), h[:, k, lo:hi], start=False, stop=False, skip_group_check=True)
                    pe.wait_ge(S["wl_ready"], j * UNITS + (u + 1))
                    for k, o, lo, hi in outs:
                        last = mm(o, high(k), low[:, k, lo:hi], start=False, stop=stop and k == h.shape[1] - 1, skip_group_check=True)
                    last.then_inc(S["unit_used"], 1)

                def turn_expert_hidden(k):
                    a, z = done_tiles(k), done_tiles(k + 1)
                    for i in range(a, z):
                        lo = i * P % (HALF * FN)
                        last = pe.transpose(bank[4 + k % 2][:, (i - a) * P:(i - a + 1) * P], ehid[:, lo:lo + P], ident[:, :])
                    last.then_inc(S["hidT_done"], 1)

                gather(0)
                pe.wait_ge(S["xg_ready"], 8)
                pe.wait_ge(S["jobs_ready"], 1)
                njobs = pe.value_load(jobi[0:1, 0:1], min_val=NE, max_val=JOBS)
                with pe.Fori(0, njobs) as j:
                    for q in range(FCH):
                        pe.wait_ge(S["hid_ready"], j * FCH + (FT + q - 1))
                        for w in range(2):
                            for kh in range(2):
                                split_product(j, 4 * q + 2 * w + kh,
                                                     [(k, bank[2 * (q % 2) + w][:, 0:FN], 0, FN) for k in range(4)],
                                                     lambda k: xgh[:, 4 * kh + k, :], lambda k: xgl[:, 4 * kh + k, :],
                                                     kh == 0, kh == 1)
                        if q >= 1:
                            pe.wait_ge(S["hid_ready"], j * FCH + (FT + q))
                            if q >= 3:
                                pe.wait_ge(S["hidT_ready"], j * FCH + (q - 2))
                            turn_expert_hidden(q - 1)
                        if q == 2:
                            turn_selection(j)
                    pe.wait_ge(S["selT_ready"], j + 1)
                    for i in range(FT):
                        for s in range(1, FCH + 1):
                            if done_tiles(s - 1) == i:
                                pe.wait_ge(S["hidT_ready"], j * FCH + (s))
                        split_product(j, 4 * FCH + i, [(0, bank[6 + o][:, :], o * 512, (o + 1) * 512) for o in range(2)],
                                             lambda k: ehidTh[:, i, :], lambda k: ehidTl[:, i, :], i == 0, i == FT - 1)
                        if i == 1:
                            pe.wait_ge(S["hid_ready"], j * FCH + (FT + FCH))
                            pe.wait_ge(S["hidT_ready"], j * FCH + (FCH - 2))
                            turn_expert_hidden(FCH - 1)
                    with pe.If(j + 1 < njobs):
                        gather(j + 1)
                    pe.wait_ge(S["y_ready"], j + 1)
                    pe.wait_ge(S["ye_act"], j + 1)
                    for o in range(4):
                        t, c = o // 2, o % 2
                        mm(bank[o][:, :], selT[:, t, :], ye[:, c * 512:(c + 1) * 512], start=True, stop=True)\
                            .then_inc(S["comb_done"], 1)
                    with pe.If(j + 1 < njobs):
                        pe.wait_ge(S["xg_ready"], 8 * j + 16)
                    pe.wait_ge(S["comb_ready"], 4 * j + 4)


_INS = ['x', 'rel_bias', 'norm1_g', 'w_in', 'conv_w', 'conv_b', 'lru_wa', 'lru_ba', 'lru_wx', 'lru_bx', 'lru_lambda',
        'q_norm_g', 'k_norm_g', 'cmp_pos', 'cmp_w1', 'cmp_w2', 'gate_b', 'out_norm_g', 'w_out', 'norm2_g',
        'ffn_w_gate', 'ffn_w_up', 'ffn_w_down', 'router_w', 'moe_w_gate', 'moe_w_up', 'moe_w_down']


def bucket_constant():
    import math
    import numpy as np
    rows = np.zeros((N_BUCKETS + 1, U_LEN), np.float32)
    exact, far = N_BUCKETS // 2, 128
    for j in range(U_LEN):
        dist = 2 * P - 1 - j
        if dist < 0:
            b = N_BUCKETS
        elif dist < exact:
            b = dist
        else:
            b = min(exact + int(np.float32(math.log(dist / exact)) / np.float32(math.log(far / exact)) * (N_BUCKETS - exact)),
                    N_BUCKETS - 1)
        rows[b, j] = 1.0
    return rows


def kernel(**inputs):
    import numpy as _np
    import concourse.bacc as _bacc
    from concourse import mybir as _mybir
    from concourse.bass_utils import run_bass_kernel_spmd as _run

    nc = _bacc.Bacc("TRN2", target_bir_lowering=False, num_devices=1)
    arrays, args = {}, []
    for name in _INS:
        a = _np.ascontiguousarray(inputs[name])
        arrays[f"in_{name}_dram"] = a
        args.append(nc.dram_tensor(f"in_{name}_dram", a.shape, _mybir.dt.from_np(a.dtype), kind="ExternalInput").ap())
    rows = bucket_constant()
    arrays["bucket_rows_dram"] = rows
    args.append(nc.dram_tensor("bucket_rows_dram", rows.shape, F32, kind="ExternalInput").ap())
    args.append(nc.dram_tensor("out_0_dram", (1, SEQ, D), F32, kind="ExternalOutput").ap())
    build(nc, *args)
    r = _run(nc, [arrays], core_ids=[0])
    return r.results[0]["out_0_dram"]
```
